# Optimizing a Trainium2 kernel written in Bass

```python
import math
import jax, jax.numpy as jnp
from jax import lax
import numpy as np

D_MODEL = 2048
BATCH = 1
SEQ = 256
DEPTH = 1
DEC_BATCH = 8
DEC_SEQ = 8
PAST_LEN = 2048
PAGE_SIZE = 128

N_BRANCH = 4
MIX_W = D_MODEL // 4
CONV_W = 4
LRU_W = MIX_W
LRU_BLOCKS = 8
LRU_BD = LRU_W // LRU_BLOCKS
LRU_C = 8.0
GM_W = MIX_W
GM_CHUNK = 128
GM_GROUPS = 4
GM_GD = GM_W // GM_GROUPS
RW_W = MIX_W
RW_HD = 64
RW_H = RW_W // RW_HD
RW_DECAY_R = 32
RW_A_R = 32
RW_G_R = 96
RW_P = 3 * RW_W + RW_DECAY_R + RW_A_R + RW_G_R
RW_LN_EPS = 64e-5
ML_W = MIX_W
ML_H = 4
ML_HD = ML_W // ML_H
ML_CHUNK = 64
D_FF = ((8 * D_MODEL + 3 * 256 - 1) // (3 * 256)) * 256
PROJ_SIZES = (LRU_W, LRU_W, GM_W, GM_W, RW_P, ML_W, ML_W, ML_W, ML_H, ML_H, N_BRANCH * D_MODEL)
P_TOTAL = sum(PROJ_SIZES)
N_STATE = 8

LAYER_PARAM_NAMES = (
    'norm_pre_mix', 'norm_post_mix', 'norm_pre_ffn', 'norm_post_ffn', 'w_in',
    'lru_conv_w', 'lru_conv_b', 'lru_wa', 'lru_ba', 'lru_wx', 'lru_bx', 'lru_lambda',
    'gmlp_ln_g', 'gmlp_ln_b', 'gmlp_ws', 'gmlp_bs',
    'rwkv_mu', 'rwkv_w0', 'rwkv_w2', 'rwkv_a0', 'rwkv_a2', 'rwkv_g2', 'rwkv_kk', 'rwkv_ka',
    'rwkv_rk', 'rwkv_ln_g', 'rwkv_ln_b',
    'mlstm_conv_w', 'mlstm_conv_b', 'mlstm_wq', 'mlstm_wk', 'mlstm_bi', 'mlstm_bf',
    'mlstm_norm_g', 'mlstm_skip',
    'w_branch', 'w_out', 'w_ff_in', 'w_ff_out')

kernel_name = 'gated_parallel_recurrent_hybrid_step'

F32 = jnp.float32

def _rmsnorm(x, g, eps=1e-6):
    xf = x.astype(F32)
    y = xf * lax.rsqrt(jnp.mean(xf * xf, axis=-1, keepdims=True) + eps)
    return (y * g.astype(F32)).astype(x.dtype)

def _layernorm(x, g, b, eps):
    xf = x.astype(F32)
    xc = xf - jnp.mean(xf, axis=-1, keepdims=True)
    y = xc * lax.rsqrt(jnp.mean(xc * xc, axis=-1, keepdims=True) + eps) * g.astype(F32)
    if b is not None:
        y = y + b.astype(F32)
    return y

def _split(z, sizes):
    idx = [int(i) for i in np.cumsum(sizes)[:-1]]
    return jnp.split(z, idx, axis=-1)

def _causal_conv(x, buf, w, b):
    T = x.shape[1]
    xp = jnp.concatenate([buf.astype(x.dtype), x], axis=1)
    y = b + w[0] * xp[:, 0:T]
    for j in range(1, CONV_W):
        y = y + w[j] * xp[:, j:j + T]
    return y, xp[:, T:]

def _lin_combine(e1, e2):
    a1, b1 = e1
    a2, b2 = e2
    return a1 * a2, a2 * b1 + b2

def _rglru_branch(z_x, z_g, conv_buf, h0, p, is_start):
    xc, conv_buf = _causal_conv(z_x, conv_buf, p['lru_conv_w'], p['lru_conv_b'])
    Bx, T, _ = xc.shape
    xb = xc.reshape(Bx, T, LRU_BLOCKS, LRU_BD)
    r = jax.nn.sigmoid((jnp.einsum('btni,nij->btnj', xb, p['lru_wa']).reshape(Bx, T, LRU_W) + p['lru_ba']).astype(F32))
    i = jax.nn.sigmoid((jnp.einsum('btni,nij->btnj', xb, p['lru_wx']).reshape(Bx, T, LRU_W) + p['lru_bx']).astype(F32))
    log_a = LRU_C * r * jax.nn.log_sigmoid(p['lru_lambda'].astype(F32))
    a = jnp.exp(log_a)
    mult = jnp.sqrt(-jnp.expm1(2.0 * log_a))
    if is_start:
        mult = mult.at[:, 0].set(1.0)
    b = mult * i * xc.astype(F32)
    b = b.at[:, 0].add(a[:, 0] * h0.astype(F32))
    _, h = lax.associative_scan(_lin_combine, (a, b), axis=1)
    y = h * jax.nn.gelu(z_g.astype(F32))
    return y, conv_buf, h[:, -1]

def _gmlp_branch(z_u, z_v, p):
    u = jax.nn.gelu(z_u.astype(F32))
    v = _layernorm(jax.nn.gelu(z_v.astype(F32)), p['gmlp_ln_g'], p['gmlp_ln_b'], 1e-5)
    Bx, T, _ = v.shape
    L = min(GM_CHUNK, T)
    nc = T // L
    vc = v.reshape(Bx, nc, L, GM_GROUPS, GM_GD)
    ws = jnp.tril(p['gmlp_ws'][:, :L, :L].astype(F32))
    bias = p['gmlp_bs'][:, :L].astype(F32).T
    s = jnp.einsum('gps,bcsgd->bcpgd', ws, vc) + bias[None, None, :, :, None]
    y = u * s.reshape(Bx, T, GM_W)
    return y, v

def _rwkv7_branch(z, shift_buf, S0, p):
    zf = z.astype(F32)
    Bx, T, _ = zf.shape
    prev = jnp.concatenate([shift_buf.astype(F32)[:, None], zf[:, :-1]], axis=1)
    zs = zf + (prev - zf) * p['rwkv_mu'].astype(F32)
    r, k, v, wd, ad, gd = _split(zs, (RW_W, RW_W, RW_W, RW_DECAY_R, RW_A_R, RW_G_R))
    w = -jax.nn.softplus(-(p['rwkv_w0'] + jnp.tanh(wd) @ p['rwkv_w2'])) - 0.5
    decay = jnp.exp(-jnp.exp(w))
    a = jax.nn.sigmoid(p['rwkv_a0'] + ad @ p['rwkv_a2'])
    g = jax.nn.sigmoid(gd) @ p['rwkv_g2']

    def hs(t):
        return t.reshape(Bx, T, RW_H, RW_HD)

    kk = hs(k * p['rwkv_kk'])
    kk = kk / jnp.maximum(jnp.linalg.norm(kk, axis=-1, keepdims=True), 1e-12)
    k = k * (1.0 + (a - 1.0) * p['rwkv_ka'])
    r, k, v, decay, a = hs(r), hs(k), hs(v), hs(decay), hs(a)

    def step(S, inp):
        r_t, w_t, k_t, v_t, kk_t, a_t = inp
        sa = jnp.einsum('bhvk,bhk->bhv', S, -kk_t)
        S = (S * w_t[:, :, None, :] + sa[..., None] * (kk_t * a_t)[:, :, None, :]
             + v_t[..., None] * k_t[:, :, None, :])
        return S, jnp.einsum('bhvk,bhk->bhv', S, r_t)

    def tm(t):
        return jnp.swapaxes(t, 0, 1)

    S, o = lax.scan(step, S0.astype(F32), (tm(r), tm(decay), tm(k), tm(v), tm(kk), tm(a)))
    o = tm(o)
    o = _layernorm(o, p['rwkv_ln_g'].reshape(RW_H, RW_HD), p['rwkv_ln_b'].reshape(RW_H, RW_HD), RW_LN_EPS)
    o = o + jnp.sum(r * k * p['rwkv_rk'].astype(F32), axis=-1, keepdims=True) * v
    y = o.reshape(Bx, T, RW_W) * g
    return y, zf[:, -1], S

def _mlstm_chunk(carry, inp):
    C, n, m = carry
    q, k, v, logi, logf = inp
    L = q.shape[2]
    b = jnp.cumsum(logf, axis=-1)
    mask = jnp.tril(jnp.ones((L, L), dtype=bool))
    logD = jnp.where(mask, b[..., :, None] - b[..., None, :] + logi[..., None, :], -jnp.inf)
    inter = b + m[..., None]
    m_t = jnp.maximum(jnp.max(logD, axis=-1), inter)
    s = jnp.einsum('bhtd,bhsd->bhts', q, k) * jnp.exp(logD - m_t[..., None])
    sc = jnp.exp(inter - m_t)
    num = jnp.einsum('bhts,bhsd->bhtd', s, v) + sc[..., None] * jnp.einsum('bhvk,bhtk->bhtv', C, q)
    den = jnp.sum(s, axis=-1) + sc * jnp.einsum('bhk,bhtk->bht', n, q)
    h = num / jnp.maximum(jnp.abs(den), jnp.exp(-m_t))[..., None]
    m_new = m_t[..., -1]
    wj = jnp.exp(b[..., -1:] - b + logi - m_new[..., None])
    dec = jnp.exp(b[..., -1] + m - m_new)
    C_new = dec[..., None, None] * C + jnp.einsum('bhs,bhsv,bhsk->bhvk', wj, v, k)
    n_new = dec[..., None] * n + jnp.einsum('bhs,bhsk->bhk', wj, k)
    return (C_new, n_new, m_new), h

def _mlstm_branch(z_x, z_v, z_o, z_i, z_f, conv_buf, C0, n0, m0, p):
    c, conv_buf = _causal_conv(z_x, conv_buf, p['mlstm_conv_w'], p['mlstm_conv_b'])
    c = jax.nn.silu(c.astype(F32))
    Bx, T, _ = c.shape
    ch = c.reshape(Bx, T, ML_H, ML_HD)
    q = jnp.einsum('bthi,hij->bhtj', ch, p['mlstm_wq'].astype(F32))
    k = jnp.einsum('bthi,hij->bhtj', ch, p['mlstm_wk'].astype(F32)) * (ML_HD ** -0.5)
    v = z_v.astype(F32).reshape(Bx, T, ML_H, ML_HD).transpose(0, 2, 1, 3)
    logi = (z_i.astype(F32) + p['mlstm_bi']).transpose(0, 2, 1)
    logf = jax.nn.log_sigmoid(z_f.astype(F32) + p['mlstm_bf']).transpose(0, 2, 1)
    L = math.gcd(T, ML_CHUNK)
    nc = T // L

    def chunk(t):
        return jnp.moveaxis(t.reshape((Bx, ML_H, nc, L) + t.shape[3:]), 2, 0)

    (C, n, m), h = lax.scan(_mlstm_chunk, (C0.astype(F32), n0.astype(F32), m0.astype(F32)),
                            (chunk(q), chunk(k), chunk(v), chunk(logi), chunk(logf)))
    h = jnp.moveaxis(h, 0, 2).reshape(Bx, ML_H, T, ML_HD).transpose(0, 2, 1, 3)
    h = _layernorm(h, p['mlstm_norm_g'].reshape(ML_H, ML_HD), None, 1e-6)
    y = jax.nn.sigmoid(z_o.astype(F32)) * (h.reshape(Bx, T, ML_W) + p['mlstm_skip'] * c)
    return y, conv_buf, C, n, m

def _layer(x, lru_buf, lru_h, rw_shift, rw_S, ml_buf, ml_C, ml_n, ml_m, p, is_start):
    dt = x.dtype
    Bx, T, _ = x.shape
    hn = _rmsnorm(x, p['norm_pre_mix'])
    z = jnp.einsum('btd,dp->btp', hn, p['w_in'])
    (z_lx, z_lg, z_gu, z_gv, z_rw, z_mx, z_mv, z_mo, z_mi, z_mf, z_gate) = _split(z, PROJ_SIZES)
    y_a, lru_buf, lru_h = _rglru_branch(z_lx, z_lg, lru_buf, lru_h, p, is_start)
    y_b, gm_v = _gmlp_branch(z_gu, z_gv, p)
    y_c, rw_shift, rw_S = _rwkv7_branch(z_rw, rw_shift, rw_S, p)
    y_d, ml_buf, ml_C, ml_n, ml_m = _mlstm_branch(z_mx, z_mv, z_mo, z_mi, z_mf, ml_buf, ml_C, ml_n, ml_m, p)
    br = jnp.stack([y_a, y_b, y_c, y_d], axis=2).astype(dt)
    br = jnp.einsum('btnc,ncd->btnd', br, p['w_branch'])
    gates = jax.nn.sigmoid(z_gate.reshape(Bx, T, N_BRANCH, D_MODEL))
    merged = jnp.sum(gates * br, axis=2)
    mix = jnp.einsum('btd,de->bte', merged, p['w_out'])
    x = x + _rmsnorm(mix, p['norm_post_mix'])
    hf = _rmsnorm(x, p['norm_pre_ffn'])
    gu = jnp.einsum('btd,df->btf', hf, p['w_ff_in'])
    g, u = jnp.split(gu, 2, axis=-1)
    ff = jnp.einsum('btf,fd->btd', jax.nn.silu(g) * u, p['w_ff_out'])
    x = x + _rmsnorm(ff, p['norm_post_ffn'])
    return x, (lru_buf, lru_h, rw_shift, rw_S, ml_buf, ml_C, ml_n, ml_m), gm_v

def _zero_states(bsz):
    def z(*s):
        return jnp.zeros((bsz,) + s, F32)
    return (z(CONV_W - 1, LRU_W), z(LRU_W), z(RW_P), z(RW_H, RW_HD, RW_HD),
            z(CONV_W - 1, ML_W), z(ML_H, ML_HD, ML_HD), z(ML_H, ML_HD), z(ML_H))

def setup_inputs(seed: int = 0) -> dict:
    key = jax.random.key(seed)
    ks = iter(jax.random.split(key, 64))

    def nrm(shape, scale=1.0):
        return jax.random.normal(next(ks), shape, jnp.float32) * scale

    def unif(shape, lo, hi):
        return jax.random.uniform(next(ks), shape, jnp.float32, lo, hi)

    def gain(shape):
        return 1.0 + 0.05 * nrm(shape)

    Ly = DEPTH
    a8 = unif((Ly, LRU_W), 0.9, 0.999) ** (1.0 / LRU_C)
    return {
        'x_prompt': nrm((BATCH, SEQ, D_MODEL)),
        'x_sample': nrm((DEC_BATCH, DEC_SEQ, D_MODEL)),
        'state_lru_conv': nrm((Ly, DEC_BATCH, CONV_W - 1, LRU_W)),
        'state_lru_h': nrm((Ly, DEC_BATCH, LRU_W), 0.5),
        'state_rwkv_shift': nrm((Ly, DEC_BATCH, RW_P)),
        'state_rwkv_wkv': nrm((Ly, DEC_BATCH, RW_H, RW_HD, RW_HD), 0.5),
        'state_mlstm_conv': nrm((Ly, DEC_BATCH, CONV_W - 1, ML_W)),
        'state_mlstm_C': nrm((Ly, DEC_BATCH, ML_H, ML_HD, ML_HD), 0.1),
        'state_mlstm_n': nrm((Ly, DEC_BATCH, ML_H, ML_HD), 0.1),
        'state_mlstm_m': nrm((Ly, DEC_BATCH, ML_H), 0.5),
        'norm_pre_mix': gain((Ly, D_MODEL)),
        'norm_post_mix': gain((Ly, D_MODEL)),
        'norm_pre_ffn': gain((Ly, D_MODEL)),
        'norm_post_ffn': gain((Ly, D_MODEL)),
        'w_in': nrm((Ly, D_MODEL, P_TOTAL), D_MODEL ** -0.5),
        'lru_conv_w': nrm((Ly, CONV_W, LRU_W), CONV_W ** -0.5),
        'lru_conv_b': nrm((Ly, LRU_W), 0.01),
        'lru_wa': nrm((Ly, LRU_BLOCKS, LRU_BD, LRU_BD), LRU_BD ** -0.5),
        'lru_ba': nrm((Ly, LRU_W), 0.01),
        'lru_wx': nrm((Ly, LRU_BLOCKS, LRU_BD, LRU_BD), LRU_BD ** -0.5),
        'lru_bx': nrm((Ly, LRU_W), 0.01),
        'lru_lambda': jnp.log(a8) - jnp.log1p(-a8),
        'gmlp_ln_g': gain((Ly, GM_W)),
        'gmlp_ln_b': nrm((Ly, GM_W), 0.01),
        'gmlp_ws': nrm((Ly, GM_GROUPS, GM_CHUNK, GM_CHUNK), GM_CHUNK ** -0.5),
        'gmlp_bs': gain((Ly, GM_GROUPS, GM_CHUNK)),
        'rwkv_mu': unif((Ly, RW_P), 0.0, 1.0),
        'rwkv_w0': unif((Ly, RW_W), -6.0, -1.0),
        'rwkv_w2': nrm((Ly, RW_DECAY_R, RW_W), 0.1),
        'rwkv_a0': nrm((Ly, RW_W), 0.1),
        'rwkv_a2': nrm((Ly, RW_A_R, RW_W), 0.1),
        'rwkv_g2': nrm((Ly, RW_G_R, RW_W), RW_G_R ** -0.5),
        'rwkv_kk': 0.85 + 0.05 * nrm((Ly, RW_W)),
        'rwkv_ka': gain((Ly, RW_W)),
        'rwkv_rk': nrm((Ly, RW_H, RW_HD), 0.1),
        'rwkv_ln_g': gain((Ly, RW_W)),
        'rwkv_ln_b': nrm((Ly, RW_W), 0.01),
        'mlstm_conv_w': nrm((Ly, CONV_W, ML_W), CONV_W ** -0.5),
        'mlstm_conv_b': nrm((Ly, ML_W), 0.01),
        'mlstm_wq': nrm((Ly, ML_H, ML_HD, ML_HD), ML_HD ** -0.5),
        'mlstm_wk': nrm((Ly, ML_H, ML_HD, ML_HD), ML_HD ** -0.5),
        'mlstm_bi': nrm((Ly, ML_H), 0.1),
        'mlstm_bf': jnp.linspace(3.0, 6.0, ML_H, dtype=jnp.float32)[None, :] + nrm((Ly, ML_H), 0.05),
        'mlstm_norm_g': gain((Ly, ML_W)),
        'mlstm_skip': gain((Ly, ML_W)),
        'w_branch': nrm((Ly, N_BRANCH, MIX_W, D_MODEL), MIX_W ** -0.5),
        'w_out': nrm((Ly, D_MODEL, D_MODEL), D_MODEL ** -0.5),
        'w_ff_in': nrm((Ly, D_MODEL, 2 * D_FF), D_MODEL ** -0.5),
        'w_ff_out': nrm((Ly, D_FF, D_MODEL), D_FF ** -0.5),
    }

def reference(x_prompt, x_sample, state_lru_conv, state_lru_h, state_rwkv_shift, state_rwkv_wkv,
              state_mlstm_conv, state_mlstm_C, state_mlstm_n, state_mlstm_m,
              norm_pre_mix, norm_post_mix, norm_pre_ffn, norm_post_ffn, w_in,
              lru_conv_w, lru_conv_b, lru_wa, lru_ba, lru_wx, lru_bx, lru_lambda,
              gmlp_ln_g, gmlp_ln_b, gmlp_ws, gmlp_bs,
              rwkv_mu, rwkv_w0, rwkv_w2, rwkv_a0, rwkv_a2, rwkv_g2, rwkv_kk, rwkv_ka,
              rwkv_rk, rwkv_ln_g, rwkv_ln_b,
              mlstm_conv_w, mlstm_conv_b, mlstm_wq, mlstm_wk, mlstm_bi, mlstm_bf,
              mlstm_norm_g, mlstm_skip,
              w_branch, w_out, w_ff_in, w_ff_out):
    weights = (norm_pre_mix, norm_post_mix, norm_pre_ffn, norm_post_ffn, w_in,
               lru_conv_w, lru_conv_b, lru_wa, lru_ba, lru_wx, lru_bx, lru_lambda,
               gmlp_ln_g, gmlp_ln_b, gmlp_ws, gmlp_bs,
               rwkv_mu, rwkv_w0, rwkv_w2, rwkv_a0, rwkv_a2, rwkv_g2, rwkv_kk, rwkv_ka,
               rwkv_rk, rwkv_ln_g, rwkv_ln_b,
               mlstm_conv_w, mlstm_conv_b, mlstm_wq, mlstm_wk, mlstm_bi, mlstm_bf,
               mlstm_norm_g, mlstm_skip,
               w_branch, w_out, w_ff_in, w_ff_out)
    sample_states = (state_lru_conv, state_lru_h, state_rwkv_shift, state_rwkv_wkv,
                     state_mlstm_conv, state_mlstm_C, state_mlstm_n, state_mlstm_m)
    bp = x_prompt.shape[0]
    yp, ys = x_prompt, x_sample
    new_p = [[] for _ in range(N_STATE)]
    new_s = [[] for _ in range(N_STATE)]
    gm_v = []
    for l in range(DEPTH):
        p = dict(zip(LAYER_PARAM_NAMES, [w[l] for w in weights]))
        yp, st_p, _ = _layer(yp, *_zero_states(bp), p, True)
        ys, st_s, v_s = _layer(ys, *[s[l] for s in sample_states], p, False)
        for j in range(N_STATE):
            new_p[j].append(st_p[j].astype(x_prompt.dtype))
            new_s[j].append(st_s[j].astype(x_sample.dtype))
        gm_v.append(v_s.astype(x_sample.dtype))
    (p_lru_conv, p_lru_h, p_rwkv_shift, p_rwkv_wkv,
     p_mlstm_conv, p_mlstm_C, p_mlstm_n, p_mlstm_m) = [jnp.stack(t, axis=0) for t in new_p]
    (s_lru_conv, s_lru_h, s_rwkv_shift, s_rwkv_wkv,
     s_mlstm_conv, s_mlstm_C, s_mlstm_n, s_mlstm_m) = [jnp.stack(t, axis=0) for t in new_s]
    s_gmlp_v = jnp.stack(gm_v, axis=0)
    return (yp, ys,
            p_lru_conv, p_lru_h, p_rwkv_shift, p_rwkv_wkv, p_mlstm_conv, p_mlstm_C, p_mlstm_n, p_mlstm_m,
            s_lru_conv, s_lru_h, s_rwkv_shift, s_rwkv_wkv, s_mlstm_conv, s_mlstm_C, s_mlstm_n, s_mlstm_m,
            s_gmlp_v)


_drawn_inputs = setup_inputs


def setup_inputs(seed=0):
    import zlib

    import numpy as np

    out = dict(_drawn_inputs(seed))
    spreads = {}
    factors = {'lru_ba': 8.0,
     'lru_bx': 8.0,
     'gmlp_ln_b': 5.722,
     'rwkv_ln_g': 2.965,
     'rwkv_ln_b': 8.0,
     'mlstm_norm_g': 2.736,
     'mlstm_skip': 5.035}
    for name, (base, spread) in spreads.items():
        noise = np.random.default_rng([zlib.crc32(name.encode()), seed]).standard_normal(out[name].shape)
        drawn = base * np.exp(spread * noise) if base else spread * noise
        out[name] = __import__('jax').numpy.asarray(drawn.astype(out[name].dtype))
    for name, factor in factors.items():
        out[name] = (out[name] * factor).astype(out[name].dtype)
    return out
```

```python
from contextlib import ExitStack

import numpy as np

import concourse.bass as bass
from concourse import mybir

F32 = mybir.dt.float32
F32R = mybir.dt.float32r
ALU = mybir.AluOpType
ACT = mybir.ActivationFunctionType
AX = mybir.AxisListType

P = 128
D = 2048
KD = D // P
TP = 256
NS, LS = 8, 8
T = TP + NS * LS
MIX = 512
C4 = MIX // P
DFF = 5632
HALF = DFF // P // 2
CW = 4
PAD3 = 3 + TP + NS * (3 + LS)
PAD1 = 1 + TP + NS * (1 + LS)
HD = 64
NSEQ = 1 + NS
PIECE = 8
RING = 4
AHEAD = 3
EXPM05 = float(np.exp(-0.5))

ZB = {"lx": 0, "lg": 4, "gu": 8, "gv": 12, "mx": 16, "mv": 20, "mo": 24, "r": 28, "k": 32, "v": 36,
      "gd": 40, "low": 41}
NZ = 42

Z0 = 0
PASS0 = Z0 + 2 * NZ
OUT0 = PASS0 + 4 * KD * 3
FF0 = OUT0 + 2 * KD
FFIN = 4 * HALF
FFOUT = 3 * KD
NPIECES = FF0 + 2 * (FFIN + FFOUT)
OUT_TILES = [8, 8, HALF - 16]


def layout(widths):
    at, n = {}, 0
    for name, w in widths:
        at[name] = (n, w)
        n += w
    return at, n


VEC, NVEC = layout([("g_pre", KD), ("g_post", KD), ("g_pre2", KD), ("g_post2", KD),
                    ("cw_l", 16), ("cb_l", 4), ("ba", 4), ("bx", 4), ("lam", 4),
                    ("ln_g", 4), ("ln_b", 4), ("cw_m", 16), ("cb_m", 4), ("norm_g", 4), ("skip", 4),
                    ("mu_gd", 1), ("mu_low", 1), ("bi", 1), ("bf", 1),
                    ("mu_r", 8), ("mu_k", 8), ("mu_v", 8), ("w0", 8), ("a0", 8), ("kk", 8), ("ka", 8),
                    ("rk", 8), ("rln_g", 8), ("rln_b", 8),
                    ("eps6", 1), ("eps5", 1), ("eps64", 1)])
CON, NCON = layout([("ident", 128), ("ones", 128), ("maskD", 256), ("maskS", 64),
                    ("n_near", 64), ("n_far", 64), ("nT_near", 64), ("sT", 64), ("iT", 64),
                    ("n_seq", 64), ("nT_seq", 64),
                    ("seq", 8)])
ROWC, NROWC = layout([("sel", 4 * 128), ("keep", T), ("drop", T)])
OUTS, NOUT = layout([("lconv", C4 * NSEQ * 3), ("lh", C4 * NSEQ), ("mconv", C4 * NSEQ * 3), ("n", 4 * NSEQ),
                     ("m", NSEQ), ("shift64", 24 * NSEQ), ("shift_gd", NSEQ), ("shift_low", NSEQ)])


def build(nc, a):
    sems = {}
    ctx = ExitStack()
    with ctx:
        def S(name):
            if name not in sems:
                sems[name] = ctx.enter_context(nc.semaphore(name))
            return sems[name]

        def sb(name, shape, dt=F32, c=ctx):
            return c.enter_context(nc.sbuf_tensor(name, shape, dt))

        w_raw = sb("w_raw", [P, RING, PIECE * P])
        w_hi = sb("w_hi", [P, RING, PIECE * P], F32R)
        w_lo = sb("w_lo", [P, RING, PIECE * P], F32R)
        x_hi = sb("x_hi", [P, KD, T], F32R)
        x_lo = sb("x_lo", [P, KD, T], F32R)
        rstd = sb("rstd", [P, T])
        vec = sb("vec", [P, NVEC])
        con = sb("con", [P, NCON])
        zev = sb("zev", [P, 2, T])

        def V(name, i=0, n=1, parts=P):
            return vec[0:parts, VEC[name][0] + i:VEC[name][0] + i + n]

        def K(name, parts=P):
            at, n = CON[name]
            return con[0:parts, at:at + n]

        gate = sb("gate", [P, 2, T])
        term = sb("term", [P, 2, T])
        ssum2 = sb("ssum2", [P, T])
        small = sb("small", [P, NOUT])

        p1 = ExitStack()
        y_hi = sb("y_hi", [P, 4 * C4, T], F32R, p1)
        y_lo = sb("y_lo", [P, 4 * C4, T], F32R, p1)
        ARENA = 17400
        arena = sb("arena", [P, ARENA], c=p1)
        p1.close()
        p2 = ExitStack()
        a_hi = sb("a_hi", [P, HALF, T], F32R, p2)
        a_lo = sb("a_lo", [P, HALF, T], F32R, p2)
        xres = sb("xres", [P, KD, T], c=p2)
        mix = sb("mix", [P, KD, T], c=p2)
        p2.close()
        merged = mix

        def psum(i):
            return ctx.enter_context(nc.psum_tensor(f"bank{i}", [P, 512], F32))

        G = [psum(i) for i in range(4)]
        M = [psum(4 + i) for i in range(4)]

        class Views:

            def __init__(self, at=0, limit=ARENA):
                self.at, self.limit = at, limit

            def take(self, *shape, parts=P):
                n = int(np.prod(shape))
                v = arena[0:parts, self.at:self.at + n]
                self.at += n
                assert self.at <= self.limit, (self.at, self.limit)
                if len(shape) == 2:
                    v = v.rearrange("p (a b) -> p a b", a=shape[0])
                if len(shape) == 3:
                    v = v.rearrange("p (a b c) -> p a b c", a=shape[0], b=shape[1])
                return v

        start = Views()
        xin = start.take(KD, T)
        xsq = start.take(KD, T)
        ssum = start.take(T)
        va = Views()
        a_cin = va.take(C4, PAD3)
        a_acc = va.take(C4, PAD3)
        a_xc = va.take(C4, T)
        a_gz = va.take(C4, T)
        a_r = va.take(C4, T)
        a_i = va.take(C4, T)
        a_a = va.take(C4, T)
        a_st = va.take(C4, NS, 3)
        a_h0 = va.take(C4, NS)
        a_wa = va.take(C4, P)
        a_wx = va.take(C4, P)
        a_t = va.take(6, C4)
        a_sm = va.take(C4, NS)
        vb = Views()
        b_u = vb.take(C4, T)
        b_v = vb.take(C4, T)
        b_q = vb.take(C4, T)
        b_std = vb.take(T)
        b_tok = vb.take(3, MIX)
        b_ws = vb.take(C4, P)
        b_wss = vb.take(C4, 64, parts=64)
        b_bias = vb.take(C4, T, parts=1)
        vd = Views()
        d_cin = vd.take(C4, PAD3)
        d_acc = vd.take(C4, PAD3)
        d_c = vd.take(C4, T)
        d_v = vd.take(C4, T)
        d_o = vd.take(C4, T)
        d_st = vd.take(C4, NS, 3)
        d_wq = vd.take(P)
        d_wk = vd.take(P)
        d_C = vd.take(NS, P)
        d_n = vd.take(4, NS)
        d_m0b = vd.take(NS, 4)
        d_rows = vd.take(7, T, parts=4)
        d_m0 = vd.take(NSEQ, parts=4)
        d_mend = vd.take(NSEQ, parts=4)
        d_md = vd.take(NSEQ, 4, parts=4)
        d_g = vd.take(12)
        d_me = vd.take(NSEQ, 4)
        d_wp = vd.take(2, 4)
        d_wm = vd.take(NS, 4, parts=64)
        d_dec = vd.take(NS, 4)
        ve = Views(limit=2 * C4 * PAD3)
        e_q = ve.take(T)
        e_k = ve.take(T)
        e_ktok = ve.take(3, P)
        e_vtok = ve.take(3, P)
        e_E = ve.take(448)
        e_em = ve.take(T)
        d_vm = vd.take(NS + 2, P)
        d_h = vd.take(T)
        d_s = vd.take(T)
        d_qs = vd.take(64)
        d_qn = vd.take(64)
        d_rc = vd.take(NROWC, parts=4)
        vc = Views()
        c_zp = vc.take(4, PAD1, parts=64)
        c_d96 = arena[0:96, vc.at:vc.at + PAD1]
        c_d = vc.take(4, PAD1, parts=64)
        c_gdp = vc.take(PAD1, parts=96)
        c_lowp = vc.take(PAD1, parts=64)
        vc.take(42)
        vh = Views(limit=vc.at)
        (h_N, h_Q, h_F, h_ak, h_rb, h_rk, h_T, h_P2, h_Q2, h_E, h_btok, h_ktok, h_vtok) = [
            vh.take(4, 64, parts=64) for _ in range(13)]
        c_r, c_k, c_v, c_w, c_a, c_kk, c_t, c_rk = [vc.take(4, T, parts=64) for _ in range(8)]
        c_gd = vc.take(T, parts=96)
        c_low = vc.take(T, parts=64)
        c_g2 = vc.take(256, parts=96)
        c_lora = vc.take(256, parts=64)
        c_wend = vc.take(4, 4 + NS, parts=64)
        c_S = vc.take(4, 64, parts=64)
        c_Ss = vc.take(4, NS, HD, parts=64)
        c_sh = vc.take(24, NS, parts=64)
        c_shlow = vc.take(NS, parts=64)
        c_shgd = vc.take(NS, parts=96)
        c_um = c_a.rearrange("p a b -> p (a b)")[:, 0:2 * NS * HD].rearrange("p (a b) -> p a b", a=2)

        def O(name, parts=P):
            at, n = OUTS[name]
            return small[0:parts, at:at + n]

        zD = a["z_scratch"]

        def bc(ap, axis, n):
            x = ap.unsqueeze(axis)
            shape = list(x.shape)
            shape[axis] = n
            return x.broadcast_to(shape)

        def seqs(ap, w):
            return ap.rearrange("p c (b e) -> p c b e", e=w)

        plan = {}
        uses = [0] * 4

        def planned(b, *key):
            plan[key] = (b, uses[b])
            uses[b] += 1

        for c in range(C4):
            planned(c, "A_r", c)
            planned(c, "A_i", c)
        planned(0, "B_sum")
        planned(1, "B_var")
        for t, b in enumerate((2, 3, 0)):
            planned(b, "B_turned", t)
        for c in range(C4):
            planned(c, "B_s", c)
        planned(0, "D_turned")
        for h in range(4):
            for b, name in ((0, "D_q"), (1, "D_k"), (2, "D_ktok"), (3, "D_vtok"), (0, "D_Mb"), (1, "D_eb"), (2, "D_sb"),
                            (3, "D_qk"), (0, "D_num"), (1, "D_den"), (2, "D_mean"), (3, "D_var")):
                planned(b, name, h)
            planned(0, "D_Cs", h, 0)
            planned(1, "D_Cs", h, 1)
            planned(2, "D_Cp", h)
        for g in range(2):
            for h in range(4):
                for key in (("C_lora", g, 0, h), ("C_lora", g, 1, h), ("C_kk_sum", g, h), ("C_rk_sum", g, h)):
                    planned(h, *key)
            for ch in range(5):
                n = 5 * g + ch
                for b, name in ((0, "C_N"), (1, "C_NT"), (2, "C_ak"), (3, "C_rb"), (0, "C_rk"), (1, "C_btok"),
                                (2, "C_ktok"), (3, "C_vtok"), (0, "C_p2"), (1, "C_q2"), (2, "C_t2"), (0, "C_p4"),
                                (1, "C_q4"), (2, "C_t4")):
                    planned(b, name, n)
                if ch < 4:
                    for b, name in ((0, "C_p8"), (2, "C_t8"), (0, "C_zT"), (1, "C_z"), (2, "C_z2"), (0, "C_e"),
                                    (3, "C_rhs"), (1, "C_y"), (2, "C_u"), (3, "C_o"), (0, "C_S")):
                        planned(b, name, n)
                else:
                    for b, name in ((0, "C_u0"), (3, "C_rhs"), (1, "C_y"), (3, "C_o")):
                        planned(b, name, n)
                    for h in range(4):
                        planned(h % 2, "C_Ss", g, h)
            for h in range(4):
                for name in ("C_mean", "C_var", "C_gate"):
                    planned(h, name, g, h)

        def full(eng, *key):
            b, i = plan[key]
            eng.wait_ge(S(f"bank_full{b}"), i + 1)

        def read(*key):
            return S(f"bank_read{plan[key][0]}")

        def use(*key):
            b, i = plan[key]
            return f"bank_read{b}", i + 1

        def was_read(eng, *key):
            b, i = plan[key]
            eng.wait_ge(S(f"bank_read{b}"), i + 1)

        def mixers_pe(pe):
            ident, ones = K("ident"), K("ones")
            ident64, ones64 = K("ident", 64)[:, 0:64], K("ones", 64)[:, 0:64]

            def bank(*key):
                b, i = plan[key]
                if i:
                    pe.wait_ge(S(f"bank_read{b}"), i)
                return M[b]

            def filled(mm, *key):
                mm.then_inc(S(f"bank_full{plan[key][0]}"), 1)

            def single(lhs, rhs, *key, parts=P):
                o = bank(*key)
                filled(pe.matmul(o[0:parts, 0:T], lhs, rhs, start=True, stop=True), *key)

            pe.wait_ge(S("A_weights_in"), 32)
            pe.wait_ge(S("A_conv"), 2 * C4)
            pe.wait_ge(S("x_std"), 1)
            for c in range(C4):
                single(a_wa[:, c, :], a_xc[:, c, :], "A_r", c)
            for c in range(C4):
                single(a_wx[:, c, :], a_xc[:, c, :], "A_i", c)

            pe.wait_ge(S("B_gelu"), 1)
            o = bank("B_sum")
            for c in range(C4):
                mm = pe.matmul(o[:, 0:T], ones, b_v[:, c, :], start=c == 0, stop=c == C4 - 1)
            filled(mm, "B_sum")
            pe.wait_ge(S("B_sq"), 1)
            o = bank("B_var")
            for c in range(C4):
                mm = pe.matmul(o[:, 0:T], ones, b_q[:, c, :], start=c == 0, stop=c == C4 - 1)
            filled(mm, "B_var")
            pe.wait_ge(S("B_v"), C4)
            for t, (t0, n) in enumerate(((0, P), (P, P), (TP, 64))):
                o = bank("B_turned", t)
                for c in range(C4):
                    mm = pe.transpose(o[0:n, c * P:(c + 1) * P], b_v[:, c, t0:t0 + n], ident)
                filled(mm, "B_turned", t)
            for t in range(3):
                was_read(pe, "B_turned", t)
            pe.wait_ge(S("B_masked"), 2)
            pe.wait_ge(S("B_bias_in"), 16)
            for c in range(C4):
                f = slice(c * P, (c + 1) * P)
                o = bank("B_s", c)
                pe.matmul(o[:, 0:T], K("ones", 1), b_bias[:, c, :], start=True, stop=False)
                pe.matmul(o[:, 0:P], b_tok[:, 0, f], b_ws[:, c, :], start=False, stop=False)
                pe.matmul(o[:, P:TP], b_tok[:, 1, f], b_ws[:, c, :], start=False, stop=False)
                filled(pe.matmul(o[:, TP:T], b_tok[0:64, 2, f], b_wss[:, c, :], start=False, stop=True), "B_s", c)

            pe.wait_ge(S("D_rows"), 1)
            token_tiles = ((0, P), (P, P), (TP, 64))
            o = bank("D_turned")
            for t, (t0, n) in enumerate(token_tiles):
                pe.transpose(o[0:n, 4 * t:4 * t + 4], d_rows[:, 1, t0:t0 + n], K("ident", 4)[:, 0:4])
            filled(pe.matmul(o[:, 16:16 + 4 * NSEQ], K("ones", 4), d_md.rearrange("p a b -> p (a b)"),
                             start=True, stop=True), "D_turned")
            pe.wait_ge(S("D_silu"), 1)
            for h in range(4):
                pe.wait_ge(S("D_wq_in"), 32 * (h + 1))
                single(d_wq, d_c[:, h, :], "D_q", h)
                single(d_wk, d_c[:, h, :], "D_k", h)
                o = bank("D_ktok", h)
                for t, (t0, n) in enumerate(token_tiles):
                    mm = pe.matmul(o[0:n, t * P:(t + 1) * P], d_c[:, h, t0:t0 + n], d_wk, start=True, stop=True,
                                   skip_group_check=True)
                filled(mm, "D_ktok", h)
                o = bank("D_vtok", h)
                for t, (t0, n) in enumerate(token_tiles):
                    mm = pe.transpose(o[0:n, t * P:(t + 1) * P], d_v[:, h, t0:t0 + n], ident)
                filled(mm, "D_vtok", h)
                sel = d_rc[:, h * P:(h + 1) * P]
                single(sel, d_rows[:, 0, :], "D_Mb", h)
                single(sel, d_rows[:, 5, :], "D_eb", h)
                o = bank("D_sb", h)
                filled(pe.matmul(o[:, 0:64], sel, d_rows[:, 6, TP:T], start=True, stop=True), "D_sb", h)
                was_read(pe, "D_q", h)
                was_read(pe, "D_k", h)
                o = bank("D_qk", h)
                pe.matmul(o[:, 0:TP], e_k[:, 0:P], e_q[:, 0:TP], start=True, stop=True, skip_group_check=True)
                pe.matmul(o[:, TP:TP + P], e_k[:, P:TP], e_q[:, P:TP], start=True, stop=True, skip_group_check=True)
                filled(pe.matmul(o[0:64, 384:448], e_k[:, TP:T], e_q[:, TP:T], start=True, stop=True,
                                 skip_group_check=True), "D_qk", h)
                was_read(pe, "D_qk", h)
                was_read(pe, "D_vtok", h)
                was_read(pe, "D_sb", h)
                pe.wait_ge(S("D_C_in"), 16 * (h + 1))
                o = bank("D_num", h)
                pe.matmul(o[:, 0:TP], e_vtok[:, 0, :], e_E[:, 0:TP], start=True, stop=False)
                pe.matmul(o[:, P:TP], e_vtok[:, 1, :], e_E[:, TP:TP + P], start=False, stop=False)
                pe.matmul(o[:, TP:T], e_vtok[0:64, 2, :], e_E[0:64, 384:448], start=False, stop=False)
                for b in range(NS):
                    mm = pe.matmul(o[:, TP + LS * b:TP + LS * b + LS], d_C[:, b, :], d_qs[:, LS * b:LS * b + LS],
                                   start=False, stop=b == NS - 1)
                filled(mm, "D_num", h)
                pe.wait_ge(S("D_qn"), h + 1)
                o = bank("D_den", h)
                pe.matmul(o[:, 0:TP], ones, e_E[:, 0:TP], start=True, stop=False)
                pe.matmul(o[:, P:TP], ones, e_E[:, TP:TP + P], start=False, stop=False)
                pe.matmul(o[:, TP:T], K("ones", 64), e_E[0:64, 384:448], start=False, stop=False)
                filled(pe.matmul(o[:, TP:T], ones, d_qn, start=False, stop=True), "D_den", h)
                was_read(pe, "D_num", h)
                single(ones, d_h, "D_mean", h)
                pe.wait_ge(S("D_sq"), h + 1)
                single(ones, d_s, "D_var", h)
                was_read(pe, "D_ktok", h)
                pe.wait_ge(S("D_vm"), 3 * (h + 1))
                for i in range(2):
                    o = bank("D_Cs", h, i)
                    filled(pe.matmul(o[:, :], e_ktok[0:64, 2, :], d_vm[0:64, 4 * i:4 * i + 4, :].rearrange("p a b -> p (a b)"),
                                     start=True, stop=True), "D_Cs", h, i)
                o = bank("D_Cp", h)
                for t in range(2):
                    pe.matmul(o[:, 0:P], e_ktok[:, t, :], d_vm[:, NS + t, :], start=t == 0, stop=t == 1,
                              skip_group_check=True)
                pe.matmul(o[:, P:P + NS], e_ktok[0:64, 2, :], d_wm[:, :, h], start=True, stop=True, skip_group_check=True)
                for t in range(2):
                    mm = pe.matmul(o[:, P + NS:P + NS + 1], e_ktok[:, t, :], d_wp[:, t, h:h + 1], start=t == 0,
                                   stop=t == 1, skip_group_check=True)
                filled(mm, "D_Cp", h)

            hs = range(4)
            for g in range(2):
                pe.wait_ge(S("C_low"), 2 * (g + 1))
                for what in range(2):
                    r = slice(32 * what, 32 * what + 32)
                    for h in hs:
                        single(c_lora[r, 64 * h:64 * h + 64], c_low[r, :], "C_lora", g, what, h, parts=64)
                pe.wait_ge(S("C_kk_sq"), g + 1)
                for h in hs:
                    single(ones64, c_t[:, h, :], "C_kk_sum", g, h, parts=64)
                pe.wait_ge(S("C_rk"), g + 1)
                for h in hs:
                    single(ones64, c_rk[:, h, :], "C_rk_sum", g, h, parts=64)
                pe.wait_ge(S("C_scaled"), g + 1)
                for ch in range(5):
                    n = 5 * g + ch
                    ts = slice(64 * ch, 64 * ch + 64)
                    smp = ch == 4
                    At, Bt, Kt, Rt, Vt = [lambda h, x=x: x[:, h, ts] for x in (c_w, c_kk, c_k, c_r, c_v)]

                    def of(x):
                        return lambda h: x[:, h, :]

                    def four(name, lhs, rhs, *more):
                        o = bank(name, n)
                        for h in hs:
                            pairs = ((lhs, rhs),) + more
                            for i, (l, r) in enumerate(pairs):
                                mm = pe.matmul(o[0:64, 64 * h:64 * h + 64], l(h), r(h), start=i == 0,
                                               stop=i == len(pairs) - 1, skip_group_check=True)
                        filled(mm, name, n)

                    four("C_N", At, Bt)
                    four("C_NT", Bt, At)
                    four("C_ak", Kt, At)
                    four("C_rb", Bt, Rt)
                    four("C_rk", Kt, Rt)
                    for name, x in (("C_btok", Bt), ("C_ktok", Kt), ("C_vtok", Vt)):
                        o = bank(name, n)
                        for h in hs:
                            mm = pe.transpose(o[0:64, 64 * h:64 * h + 64], x(h), ident64)
                        filled(mm, name, n)
                    pe.wait_ge(S("C_QI"), n + 1)
                    four("C_p2", of(h_Q), of(h_N))
                    four("C_q2", of(h_N), of(h_Q))
                    was_read(pe, "C_p2", n)
                    was_read(pe, "C_q2", n)
                    four("C_t2", of(h_P2), of(h_T))
                    four("C_p4", of(h_Q2), of(h_P2))
                    four("C_q4", of(h_P2), of(h_Q2))
                    was_read(pe, "C_p4", n)
                    was_read(pe, "C_q4", n)
                    was_read(pe, "C_t2", n)
                    four("C_t4", of(h_P2), of(h_T))
                    if not smp:
                        four("C_p8", of(h_Q2), of(h_P2))
                        was_read(pe, "C_p8", n)
                        was_read(pe, "C_t4", n)
                        four("C_t8", of(h_P2), of(h_T))
                        was_read(pe, "C_t8", n)
                        four("C_zT", of(h_F), of(h_T))
                        four("C_z", of(h_T), of(h_F))
                        was_read(pe, "C_zT", n)
                        was_read(pe, "C_z", n)
                        four("C_z2", of(h_P2), of(h_Q2))
                        was_read(pe, "C_z2", n)
                        pe.wait_ge(S("C_E"), 4 * g + ch + 1)
                        four("C_e", of(h_N), of(h_E))
                        pe.wait_ge(S("C_S_ready"), 5 * g + ch + 1)
                        four("C_rhs", of(h_ak), of(h_vtok), (At, of(c_S)))
                        was_read(pe, "C_rhs", n)
                        four("C_y", of(h_T), of(h_P2))
                        was_read(pe, "C_e", n)
                        was_read(pe, "C_y", n)
                        four("C_u", of(h_E), of(h_Q2))
                        was_read(pe, "C_u", n)
                        four("C_o", of(h_vtok), of(h_rk), (of(h_F), of(h_rb)), (of(c_S), Rt))
                        four("C_S", of(h_btok), of(h_F), (of(h_ktok), of(h_vtok)))
                    else:
                        pe.wait_ge(S("C_Ss_in"), 16 * (g + 1))
                        o = bank("C_u0", n)
                        for h in hs:
                            for b in range(NS):
                                mm = pe.matmul(o[0:64, 64 * h + LS * b:64 * h + LS * b + LS], c_Ss[:, h, b, :],
                                               c_w[:, h, TP + LS * b:TP + LS * b + LS], start=True, stop=True,
                                               skip_group_check=True)
                        filled(mm, "C_u0", n)
                        was_read(pe, "C_u0", n)
                        was_read(pe, "C_t4", n)
                        four("C_rhs", of(h_ak), of(h_vtok), (of(h_N), lambda h: ident64))
                        was_read(pe, "C_rhs", n)
                        four("C_y", of(h_T), of(h_P2))
                        was_read(pe, "C_y", n)
                        o = bank("C_o", n)
                        for h in hs:
                            oh = o[0:64, 64 * h:64 * h + 64]
                            pe.matmul(oh, h_vtok[:, h, :], h_rk[:, h, :], start=True, stop=False, skip_group_check=True)
                            pe.matmul(oh, h_F[:, h, :], h_rb[:, h, :], start=False, stop=False, skip_group_check=True)
                            for b in range(NS):
                                mm = pe.matmul(o[0:64, 64 * h + LS * b:64 * h + LS * b + LS], c_Ss[:, h, b, :],
                                               c_r[:, h, TP + LS * b:TP + LS * b + LS], start=False, stop=b == NS - 1,
                                               skip_group_check=True)
                        filled(mm, "C_o", n)
                        for h in hs:
                            pe.wait_ge(S("C_um"), 2 * (4 * g + h) + 2)
                            o = bank("C_Ss", g, h)
                            pe.matmul(o[0:64, :], h_btok[:, h, :], c_um[:, 0, :], start=True, stop=False)
                            filled(pe.matmul(o[0:64, :], h_ktok[:, h, :], c_um[:, 1, :], start=False, stop=True),
                                   "C_Ss", g, h)
                was_read(pe, "C_o", 5 * g + 4)
                for h in hs:
                    single(ones64, c_t[:, h, :], "C_mean", g, h, parts=64)
                pe.wait_ge(S("C_osq"), g + 1)
                for h in hs:
                    single(ones64, c_k[:, h, :], "C_var", g, h, parts=64)
                for h in hs:
                    single(c_g2[:, 64 * h:64 * h + 64], c_gd, "C_gate", g, h, parts=64)

        def padded(eng, dst, rows, pad, sem):
            src = zD[rows] if isinstance(rows, int) else rows
            eng.dma_start(dst[:, pad:pad + TP], src[:, 0:TP]).then_inc(sem, 16)
            eng.dma_start(dst[:, pad + TP:].rearrange("p (b e) -> p b e", b=NS)[:, :, pad:],
                          src[:, TP:T].rearrange("p (b e) -> p b e", b=NS)).then_inc(sem, 16)

        def whole(name):
            return zD[ZB[name]:ZB[name] + 4].rearrange("c p t -> p c t")

        def mixers_act(act):
            sc = nc.scalar
            act.wait_ge(S("x_lo_made"), KD)
            act.wait_ge(S("x_ss"), 1)
            for c in range(C4):
                padded(act, a_cin[:, c, :], ZB["lx"] + c, 3, S("A_in"))
            act.dma_start(a_st, a["lru_st"]).then_inc(S("A_in"), 16)
            act.dma_start(a_h0, a["lru_h"]).then_inc(S("A_in"), 16)
            act.dma_start(a_gz, whole("lg")).then_inc(S("A_gz_in"), 16)
            act.dma_start(a_wa, a["lru_wa"]).then_inc(S("A_weights_in"), 16)
            act.dma_start(a_wx, a["lru_wx"]).then_inc(S("A_weights_in"), 16)
            act.wait_ge(S("A_abs"), 1)
            sc.activation(a_t[:, 1, :], a_t[:, 0, :], ACT.Exp, scale=-1.0).then_inc(S("A_exp"), 1)
            act.wait_ge(S("A_gz_in"), 16)
            sc.activation(a_gz, a_gz, ACT.Gelu_apprx_tanh).then_inc(S("A_gelu"), 1)
            for c in range(C4):
                full(act, "A_r", c)
                sc.activation(a_r[:, c, :], M[c][:, 0:T], ACT.Sigmoid, bias=V("ba", c)).then_inc(read("A_r", c), 1)
            for c in range(C4):
                full(act, "A_i", c)
                sc.activation(a_i[:, c, :], M[c][:, 0:T], ACT.Sigmoid, bias=V("bx", c)).then_inc(read("A_i", c), 1)
            act.wait_ge(S("A_soft"), 1)
            for c in range(C4):
                was_read(act, "A_r", c)
                sc.activation(a_r[:, c, :], a_r[:, c, :], ACT.Tanh, scale=a_t[:, 4, c:c + 1]).then_inc(S("A_p"), 1)
            act.wait_ge(S("A_p"), C4)
            act.wait_ge(S("A_conv"), 2 * C4)
            sc.activation(a_acc[:, :, 0:T], a_r, ACT.Sqrt).then_inc(S("A_root"), 1)
            act.wait_ge(S("A_y"), 1)
            for c in range(C4):
                sc.activation(y_hi[:, c, :], a_i[:, c, :], ACT.Copy).then_inc(S("y_hi0"), 1)

            act.wait_ge(S("y_lo0"), C4)
            act.dma_start(b_v, whole("gv")).then_inc(S("B_v_in"), 16)
            act.dma_start(b_u, whole("gu")).then_inc(S("B_u_in"), 16)
            act.dma_start(b_ws, a["ws"]).then_inc(S("B_ws_in"), 16)
            act.dma_start(b_wss, a["wss"]).then_inc(S("B_ws_in"), 16)
            act.dma_start(b_bias, a["gbias"]).then_inc(S("B_bias_in"), 16)
            act.wait_ge(S("B_v_in"), 16)
            sc.activation(b_v, b_v, ACT.Gelu_apprx_tanh).then_inc(S("B_gelu"), 1)
            act.wait_ge(S("B_u_in"), 16)
            sc.activation(b_u, b_u, ACT.Gelu_apprx_tanh).then_inc(S("B_gelu_u"), 1)
            full(act, "B_var")
            sc.activation(b_std, M[1][:, 0:T], ACT.Sqrt, scale=1.0 / MIX, bias=V("eps5")).then_inc(read("B_var"), 1)
            for t, (n, bank) in enumerate(((P, 2), (P, 3), (64, 0))):
                full(act, "B_turned", t)
                sc.activation(b_tok[0:n, t, :], M[bank][0:n, :], ACT.Copy).then_inc(read("B_turned", t), 1)
            act.dma_start(a["gv"], b_v[:, :, TP:T]).then_inc(S("B_out"), 16)
            for c in range(C4):
                was_read(act, "B_s", c)
                sc.activation(y_hi[:, 4 + c, :], b_q[:, c, :], ACT.Copy).then_inc(S("y_hi1"), 1)

            act.wait_ge(S("y_lo1"), C4)
            act.wait_ge(S("B_out"), 16)
            for c in range(C4):
                padded(act, d_cin[:, c, :], ZB["mx"] + c, 3, S("D_in"))
            act.dma_start(d_st, a["ml_st"]).then_inc(S("D_in"), 16)
            low = zD[ZB["low"]]
            act.dma_start(d_rows[:, 0, :], low[64:68, :]).then_inc(S("D_rows_in"), 16)
            act.dma_start(d_rows[:, 1, :], low[96:100, :]).then_inc(S("D_rows_in"), 16)
            act.dma_start(d_rc, a["rowc"]).then_inc(S("D_rows_in"), 16)
            act.dma_start(d_m0, a["ml_m"]).then_inc(S("D_rows_in"), 16)
            act.dma_start(d_m0b, a["ml_mb"]).then_inc(S("D_rows_in"), 16)
            act.dma_start(d_n, a["ml_n"]).then_inc(S("D_n_in"), 16)
            act.dma_start(d_v, whole("mv")).then_inc(S("D_v_in"), 16)
            act.dma_start(d_o, whole("mo")).then_inc(S("D_o_in"), 16)
            act.dma_start(d_wq, a["ml_wq"][0]).then_inc(S("D_wq_in"), 16)
            act.dma_start(d_wk, a["ml_wk"][0]).then_inc(S("D_wq_in"), 16)
            act.dma_start(d_C, a["ml_C"][:, 0]).then_inc(S("D_C_in"), 16)
            act.wait_ge(S("D_abs"), 1)
            sc.activation(d_rows[:, 4, :], d_rows[:, 3, :], ACT.Exp, scale=-1.0).then_inc(S("D_exp"), 1)
            act.wait_ge(S("D_bm"), 2)
            sc.activation(d_rows[:, 5, :], d_rows[:, 5, :], ACT.Exp, scale=-1.0).then_inc(S("D_ex"), 1)
            sc.activation(d_rows[:, 6, TP:T], d_rows[:, 6, TP:T], ACT.Exp).then_inc(S("D_ex"), 1)
            act.wait_ge(S("D_warg"), 3)
            sc.activation(d_wp, d_wp, ACT.Exp).then_inc(S("D_wexp"), 1)
            sc.activation(d_wm, d_wm, ACT.Exp).then_inc(S("D_wexp"), 1)
            sc.activation(d_dec, d_dec, ACT.Exp).then_inc(S("D_wexp"), 1)
            act.wait_ge(S("D_conv"), 2 * C4)
            sc.activation(d_c, d_c, ACT.Silu).then_inc(S("D_silu"), 1)
            act.wait_ge(S("D_o_in"), 16)
            sc.activation(d_o, d_o, ACT.Sigmoid).then_inc(S("D_osig"), 1)
            for h in range(4):
                full(act, "D_q", h)
                sc.activation(e_q, M[0][:, 0:T], ACT.Copy).then_inc(read("D_q", h), 1)
                full(act, "D_k", h)
                sc.activation(e_k, M[1][:, 0:T], ACT.Copy, scale=float(P) ** -0.5).then_inc(read("D_k", h), 1)
                full(act, "D_eb", h)
                sc.activation(e_em, M[1][:, 0:T], ACT.Copy).then_inc(read("D_eb", h), 1)
                act.wait_ge(S("D_E"), 2 * (h + 1))
                was_read(act, "D_Mb", h)
                sc.activation(e_E[:, 0:384], e_E[:, 0:384], ACT.Exp, scale=-1.0).then_inc(S("D_Eexp"), 1)
                sc.activation(e_E[0:64, 384:448], e_E[0:64, 384:448], ACT.Exp, scale=-1.0).then_inc(S("D_Eexp"), 1)
                full(act, "D_var", h)
                sc.activation(d_s, M[3][:, 0:T], ACT.Sqrt, scale=1.0 / P, bias=V("eps6")).then_inc(read("D_var", h), 1)
                act.wait_ge(S("D_y"), h + 1)
                sc.activation(y_hi[:, 12 + h, :], d_h, ACT.Copy).then_inc(S("D_yhi"), 1)
                was_read(act, "D_Cs", h, 0)
                was_read(act, "D_Cs", h, 1)
                act.dma_start(a["mCs"][:, h], d_C).then_inc(S("D_out"), 16)
                act.wait_ge(S("D_Cp"), h + 1)
                act.dma_start(a["mCp"][:, h], e_vtok[:, 0, :]).then_inc(S("D_out"), 16)
                act.wait_ge(S("D_out"), 32 * (h + 1))
                if h < 3:
                    act.dma_start(d_wq, a["ml_wq"][h + 1]).then_inc(S("D_wq_in"), 16)
                    act.dma_start(d_wk, a["ml_wk"][h + 1]).then_inc(S("D_wq_in"), 16)
                    act.dma_start(d_C, a["ml_C"][:, h + 1]).then_inc(S("D_C_in"), 16)
                nc.scalar.nop().then_inc(S("D_out_done"), 1)

            act.wait_ge(S("y_lo3"), C4)
            was_read(act, "D_Cp", 3)
            for g in range(2):
                for x, name in enumerate(("r", "k", "v")):
                    if 3 * g + x:
                        act.wait_ge(S("C_mixed"), 2 * (3 * g + x))
                        act.wait_ge(S("C_mixed_low"), 4 * g + 4 * (x > 0))
                    if g and not x:
                        act.wait_ge(S("C_ylo"), 4)
                    for h in range(4):
                        blk, part = ZB[name] + 2 * g + h // 2, 64 * (h % 2)
                        padded(act, c_zp[:, h, :], zD[blk][part:part + 64], 1, S("C_z_in"))
                    if not x:
                        padded(act, c_lowp, zD[ZB["low"]][0:64], 1, S("C_z_in"))
                        padded(act, c_gdp, zD[ZB["gd"]][0:96], 1, S("C_z_in"))
                        act.dma_start(c_lora, a["rw_lora"][:, 256 * g:256 * g + 256]).then_inc(S("C_lora_in"), 16)
                        act.dma_start(c_g2, a["rw_g2"][:, 256 * g:256 * g + 256]).then_inc(S("C_lora_in"), 16)
                        if g == 0:
                            act.dma_start(c_sh, a["rw_sh"]).then_inc(S("C_sh_in"), 16)
                            act.dma_start(c_shlow, a["rw_low"]).then_inc(S("C_sh_in"), 16)
                            act.dma_start(c_shgd, a["rw_gd"]).then_inc(S("C_sh_in"), 16)
                        act.dma_start(c_Ss, a["rw_S"][:, 4 * g:4 * g + 4]).then_inc(S("C_Ss_in"), 16)
                act.wait_ge(S("C_mixed_low"), 4 * (g + 1))
                act.wait_ge(S("C_lora_in"), 32 * (g + 1))
                sc.activation(c_low[0:32, :], c_low[0:32, :], ACT.Tanh).then_inc(S("C_low"), 1)
                sc.activation(c_gd, c_gd, ACT.Sigmoid).then_inc(S("C_low"), 1)
                for what, dst, bias in ((0, c_w, "w0"), (1, c_a, "a0")):
                    for h in range(4):
                        full(act, "C_lora", g, what, h)
                        sc.activation(dst[:, h, :], M[h][0:64, 0:T], ACT.Sigmoid,
                                      bias=V(bias, 4 * g + h, parts=64)).then_inc(read("C_lora", g, what, h), 1)
                for h in range(4):
                    was_read(act, "C_lora", g, 0, h)
                sc.activation(c_w, c_w, ACT.Exp, scale=-EXPM05).then_inc(S("C_decay"), 1)
                for h in range(4):
                    full(act, "C_kk_sum", g, h)
                    sc.activation(c_rk[:, h, :], M[h][0:64, 0:T], ACT.Sqrt).then_inc(read("C_kk_sum", g, h), 1)
                for h in range(4):
                    full(act, "C_var", g, h)
                    sc.activation(c_k[:, h, :], M[h][0:64, 0:T], ACT.Sqrt, scale=1.0 / HD,
                                  bias=V("eps64", parts=64)).then_inc(read("C_var", g, h), 1)
                for h in range(4):
                    was_read(act, "C_gate", g, h)
                for h in range(4):
                    o = 64 * (h % 2)
                    sc.activation(y_hi[o:o + 64, 8 + 2 * g + h // 2, :], c_t[:, h, :], ACT.Copy).then_inc(S("C_yhi"), 1)
                act.wait_ge(S("C_S_ready"), 5 * g + 5)
                act.dma_start(a["Sp"][:, 4 * g:4 * g + 4], c_S).then_inc(S("C_out"), 16)
                act.wait_ge(S("C_Ss_made"), 4 * g + 4)
                act.dma_start(a["Ss"][:, 4 * g:4 * g + 4], c_Ss).then_inc(S("C_out"), 16)
                act.wait_ge(S("C_out"), 32 * (g + 1))
                nc.scalar.nop().then_inc(S("C_out_done"), 1)

        def mixers_dve(dve, link, sync):
            v = nc.vector
            tt, ts, stt = v.tensor_tensor, v.tensor_scalar, v.scalar_tensor_tensor

            def put(ins, name, n):
                ins.then_inc(S(name), 1)
                dve.wait_ge(S(name), n)

            def softplus_of(x, y, s, s2, q, out, n_out):
                link(ts(s, y, 2.0, None, ALU.add)); sync()
                link(v.reciprocal(s, s)); sync()
                link(tt(s, s, y, ALU.mult)); sync()
                link(tt(s2, s, s, ALU.mult)); sync()
                link(ts(q, s2, 1.0 / 15, None, ALU.mult)); sync()
                for d in (13, 11, 9, 7, 5, 3):
                    link(stt(q, q, 1.0 / d, s2, ALU.add, ALU.mult)); sync()
                link(stt(q, q, 1.0, s, ALU.add, ALU.mult)); sync()
                link(ts(s, x, -1.0, 0.0, ALU.mult, ALU.max)); sync()
                link(stt(out, q, 2.0, s, ALU.mult, ALU.add)); sync()

            def conv(cin, acc, out, w, b, done):
                n = PAD3 - 3
                for c in range(C4):
                    link(ts(acc[:, c, 0:n], cin[:, c, 0:n], V(w, c), V(b, c), ALU.mult, ALU.add))
                for j in (1, 2):
                    sync()
                    for c in range(C4):
                        link(stt(acc[:, c, 0:n], cin[:, c, j:j + n], V(w, C4 * j + c), acc[:, c, 0:n], ALU.mult, ALU.add))
                sync()
                for c in range(C4):
                    stt(out[:, c, 0:TP], cin[:, c, 3:3 + TP], V(w, C4 * 3 + c), acc[:, c, 0:TP], ALU.mult,
                        ALU.add).then_inc(S(done), 1)
                    cs, as_ = [x[:, c, 3 + TP:].rearrange("p (b e) -> p b e", b=NS) for x in (cin, acc)]
                    stt(out[:, c, TP:T].rearrange("p (b e) -> p b e", b=NS), cs[:, :, 3:], V(w, C4 * 3 + c),
                        as_[:, :, 0:LS], ALU.mult, ALU.add).then_inc(S(done), 1)

            def conv_pads(cin, st, out):
                link(v.memset(cin[:, :, 0:3], 0.0))
                samples = cin[:, :, 3 + TP:].rearrange("p c (b e) -> p c b e", b=NS)
                link(v.tensor_copy(samples[:, :, :, 0:3], st))
                o = out.rearrange("p (c s e) -> p c s e", c=C4, e=3)
                sync()
                link(v.tensor_copy(o[:, :, 0, :], cin[:, :, TP:TP + 3]))
                link(v.tensor_copy(o[:, :, 1:, :], samples[:, :, :, LS:]))

            def halves(n0, src, hi_name, lo_name):
                for c in range(C4):
                    dve.wait_ge(S(hi_name), c + 1)
                    tt(y_lo[:, n0 + c, :], src[:, c, :], y_hi[:, n0 + c, :].bitcast(F32), ALU.subtract).then_inc(S(lo_name), 1)

            link(stt(a_t[:, 0, :], V("lam", 0, 4), -1.0, V("lam", 0, 4), ALU.mult, ALU.max)); sync()
            v.nop().then_inc(S("A_abs"), 1)
            dve.wait_ge(S("A_exp"), 1)
            softplus_of(V("lam", 0, 4), a_t[:, 1, :], a_t[:, 2, :], a_t[:, 3, :], a_t[:, 5, :], a_t[:, 4, :], 1)
            put(ts(a_t[:, 4, :], a_t[:, 4, :], 4.0, None, ALU.mult), "A_soft", 1)
            dve.wait_ge(S("A_in"), 16 * (2 * C4 + 2))
            conv_pads(a_cin, a_st, O("lconv"))
            conv(a_cin, a_acc, a_xc, "cw_l", "cb_l", "A_conv")
            dve.wait_ge(S("A_conv"), 2 * C4)
            dve.wait_ge(S("A_p"), C4)
            link(ts(a_a, a_r, 1.0, None, ALU.add)); sync()
            link(v.reciprocal(a_a, a_a)); sync()
            for c in range(C4):
                was_read(dve, "A_i", c)
            link(tt(a_i, a_i, a_xc, ALU.mult))
            dve.wait_ge(S("A_root"), 1)
            link(stt(a_r, a_acc[:, :, 0:T], 2.0, a_a, ALU.mult, ALU.mult)); sync()
            link(v.memset(a_r[:, :, 0:1], 1.0)); sync()
            link(tt(a_i, a_i, a_r, ALU.mult))
            link(ts(a_a, a_a, 2.0, -1.0, ALU.mult, ALU.add)); sync()
            a0, i0 = [x[:, :, TP:T].rearrange("p c (b e) -> p c b e", b=NS)[:, :, :, 0] for x in (a_a, a_i)]
            link(tt(a_sm, a0, a_h0, ALU.mult)); sync()
            link(tt(i0, i0, a_sm, ALU.add))
            link(v.memset(a0, 0.0)); sync()
            for c in range(C4):
                link(v.tensor_tensor_scan(a_r[:, c, :], a_a[:, c, :], a_i[:, c, :], 0.0, ALU.mult, ALU.add))
            sync()
            dve.wait_ge(S("A_gelu"), 1)
            o = O("lh").rearrange("p (c s) -> p c s", c=C4)
            link(v.tensor_copy(o[:, :, 0:1], a_r[:, :, TP - 1:TP]))
            link(v.tensor_copy(o[:, :, 1:], a_r[:, :, TP:T].rearrange("p c (b e) -> p c b e", b=NS)[:, :, :, LS - 1]))
            put(tt(a_i, a_r, a_gz, ALU.mult), "A_y", 1)
            halves(0, a_i, "y_hi0", "y_lo0")

            full(dve, "B_sum")
            put(stt(b_v, bc(M[0][:, 0:T], 1, C4), -1.0 / MIX, b_v, ALU.mult, ALU.add), *use("B_sum"))
            put(tt(b_q, b_v, b_v, ALU.mult), "B_sq", 1)
            dve.wait_ge(S("B_ws_in"), 32)
            tt(b_ws, b_ws, bc(K("maskD")[:, 0:P], 1, C4), ALU.mult).then_inc(S("B_masked"), 1)
            tt(b_wss, b_wss, bc(K("maskS", 64), 1, C4), ALU.mult).then_inc(S("B_masked"), 1)
            was_read(dve, "B_var")
            link(v.reciprocal(b_std, b_std)); sync()
            link(tt(b_v, b_v, bc(b_std, 1, C4), ALU.mult)); sync()
            for c in range(C4):
                ts(b_v[:, c, :], b_v[:, c, :], V("ln_g", c), V("ln_b", c), ALU.mult, ALU.add).then_inc(S("B_v"), 1)
            dve.wait_ge(S("B_gelu_u"), 1)
            for c in range(C4):
                full(dve, "B_s", c)
                tt(b_q[:, c, :], M[c][:, 0:T], b_u[:, c, :], ALU.mult).then_inc(read("B_s", c), 1)
            for c in range(C4):
                was_read(dve, "B_s", c)
            halves(4, b_q, "y_hi1", "y_lo1")

            dve.wait_ge(S("D_rows_in"), 80)
            ri, rf, r2, r3, r4, r5, r6 = [d_rows[:, i, :] for i in range(7)]
            keep = d_rc[:, ROWC["keep"][0]:ROWC["keep"][0] + T]
            drop = d_rc[:, ROWC["drop"][0]:ROWC["drop"][0] + T]

            def ends(row):
                return row[:, TP:T].rearrange("p (b e) -> p b e", b=NS)[:, :, LS - 1]

            def starts(row):
                return row[:, TP:T].rearrange("p (b e) -> p b e", b=NS)[:, :, 0]

            link(ts(ri, ri, V("bi", parts=4), None, ALU.add))
            link(ts(rf, rf, V("bf", parts=4), None, ALU.add)); sync()
            put(stt(r3, rf, -1.0, rf, ALU.mult, ALU.max), "D_abs", 1)
            dve.wait_ge(S("D_exp"), 1)
            softplus_of(rf, r4, r2, r3, r5, r6, 1)
            link(ts(r6, r6, -1.0, None, ALU.mult)); sync()
            link(v.tensor_tensor_scan(r2, keep, r6, 0.0, ALU.mult, ALU.add)); sync()
            link(tt(rf, ri, r2, ALU.subtract)); sync()
            link(v.tensor_copy(r3, rf)); sync()
            link(tt(r3[:, 0:1], rf[:, 0:1], d_m0[:, 0:1], ALU.max))
            link(tt(starts(r3), starts(rf), d_m0[:, 1:], ALU.max)); sync()
            link(v.tensor_tensor_scan(ri, drop, r3, 0.0, ALU.add, ALU.max)); sync()
            put(tt(r5, r2, ri, ALU.add), "D_bm", 1)
            link(v.tensor_copy(O("m", 4)[:, 0:1], r5[:, TP - 1:TP]))
            link(v.tensor_copy(O("m", 4)[:, 1:], ends(r5))); sync()
            put(tt(r6[:, TP:T].rearrange("p (b e) -> p b e", b=NS), bc(d_m0[:, 1:], 2, LS),
                   ri[:, TP:T].rearrange("p (b e) -> p b e", b=NS), ALU.subtract), "D_bm", 2)
            link(v.tensor_copy(d_mend[:, 0:1], ri[:, TP - 1:TP]))
            link(v.tensor_copy(d_mend[:, 1:], ends(ri))); sync()
            put(tt(d_md, bc(d_mend, 2, 4), bc(K("ident", 4)[:, 0:4], 1, NSEQ), ALU.mult), "D_rows", 1)
            full(dve, "D_turned")
            dve.wait_ge(S("D_ex"), 2)
            link(v.tensor_copy(d_g[:, 0:8], M[0][:, 0:8]))
            link(v.tensor_copy(d_g[0:64, 8:12], M[0][0:64, 8:12]))
            sync()
            put(v.tensor_copy(d_me.rearrange("p a b -> p (a b)"), M[0][:, 16:16 + 4 * NSEQ]), *use("D_turned"))
            g3 = d_g.rearrange("p (t h) -> p t h", t=3)
            tt(d_wp, g3[:, 0:2, :], bc(d_me[:, 0, :], 1, 2), ALU.subtract).then_inc(S("D_warg"), 1)
            link(tt(d_wm, bc(g3[0:64, 2, :], 1, NS), d_me[0:64, 1:, :], ALU.subtract)); sync()
            ts(d_wm, d_wm, 0.0, None, ALU.min).then_inc(S("D_warg"), 1)
            tt(d_dec, d_m0b, d_me[:, 1:, :], ALU.subtract).then_inc(S("D_warg"), 1)
            dve.wait_ge(S("D_in"), 16 * (2 * C4 + 1))
            conv_pads(d_cin, d_st, O("mconv"))
            conv(d_cin, d_acc, d_c, "cw_m", "cb_m", "D_conv")
            dve.wait_ge(S("D_conv"), 2 * C4)
            sync()
            dve.wait_ge(S("D_wexp"), 3)
            link(tt(d_wm, d_wm, bc(K("seq", 64), 2, 4), ALU.mult)); sync()
            dve.wait_ge(S("D_silu"), 1)
            dve.wait_ge(S("D_osig"), 1)
            dve.wait_ge(S("D_n_in"), 16)
            dve.wait_ge(S("D_v_in"), 16)
            for h in range(4):
                tok = lambda bank: M[bank][:, 0:TP].rearrange("p (t e) -> p t e", t=2)
                if h:
                    dve.wait_ge(S("D_out_done"), h)
                full(dve, "D_ktok", h)
                link(ts(e_ktok[:, 0:2, :], tok(2), float(P) ** -0.5, None, ALU.mult))
                ts(e_ktok[0:64, 2, :], M[2][0:64, TP:TP + P], float(P) ** -0.5, None, ALU.mult).then_inc(read("D_ktok", h), 1)
                full(dve, "D_vtok", h)
                link(v.tensor_copy(e_vtok[:, 0:2, :], tok(3)))
                v.tensor_copy(e_vtok[0:64, 2, :], M[3][0:64, TP:TP + P]).then_inc(read("D_vtok", h), 1)
                full(dve, "D_Mb", h)
                for lo, n, t0, t in ((0, P, 0, 0), (TP, P, P, 1)):
                    w = TP if t == 0 else P
                    ts(e_E[:, lo:lo + w], M[0][:, t0:TP], g3[:, t, h:h + 1], 0.0, ALU.subtract, ALU.max).then_inc(S("D_E"), 1)
                ts(e_E[0:64, 384:448], M[0][0:64, TP:T], g3[0:64, 2, h:h + 1], 0.0, ALU.subtract, ALU.max).then_inc(read("D_Mb", h), 1)
                full(dve, "D_sb", h)
                was_read(dve, "D_q", h)
                put(tt(d_qs, e_q[:, TP:T], M[2][:, 0:64], ALU.mult), *use("D_sb", h))
                qs3, qn3 = [x.rearrange("p (b e) -> p b e", b=NS) for x in (d_qs, d_qn)]
                tt(qn3, qs3, bc(d_n[:, h, :], 2, LS), ALU.mult).then_inc(S("D_qn"), 1)
                dve.wait_ge(S("D_Eexp"), 2 * h + 2)
                link(tt(e_E[:, 0:TP], e_E[:, 0:TP], K("maskD"), ALU.mult))
                link(tt(e_E[:, TP:TP + P], e_E[:, TP:TP + P], K("maskD")[:, 0:P], ALU.mult))
                link(tt(e_E[0:64, 384:448], e_E[0:64, 384:448], K("maskS", 64), ALU.mult)); sync()
                full(dve, "D_qk", h)
                link(tt(e_E[:, 0:384], e_E[:, 0:384], M[3][:, 0:384], ALU.mult))
                was_read(dve, "D_Mb", h)
                tt(e_E[0:64, 384:448], e_E[0:64, 384:448], M[3][0:64, 384:448], ALU.mult).then_inc(read("D_qk", h), 1)
                full(dve, "D_den", h)
                was_read(dve, "D_eb", h)
                link(stt(d_s, M[1][:, 0:T], -1.0, e_em, ALU.mult, ALU.max)); sync()
                put(tt(d_s, d_s, M[1][:, 0:T], ALU.max), *use("D_den", h))
                link(v.reciprocal(d_s, d_s)); sync()
                full(dve, "D_num", h)
                put(tt(d_h, M[0][:, 0:T], d_s, ALU.mult), *use("D_num", h))
                full(dve, "D_mean", h)
                put(stt(d_h, M[2][:, 0:T], -1.0 / P, d_h, ALU.mult, ALU.add), *use("D_mean", h))
                put(tt(d_s, d_h, d_h, ALU.mult), "D_sq", h + 1)
                for t in range(2):
                    ts(d_vm[:, NS + t, :], e_vtok[:, t, :], d_wp[:, t, h:h + 1], None, ALU.mult).then_inc(S("D_vm"), 1)
                tt(d_vm[0:64, 0:NS, :], bc(e_vtok[0:64, 2, :], 1, NS), bc(d_wm[:, :, h], 2, P), ALU.mult).then_inc(S("D_vm"), 1)
                was_read(dve, "D_var", h)
                link(v.reciprocal(d_s, d_s)); sync()
                link(stt(d_h, d_h, V("norm_g", h), d_s, ALU.mult, ALU.mult)); sync()
                link(stt(d_h, d_c[:, h, :], V("skip", h), d_h, ALU.mult, ALU.add)); sync()
                put(tt(d_h, d_h, d_o[:, h, :], ALU.mult), "D_y", h + 1)
                dve.wait_ge(S("D_yhi"), h + 1)
                tt(y_lo[:, 12 + h, :], d_h, y_hi[:, 12 + h, :].bitcast(F32), ALU.subtract).then_inc(S("y_lo3"), 1)
                link(tt(d_C, d_C, bc(d_dec[:, :, h], 2, P), ALU.mult)); sync()
                for i in range(2):
                    full(dve, "D_Cs", h, i)
                    c4 = d_C[:, 4 * i:4 * i + 4, :]
                    tt(c4, c4, M[i][:, :].rearrange("p (a b) -> p a b", a=4), ALU.add).then_inc(read("D_Cs", h, i), 1)
                full(dve, "D_Cp", h)
                v.tensor_copy(e_vtok[:, 0, :], M[2][:, 0:P]).then_inc(S("D_Cp"), 1)
                on = O("n").rearrange("p (h s) -> p h s", h=4)
                link(v.tensor_copy(on[:, h, 0:1], M[2][:, P + NS:P + NS + 1]))
                link(tt(d_n[:, h, :], d_n[:, h, :], d_dec[:, :, h], ALU.mult)); sync()
                tt(on[:, h, 1:], d_n[:, h, :], M[2][:, P:P + NS], ALU.add).then_inc(read("D_Cp", h), 1)

            def seq9(x):
                return x[:, :, 1 + TP:].rearrange("p c (b e) -> p c b e", b=NS)

            def mix_in(zp, d, out, mu, shift_out, parts, heads, name, n):
                so = shift_out
                link(v.tensor_copy(so[:, :, 0:1], zp[:, :, TP:TP + 1]))
                link(v.tensor_copy(so[:, :, 1:], seq9(zp)[:, :, :, LS]))
                dd = d[:, :, 0:PAD1 - 1]
                link(tt(dd, zp[:, :, 0:PAD1 - 1], zp[:, :, 1:PAD1], ALU.subtract)); sync()
                link(tt(dd, dd, bc(mu, 2, PAD1 - 1), ALU.mult)); sync()
                tt(out[:, :, 0:TP], d[:, :, 0:TP], zp[:, :, 1:1 + TP], ALU.add).then_inc(S(name), 1)
                dz = d[:, :, TP + 1:TP + 1 + 9 * NS].rearrange("p c (b e) -> p c b e", b=NS)[:, :, :, 0:LS]
                tt(out[:, :, TP:T].rearrange("p c (b e) -> p c b e", b=NS), dz, seq9(zp)[:, :, :, 1:],
                   ALU.add).then_inc(S(name), 1)
                dve.wait_ge(S(name), n)

            seq_starts = lambda x: x[:, :, TP:T].rearrange("p c (b e) -> p c b e", b=NS)[:, :, :, 0]
            chunk_starts = lambda x: x[:, :, 0:TP].rearrange("p c (b e) -> p c b e", b=4)[:, :, :, 0]
            for g in range(2):
                zin = 0
                base = 16 * (2 * 12 + 4) * g
                sh64 = O("shift64", 64).rearrange("p (c s) -> p c s", c=24)
                for x, (dst, mu) in enumerate(((c_r, "mu_r"), (c_k, "mu_k"), (c_v, "mu_v"))):
                    dve.wait_ge(S("C_z_in"), base + 16 * (8 * (x + 1) + 4))
                    if g == 0 and x == 0:
                        dve.wait_ge(S("D_out_done"), 4)
                    if g == 1 and x == 0:
                        dve.wait_ge(S("C_out_done"), 1)
                    link(v.memset(c_zp[:, :, 0:1], 0.0))
                    if g == 0 and x == 0:
                        dve.wait_ge(S("C_sh_in"), 48)
                    link(v.tensor_copy(seq9(c_zp)[:, :, :, 0], c_sh[:, 8 * x + 4 * g:8 * x + 4 * g + 4, :]))
                    sync()
                    mix_in(c_zp, c_d, dst, V(mu, 4 * g, 4, parts=64), sh64[:, 8 * x + 4 * g:8 * x + 4 * g + 4, :], 64, 4,
                           "C_mixed", 2 * (3 * g + x + 1))
                    if x == 0:
                        for zp, out, mu_, st, so, parts in (
                                (c_lowp, c_low, "mu_low", c_shlow, O("shift_low", 64), 64),
                                (c_gdp, c_gd, "mu_gd", c_shgd, O("shift_gd", 96), 96)):
                            z3, o3 = zp.unsqueeze(1), out.unsqueeze(1)
                            d3 = c_d96[0:parts, :].unsqueeze(1)
                            link(v.memset(z3[:, :, 0:1], 0.0))
                            link(v.tensor_copy(seq9(z3)[:, :, :, 0], st.unsqueeze(1))); sync()
                            mix_in(z3, d3, o3, V(mu_, parts=parts), so.unsqueeze(1), parts, 1, "C_mixed_low",
                                   2 * (2 * g + 1 + (parts == 96)))
                hg = slice(4 * g, 4 * g + 4)
                vb4 = lambda name: bc(V(name, 4 * g, 4, parts=64), 2, T)
                link(tt(c_kk, c_k, vb4("kk"), ALU.mult)); sync()
                put(tt(c_t, c_kk, c_kk, ALU.mult), "C_kk_sq", g + 1)
                for h in range(4):
                    was_read(dve, "C_lora", g, 1, h)
                    was_read(dve, "C_kk_sum", g, h)
                link(ts(c_rk, c_rk, 1e-12, None, ALU.max)); sync()
                link(v.reciprocal(c_rk, c_rk)); sync()
                link(tt(c_kk, c_kk, c_rk, ALU.mult)); sync()
                link(stt(c_t, c_a, -1.0, vb4("ka"), ALU.add, ALU.mult)); sync()
                link(stt(c_k, c_t, 1.0, c_k, ALU.add, ALU.mult)); sync()
                link(tt(c_rk, c_r, c_k, ALU.mult)); sync()
                put(tt(c_rk, c_rk, vb4("rk"), ALU.mult), "C_rk", g + 1)
                dve.wait_ge(S("C_decay"), g + 1)
                link(v.memset(c_t, 0.0)); sync()
                for sel in (seq_starts, chunk_starts):
                    link(v.tensor_copy(sel(c_t), sel(c_w)))
                sync()
                for sel in (seq_starts, chunk_starts):
                    link(v.memset(sel(c_w), 0.0))
                sync()
                for h in range(4):
                    link(v.tensor_tensor_scan(c_t[:, h, :], c_w[:, h, :], c_t[:, h, :], 0.0, ALU.mult, ALU.add))
                sync()
                link(stt(c_w[:, :, 1:T], c_kk[:, :, 1:T], -1.0, c_t[:, :, 0:T - 1], ALU.mult, ALU.mult)); sync()
                for sel in (seq_starts, chunk_starts):
                    link(ts(sel(c_w), sel(c_kk), -1.0, None, ALU.mult))
                sync()
                link(tt(c_kk, c_kk, c_a, ALU.mult)); sync()
                link(v.reciprocal(c_a, c_t)); sync()
                link(tt(c_kk, c_kk, c_a, ALU.mult))
                link(tt(c_k, c_k, c_a, ALU.mult))
                link(tt(c_r, c_r, c_t, ALU.mult))
                link(v.tensor_copy(c_wend[:, :, 0:4], c_t[:, :, 0:TP].rearrange("p c (b e) -> p c b e", b=4)[:, :, :, 63]))
                link(v.tensor_copy(c_wend[:, :, 4:], c_t[:, :, TP:T].rearrange("p c (b e) -> p c b e", b=NS)[:, :, :, LS - 1]))
                for h in range(4):
                    full(dve, "C_rk_sum", g, h)
                    tt(c_rk[:, h, :], M[h][0:64, 0:T], c_v[:, h, :], ALU.mult).then_inc(read("C_rk_sum", g, h), 1)
                for h in range(4):
                    was_read(dve, "C_rk_sum", g, h)
                sync()
                v.nop().then_inc(S("C_scaled"), 1)
                link(v.memset(c_S, 0.0)); sync()
                v.nop().then_inc(S("C_S_ready"), 1)
                for ch in range(5):
                    n = 5 * g + ch
                    m = 4 * g + ch
                    smp = ch == 4
                    bank = lambda i: M[i][0:64, 0:256].rearrange("p (h e) -> p h e", h=4)

                    def masked(dst, i, mask, name):
                        full(dve, name, n)
                        put(tt(dst, bank(i), bc(K(mask, 64), 1, 4), ALU.mult), *use(name, n))

                    def copied(dst, i, *key):
                        full(dve, *key)
                        put(v.tensor_copy(dst, bank(i)), *use(*key))

                    def added(dst, i, *key):
                        full(dve, *key)
                        put(tt(dst, dst, bank(i), ALU.add), *use(*key))

                    near = "n_seq" if smp else "n_near"
                    full(dve, "C_N", n)
                    if not smp:
                        link(tt(h_F, bank(0), bc(K("n_far", 64), 1, 4), ALU.mult)); sync()
                    masked(h_N, 0, near, "C_N")
                    masked(h_Q, 1, "nT_seq" if smp else "nT_near", "C_NT")
                    masked(h_ak, 2, "nT_seq" if smp else "sT", "C_ak")
                    masked(h_rb, 3, "maskS" if smp else "iT", "C_rb")
                    masked(h_rk, 0, "maskS" if smp else "iT", "C_rk")
                    copied(h_btok, 1, "C_btok", n)
                    copied(h_ktok, 2, "C_ktok", n)
                    copied(h_vtok, 3, "C_vtok", n)
                    put(tt(h_T, h_Q, bc(K("ident", 64)[:, 0:64], 1, 4), ALU.add), "C_QI", n + 1)
                    copied(h_P2, 0, "C_p2", n)
                    copied(h_Q2, 1, "C_q2", n)
                    added(h_T, 2, "C_t2", n)
                    full(dve, "C_q4", n)
                    copied(h_P2, 0, "C_p4", n)
                    copied(h_Q2, 1, "C_q4", n)
                    added(h_T, 2, "C_t4", n)
                    if not smp:
                        copied(h_P2, 0, "C_p8", n)
                        added(h_T, 2, "C_t8", n)
                        copied(h_P2, 0, "C_zT", n)
                        copied(h_Q2, 1, "C_z", n)
                        put(tt(h_E, h_P2, bc(K("ident", 64)[:, 0:64], 1, 4), ALU.add), "C_E", m + 1)
                        copied(h_N, 2, "C_z2", n)
                        added(h_E, 0, "C_e", n)
                        copied(h_P2, 3, "C_rhs", n)
                        copied(h_Q2, 1, "C_y", n)
                        copied(h_F, 2, "C_u", n)
                    else:
                        copied(h_N, 0, "C_u0", n)
                        copied(h_P2, 3, "C_rhs", n)
                        copied(h_F, 1, "C_y", n)
                    copied(c_t[:, :, 64 * ch:64 * ch + 64], 3, "C_o", n)
                    if not smp:
                        added(c_S, 0, "C_S", n)
                        put(tt(c_S, c_S, bc(c_wend[:, :, ch], 2, 64), ALU.mult), "C_S_ready", 5 * g + ch + 2)
                    else:
                        for h in range(4):
                            if h:
                                full(dve, "C_Ss", g, h - 1)
                            for x, src in ((0, h_F), (1, h_vtok)):
                                um = c_um[:, x, :].rearrange("p (b e) -> p b e", b=NS)
                                tt(um, bc(src[:, h, :], 1, NS), bc(K("seq", 64), 2, HD), ALU.mult).then_inc(S("C_um"), 1)
                            full(dve, "C_Ss", g, h)
                            put(tt(c_Ss[:, h, :, :], c_Ss[:, h, :, :], M[h % 2][0:64, :].rearrange("p (b e) -> p b e", b=NS),
                                   ALU.add), *use("C_Ss", g, h))
                            tt(c_Ss[:, h, :, :], c_Ss[:, h, :, :], bc(c_wend[:, h, 4:], 2, HD), ALU.mult).then_inc(S("C_Ss_made"), 1)
                        dve.wait_ge(S("C_Ss_made"), 4 * g + 4)
                for h in range(4):
                    full(dve, "C_mean", g, h)
                    stt(c_t[:, h, :], M[h][0:64, 0:T], -1.0 / HD, c_t[:, h, :], ALU.mult, ALU.add).then_inc(read("C_mean", g, h), 1)
                for h in range(4):
                    was_read(dve, "C_mean", g, h)
                put(tt(c_k, c_t, c_t, ALU.mult), "C_osq", g + 1)
                for h in range(4):
                    was_read(dve, "C_var", g, h)
                link(v.reciprocal(c_k, c_k)); sync()
                link(tt(c_t, c_t, c_k, ALU.mult)); sync()
                link(tt(c_t, c_t, vb4("rln_g"), ALU.mult)); sync()
                link(tt(c_t, c_t, vb4("rln_b"), ALU.add)); sync()
                link(tt(c_t, c_t, c_rk, ALU.add)); sync()
                for h in range(4):
                    full(dve, "C_gate", g, h)
                    tt(c_t[:, h, :], M[h][0:64, 0:T], c_t[:, h, :], ALU.mult).then_inc(read("C_gate", g, h), 1)
                for h in range(4):
                    was_read(dve, "C_gate", g, h)
                dve.wait_ge(S("C_yhi"), 4 * g + 4)
                for h in range(4):
                    o = 64 * (h % 2)
                    tt(y_lo[o:o + 64, 8 + 2 * g + h // 2, :], c_t[:, h, :],
                       y_hi[o:o + 64, 8 + 2 * g + h // 2, :].bitcast(F32), ALU.subtract).then_inc(S("C_ylo"), 1)
                dve.wait_ge(S("C_ylo"), 4 * g + 4)
            v.nop().then_inc(S("y_lo2"), 4)
            sync()
            v.nop().then_inc(S("small_done"), 1)

        block = ctx.enter_context(nc.Block())

        use_pass = [NZ // 2, NZ // 2, 0, 0]
        use_out = [u + v for u, v in zip(use_pass, [32, 32, 32, 32])]
        use_ff = [[use_out[0] + 8 + 15 * h, use_out[1] + 8 + 15 * h, use_out[2] + 15 * h, use_out[3] + 15 * h]
                  for h in range(2)]
        use_ffo = [[u + 11 for u in use_ff[h]] for h in range(2)]

        def phases():
            yield "z", Z0, NZ // 2, [8, 8, 8, 8]
            for n in range(4):
                yield f"pass{n}", PASS0 + 48 * n, 4, [8, 8, 4] * 4
            yield "out", OUT0, KD // 2, [8, 8, 8, 8]
            for h in range(2):
                yield f"in{h}", FF0 + h * (FFIN + FFOUT), HALF // 2, [8] * 8
                yield f"ff{h}", FF0 + h * (FFIN + FFOUT) + FFIN, 4, OUT_TILES * 4

        tiles_of = {}
        for _, base, turns, pat in phases():
            for q in range(turns * len(pat)):
                tiles_of[base + q] = pat[q % len(pat)]
        assert len(tiles_of) == NPIECES

        @block.sync
        def _(sp):
            def load(p, q, src):
                sp.wait_ge(S("w_lo_made"), p + 1)
                sp.dma_start(w_raw[:, q % RING, 0:src.shape[1]], src).then_inc(S(f"w_raw_in{q % RING}"), 16)

            def one(ap):
                return ap.rearrange("a p n -> (a p) n")

            sp.dma_start(vec[:, :], a["vec"]).then_inc(S("vec_in"), 16)
            for h in range(2):
                sp.dma_start(xin[:, 8 * h:8 * h + 8, :], a["x"][:, 8 * h:8 * h + 8, :]).then_inc(S(f"x_in{h}"), 16)
            with sp.Fori(0, NZ // 2) as i:
                for q in range(4):
                    load(i * 4 + q, q, one(a["w_z"][bass.ds(i * 2 + q // 2, 1), :, (q % 2) * 1024:(q % 2) * 1024 + 1024]))
            for n, br in enumerate((0, 1, 3, 2)):
                with sp.Fori(0, 4) as i:
                    for j in range(4):
                        row = bass.ds(i * 4 + (br * KD + j), 1)
                        p = i * 12 + (PASS0 + 48 * n + 3 * j)
                        load(p, 3 * j, one(a["w_gate"][row, :, 0:1024]))
                        load(p + 1, 3 * j + 1, one(a["w_gate"][row, :, 1024:2048]))
                        load(p + 2, 3 * j + 2, one(a["w_br"][row, :, :]))
            with sp.Fori(0, KD // 2) as i:
                for q in range(4):
                    load(i * 4 + (OUT0 + q), q, one(a["w_o"][bass.ds(i * 2 + q // 2, 1), :, (q % 2) * 1024:(q % 2) * 1024 + 1024]))
            for h in range(2):
                with sp.Fori(0, HALF // 2) as i:
                    for q in range(8):
                        load(i * 8 + (FF0 + h * (FFIN + FFOUT) + q), q,
                             one(a["w_fi"][bass.ds(i * 4 + (h * HALF * 2 + q // 2), 1), :, (q % 2) * 1024:(q % 2) * 1024 + 1024]))
                with sp.Fori(0, 4) as i:
                    for q in range(12):
                        c0 = sum(OUT_TILES[:q % 3]) * P
                        load(i * 12 + (FF0 + h * (FFIN + FFOUT) + FFIN + q), q,
                             one(a["w_fo"][bass.ds(i * 4 + (h * KD + q // 3), 1), :, c0:c0 + OUT_TILES[q % 3] * P]))

        @block.gpsimd
        def _(pool):
            nc.gpsimd.nop().then_inc(S("w_lo_made"), RING)
            for name, base, turns, pat in phases():
                with pool.Fori(0, turns) as i:
                    for q, tiles in enumerate(pat):
                        n = tiles * P
                        pool.wait_ge(S("w_hi_made"), i * len(pat) + (base + q + 1))
                        nc.gpsimd.tensor_tensor(w_lo[:, q % RING, 0:n], w_raw[:, q % RING, 0:n],
                                                w_hi[:, q % RING, 0:n].bitcast(F32), ALU.subtract).then_inc(S("w_lo_made"), 1)

        @block.tensor
        def _(pe):
            nc.tensor.nop().then_inc(S("w_used"), RING)
            for b in range(4):
                nc.tensor.nop().then_inc(S(f"evac{b}"), 1)

            def products(p, q, b, tiles, hi, lo, k0, first, last):
                pe.wait_ge(S("w_lo_made"), p + (RING + 1))
                for k in range(tiles):
                    wh = w_hi[:, q % RING, k * P:(k + 1) * P]
                    wl = w_lo[:, q % RING, k * P:(k + 1) * P]
                    out = G[b][:, 0:T]
                    pe.matmul(out, wh, hi[:, k0 + k, :], start=first and k == 0, stop=False)
                    pe.matmul(out, wh, lo[:, k0 + k, :], start=False, stop=False)
                    mm = pe.matmul(out, wl, hi[:, k0 + k, :], start=False, stop=last and k == tiles - 1)
                mm.then_inc(S("w_used"), 1)

            def block_of(use, b, parts):
                pe.wait_ge(S(f"evac{b}"), use + 1)
                for n, (p, q, tiles, hi, lo, k0) in enumerate(parts):
                    products(p, q, b, tiles, hi, lo, k0, n == 0, n == len(parts) - 1)

            def sum_squares(ready):
                pe.wait_ge(S(ready), 1)
                pe.matmul(M[0][:, 0:T], K("ones"), ssum if ready == "x_ss" else ssum2[:, :], start=True,
                          stop=True).then_inc(S(ready + "_all"), 1)

            pe.wait_ge(S("con_in"), 16)
            sum_squares("x_ss")
            pe.wait_ge(S("x_lo_made"), KD)
            with pe.Fori(0, NZ // 2) as i:
                for j in range(2):
                    p = i * 4 + 2 * j
                    block_of(i, j, [(p, 2 * j, 8, x_hi, x_lo, 0), (p + 1, 2 * j + 1, 8, x_hi, x_lo, 8)])
            mixers_pe(pe)
            for n, br in enumerate((0, 1, 3, 2)):
                pe.wait_ge(S(f"y_lo{br}"), 4)
                with pe.Fori(0, 4) as i:
                    for j in range(4):
                        p = i * 12 + (PASS0 + 48 * n + 3 * j)
                        g, b = j % 2, 2 + j % 2
                        block_of(i * 2 + (use_pass[g] + 8 * n + j // 2), g,
                                 [(p, 3 * j, 8, x_hi, x_lo, 0), (p + 1, 3 * j + 1, 8, x_hi, x_lo, 8)])
                        block_of(i * 2 + (use_pass[b] + 8 * n + j // 2), b,
                                 [(p + 2, 3 * j + 2, 4, y_hi, y_lo, 4 * br)])
            pe.wait_ge(S("m_lo_made"), 4)
            with pe.Fori(0, KD // 2) as i:
                for j in range(2):
                    p = i * 4 + (OUT0 + 2 * j)
                    block_of(i + use_out[j], j, [(p, 2 * j, 8, x_hi, x_lo, 0), (p + 1, 2 * j + 1, 8, x_hi, x_lo, 8)])
            sum_squares("mix_ss")
            sum_squares("x2_ss")
            pe.wait_ge(S("x2_lo_made"), KD)
            for h in range(2):
                base = FF0 + h * (FFIN + FFOUT)
                with pe.Fori(0, HALF // 2) as i:
                    for b in range(4):
                        p = i * 8 + (base + 2 * b)
                        block_of(i + use_ff[h][b], b, [(p, 2 * b, 8, x_hi, x_lo, 0), (p + 1, 2 * b + 1, 8, x_hi, x_lo, 8)])
                pe.wait_ge(S("a_lo_made"), HALF * (h + 1))
                base += FFIN
                with pe.Fori(0, 4) as i:
                    for b in range(4):
                        p = i * 12 + (base + 3 * b)
                        block_of(i + use_ffo[h][b], b, [(p + t, 3 * b + t, OUT_TILES[t], a_hi, a_lo, 8 * t) for t in range(3)])
            sum_squares("ff_ss")

        @block.scalar
        def _(act):
            def run(base, turns, pat, tasks):
                n = len(pat)

                def turn(i, last):
                    for q in range(n):
                        ahead = q + AHEAD
                        if last:
                            p = base + (turns - 1) * n + ahead
                            if p < NPIECES:
                                split_at(p, ahead, tiles_of[p], None, None)
                        else:
                            split_at(base + ahead, ahead, pat[ahead % n], i, n)
                        if q in tasks:
                            tasks[q](i)

                def split_at(p0, q, tiles, i, n):
                    slot = q % RING
                    raw = 16 * (p0 // RING + 1)
                    act.wait_ge(S(f"w_raw_in{slot}"), raw if i is None else i * (16 * n // RING) + raw)
                    act.wait_ge(S("w_used"), p0 + 1 if i is None else i * n + (p0 + 1))
                    nc.scalar.activation(w_hi[:, slot, 0:tiles * P], w_raw[:, slot, 0:tiles * P],
                                         ACT.Copy).then_inc(S("w_hi_made"), 1)

                with act.Fori(0, turns - 1) as i:
                    turn(i, False)
                turn(turns - 1, True)

            def root(src, dst, name, wait):
                act.wait_ge(S(wait), 1)
                nc.scalar.activation(dst, src, ACT.Sqrt, scale=1.0 / D, bias=V("eps6")).then_inc(S(name), 1)

            act.dma_start(con[:, :], a["con"]).then_inc(S("con_in"), 16)
            act.wait_ge(S("vec_in"), 16)
            for k in range(KD):
                act.wait_ge(S(f"x_in{k // 8}"), 16)
                nc.scalar.activation(x_hi[:, k, :], xin[:, k, :], ACT.Copy, scale=V("g_pre", k)).then_inc(S("x_hi_made"), 1)
            for p in range(AHEAD):
                act.wait_ge(S(f"w_raw_in{p}"), 16)
                act.wait_ge(S("w_used"), p + 1)
                nc.scalar.activation(w_hi[:, p, :], w_raw[:, p, :], ACT.Copy).then_inc(S("w_hi_made"), 1)
            nc.scalar.activation(xsq[:, :, :], xin[:, :, :], ACT.Square).then_inc(S("x_sq"), 1)
            root(M[0][:, 0:T], rstd[:, :], "x_std", "x_ss_all")

            def z_store(j):
                def task(i):
                    act.wait_ge(S(f"evac{j}"), i + 2)
                    act.dma_start(zD[bass.ds(i * 2 + j, 1), :, :].rearrange("a p n -> (a p) n"),
                                  zev[:, j, :]).then_inc(S(f"z_out{j}"), 16)
                return task

            nc.scalar.nop().then_inc(S("z_out0"), 16)
            nc.scalar.nop().then_inc(S("z_out1"), 16)
            run(Z0, NZ // 2, [8] * 4, {1: z_store(0), 3: z_store(1)})
            for j in range(2):
                act.wait_ge(S(f"z_out{j}"), 16 * (NZ // 2 + 1))
            mixers_act(act)

            for n in range(4):
                def sig(j):
                    def task(i):
                        act.wait_ge(S(f"evac{j % 2}"), i * 2 + (use_pass[j % 2] + 8 * n + j // 2 + 2))
                        nc.scalar.activation(gate[:, j % 2, :], gate[:, j % 2, :], ACT.Sigmoid).then_inc(S("gate_made"), 1)
                    return task
                run(PASS0 + 48 * n, 4, [8, 8, 4] * 4, {3 * j + 1: sig(j) for j in range(4)})
            act.wait_ge(S("merged"), 4 * KD + 1)
            for k in range(4):
                nc.scalar.activation(x_hi[:, 4 * k:4 * k + 4, :], merged[:, 4 * k:4 * k + 4, :], ACT.Copy).then_inc(S("m_hi_made"), 1)
            act.wait_ge(S("m_lo_made"), 4)
            act.dma_start(xres[:, :, :], a["x"]).then_inc(S("x_again"), 16)
            run(OUT0, KD // 2, [8] * 4, {})
            root(M[0][:, 0:T], rstd[:, :], "mix_std", "mix_ss_all")
            for k in range(KD):
                act.wait_ge(S("x2_made"), k + 1)
                nc.scalar.activation(x_hi[:, k, :], xres[:, k, :], ACT.Copy, scale=V("g_pre2", k)).then_inc(S("x2_hi_made"), 1)
            nc.scalar.activation(mix[:, :, :], xres[:, :, :], ACT.Square).then_inc(S("x2_sq"), 1)
            root(M[0][:, 0:T], rstd[:, :], "x2_std", "x2_ss_all")
            for h in range(2):
                def silu(j):
                    def task(i):
                        act.wait_ge(S(f"evac{2 * j}"), i + (use_ff[h][2 * j] + 2))
                        nc.scalar.activation(gate[:, j, :], gate[:, j, :], ACT.Silu).then_inc(S("silu_made"), 1)
                    return task

                def high(j):
                    def task(i):
                        act.wait_ge(S("a_made"), i * 2 + (h * HALF + j + 1))
                        row = bass.ds(i * 2 + j, 1) if not isinstance(i, int) else slice(i * 2 + j, i * 2 + j + 1)
                        nc.scalar.activation(a_hi[:, row, :], term[:, j:j + 1, :], ACT.Copy).then_inc(S("a_hi_made"), 1)
                    return task
                base = FF0 + h * (FFIN + FFOUT)
                run(base, HALF // 2, [8] * 8, {1: silu(0), 3: high(0), 5: silu(1), 7: high(1)})
                run(base + FFIN, 4, OUT_TILES * 4, {})
            root(M[0][:, 0:T], rstd[:, :], "ff_std", "ff_ss_all")
            for k in range(4):
                act.wait_ge(S("y_made"), 4 * k + 4)
                act.dma_start(a["y"][:, 4 * k:4 * k + 4, :], xres[:, 4 * k:4 * k + 4, :]).then_inc(S("y_out"), 16)
            act.wait_ge(S("small_done"), 1)
            act.dma_start(a["small"], small[:, :]).then_inc(S("small_out"), 16)
            act.wait_ge(S("small_out"), 16)
            act.wait_ge(S("y_out"), 64)

        @block.vector
        def _(dve):
            count = [0]

            def link(ins):
                count[0] += 1
                ins.then_inc(S("dve_order"), 1)

            def sync():
                dve.wait_ge(S("dve_order"), count[0])

            v = nc.vector

            def multiplied(p):
                dve.wait_ge(S("w_used"), p + (RING + 1))

            def flip(std, made):
                dve.wait_ge(S(std), 1)
                v.reciprocal(rstd[:, :], rstd[:, :]).then_inc(S(made), 1)
                dve.wait_ge(S(made), 1)

            link(v.memset(small[:, :], 0.0))
            for k in range(KD):
                dve.wait_ge(S("x_hi_made"), k + 1)
                v.scalar_tensor_tensor(x_lo[:, k, :], xin[:, k, :], V("g_pre", k), x_hi[:, k, :].bitcast(F32),
                                       ALU.mult, ALU.subtract).then_inc(S("x_lo_made"), 1)
            dve.wait_ge(S("x_sq"), 1)
            v.tensor_reduce(ssum, xsq.rearrange("p k t -> p t k"), AX.X, ALU.add).then_inc(S("x_ss"), 1)
            flip("x_std", "x_rstd")

            with dve.Fori(0, NZ // 2) as i:
                for j in range(2):
                    multiplied(i * 4 + (2 * j + 1))
                    dve.wait_ge(S(f"z_out{j}"), i * 16 + 16)
                    v.tensor_tensor(zev[:, j, :], G[j][:, 0:T], rstd[:, :], ALU.mult).then_inc(S(f"evac{j}"), 1)
            mixers_dve(dve, link, sync)

            dve.wait_ge(S("C_out_done"), 2)
            v.memset(merged[:, :, :], 0.0).then_inc(S("merged"), 1)
            for n in range(4):
                with dve.Fori(0, 4) as i:
                    for j in range(4):
                        g, b = j % 2, 2 + j % 2
                        ub = i * 2 + (use_pass[b] + 8 * n + j // 2)
                        block_no = i * 4 + (KD * n + j)
                        row = bass.ds(i * 4 + j, 1)
                        multiplied(i * 12 + (PASS0 + 48 * n + 3 * j + 1))
                        v.tensor_tensor(gate[:, g, :], G[g][:, 0:T], rstd[:, :], ALU.mult).then_inc(S(f"evac{g}"), 1)
                        multiplied(i * 12 + (PASS0 + 48 * n + 3 * j + 2))
                        dve.wait_ge(S("gate_made"), block_no + 1)
                        v.tensor_tensor(term[:, g, :], G[b][:, 0:T], gate[:, g, :], ALU.mult).then_inc(S(f"evac{b}"), 1)
                        dve.wait_ge(S(f"evac{b}"), ub + 2)
                        dve.wait_ge(S("merged"), block_no + 1)
                        v.tensor_tensor(merged[:, row, :], merged[:, row, :], term[:, g:g + 1, :],
                                        ALU.add).then_inc(S("merged"), 1)
            for k in range(4):
                dve.wait_ge(S("m_hi_made"), k + 1)
                v.tensor_tensor(x_lo[:, 4 * k:4 * k + 4, :], merged[:, 4 * k:4 * k + 4, :],
                                x_hi[:, 4 * k:4 * k + 4, :].bitcast(F32), ALU.subtract).then_inc(S("m_lo_made"), 1)

            def square(n, src, made, added):
                v.tensor_tensor(term[:, 0:1, :], src, src, ALU.mult).then_inc(S(made), 1)
                dve.wait_ge(S(made), n + 1)
                dve.wait_ge(S(added), n + 1)
                v.tensor_tensor(ssum2[:, :], ssum2[:, :], term[:, 0, :], ALU.add).then_inc(S(added), 1)

            v.memset(ssum2[:, :], 0.0).then_inc(S("mix_added"), 1)
            with dve.Fori(0, KD // 2) as i:
                for j in range(2):
                    row = mix[:, bass.ds(i * 2 + j, 1), :]
                    multiplied(i * 4 + (OUT0 + 2 * j + 1))
                    v.tensor_copy(row, G[j][:, 0:T].unsqueeze(1)).then_inc(S(f"evac{j}"), 1)
                    dve.wait_ge(S(f"evac{j}"), i + (use_out[j] + 2))
                    square(i * 2 + j, row, "mix_sq", "mix_added")
            dve.wait_ge(S("mix_added"), KD + 1)
            v.nop().then_inc(S("mix_ss"), 1)
            flip("mix_std", "mix_rstd")
            dve.wait_ge(S("x_again"), 16)
            for k in range(KD):
                link(v.scalar_tensor_tensor(mix[:, k, :], mix[:, k, :], V("g_post", k), rstd[:, :], ALU.mult, ALU.mult))
            sync()
            for k in range(KD):
                v.tensor_tensor(xres[:, k, :], xres[:, k, :], mix[:, k, :], ALU.add).then_inc(S("x2_made"), 1)
            for k in range(KD):
                dve.wait_ge(S("x2_hi_made"), k + 1)
                v.scalar_tensor_tensor(x_lo[:, k, :], xres[:, k, :], V("g_pre2", k), x_hi[:, k, :].bitcast(F32),
                                       ALU.mult, ALU.subtract).then_inc(S("x2_lo_made"), 1)
            dve.wait_ge(S("x2_sq"), 1)
            v.tensor_reduce(ssum2[:, :], mix[:, :, :].rearrange("p k t -> p t k"), AX.X, ALU.add).then_inc(S("x2_ss"), 1)
            flip("x2_std", "x2_rstd")
            v.memset(mix[:, :, :], 0.0).then_inc(S("ff_sum"), 1)
            v.memset(ssum2[:, :], 0.0).then_inc(S("ff_added"), 1)
            for h in range(2):
                base = FF0 + h * (FFIN + FFOUT)
                with dve.Fori(0, HALF // 2) as i:
                    for j in range(2):
                        uu = i + use_ff[h][2 * j + 1]
                        pair = i * 2 + (h * HALF + j)
                        multiplied(i * 8 + (base + 4 * j + 1))
                        v.tensor_tensor(gate[:, j, :], G[2 * j][:, 0:T], rstd[:, :], ALU.mult).then_inc(S(f"evac{2 * j}"), 1)
                        multiplied(i * 8 + (base + 4 * j + 3))
                        v.tensor_tensor(term[:, j, :], G[2 * j + 1][:, 0:T], rstd[:, :], ALU.mult).then_inc(S(f"evac{2 * j + 1}"), 1)
                        dve.wait_ge(S(f"evac{2 * j + 1}"), uu + 2)
                        dve.wait_ge(S("silu_made"), pair + 1)
                        v.tensor_tensor(term[:, j, :], term[:, j, :], gate[:, j, :], ALU.mult).then_inc(S("a_made"), 1)
                        dve.wait_ge(S("a_hi_made"), pair + 1)
                        row = bass.ds(i * 2 + j, 1)
                        v.tensor_tensor(a_lo[:, row, :], term[:, j:j + 1, :], a_hi[:, row, :].bitcast(F32),
                                        ALU.subtract).then_inc(S("a_lo_made"), 1)
                with dve.Fori(0, 4) as i:
                    for b in range(4):
                        row = mix[:, bass.ds(i * 4 + b, 1), :]
                        multiplied(i * 12 + (base + FFIN + 3 * b + 2))
                        dve.wait_ge(S("ff_sum"), 1)
                        v.tensor_tensor(row, row, G[b][:, 0:T].unsqueeze(1), ALU.add).then_inc(S(f"evac{b}"), 1)
                        if h == 1:
                            dve.wait_ge(S(f"evac{b}"), i + (use_ffo[h][b] + 2))
                            square(i * 4 + b, row, "ff_sq", "ff_added")
                if h == 0:
                    for b in range(4):
                        dve.wait_ge(S(f"evac{b}"), use_ffo[h][b] + 5)
            dve.wait_ge(S("ff_added"), KD + 1)
            v.nop().then_inc(S("ff_ss"), 1)
            flip("ff_std", "ff_rstd")
            for k in range(KD):
                link(v.scalar_tensor_tensor(mix[:, k, :], mix[:, k, :], V("g_post2", k), rstd[:, :], ALU.mult, ALU.mult))
            sync()
            for k in range(KD):
                v.tensor_tensor(xres[:, k, :], xres[:, k, :], mix[:, k, :], ALU.add).then_inc(S("y_made"), 1)


def kernel(**inp):
    import concourse.bacc as bacc
    from concourse.bass_utils import run_bass_kernel_spmd as run

    f = {k: np.asarray(v) for k, v in inp.items()}
    dt = f["w_in"].dtype
    g = {k: (v[0] if k not in ("x_prompt", "x_sample") else v) for k, v in f.items()}

    def feat(x):
        return x.reshape(-1, P).T

    def head(x):
        return np.concatenate([x.reshape(-1, 64).T, np.zeros((64, x.size // 64), dt)])

    def rows(x, at=0):
        out = np.zeros((P, 1), dt)
        out[at:at + x.size, 0] = x
        return out

    def conv_w(w):
        return w.reshape(CW, C4, P).transpose(2, 0, 1).reshape(P, CW * C4)

    mu = g["rwkv_mu"]
    full = np.ones((P, 1), dt)
    parts = {
        "g_pre": feat(g["norm_pre_mix"]), "g_post": feat(g["norm_post_mix"]),
        "g_pre2": feat(g["norm_pre_ffn"]), "g_post2": feat(g["norm_post_ffn"]),
        "cw_l": conv_w(g["lru_conv_w"]), "cb_l": feat(g["lru_conv_b"]), "ba": feat(g["lru_ba"]),
        "bx": feat(g["lru_bx"]), "lam": feat(g["lru_lambda"]), "ln_g": feat(g["gmlp_ln_g"]),
        "ln_b": feat(g["gmlp_ln_b"]), "cw_m": conv_w(g["mlstm_conv_w"]), "cb_m": feat(g["mlstm_conv_b"]),
        "norm_g": feat(g["mlstm_norm_g"]), "skip": feat(g["mlstm_skip"]),
        "mu_gd": rows(mu[3 * MIX + 64:]), "mu_low": rows(mu[3 * MIX:3 * MIX + 64]),
        "bi": rows(g["mlstm_bi"]), "bf": rows(g["mlstm_bf"]),
        "mu_r": head(mu[0:MIX]), "mu_k": head(mu[MIX:2 * MIX]), "mu_v": head(mu[2 * MIX:3 * MIX]),
        "w0": head(g["rwkv_w0"]), "a0": head(g["rwkv_a0"]), "kk": head(g["rwkv_kk"]), "ka": head(g["rwkv_ka"]),
        "rk": head(g["rwkv_rk"].reshape(-1)), "rln_g": head(g["rwkv_ln_g"]), "rln_b": head(g["rwkv_ln_b"]),
        "eps6": full * dt.type(1e-6), "eps5": full * dt.type(1e-5), "eps64": full * dt.type(64e-5),
    }
    vec = np.concatenate([parts[n] for n in VEC], 1)
    assert vec.shape == (P, NVEC)

    r, c = np.arange(P)[:, None], np.arange(P)[None, :]
    r6, c6 = r[:64], c[:, :64]
    near, oneseq = r6 // 16 == c6 // 16, r6 // LS == c6 // LS
    con_parts = {
        "ident": r == c, "ones": np.ones((P, P)),
        "maskD": np.arange(P)[:, None] <= np.arange(TP)[None, :], "maskS": (r6 <= c6) & oneseq,
        "n_near": (r6 > c6) & near, "n_far": (r6 > c6) & ~near, "nT_near": (r6 < c6) & near,
        "sT": r6 < c6, "iT": r6 <= c6, "n_seq": (r6 > c6) & oneseq, "nT_seq": (r6 < c6) & oneseq,
        "seq": r6 // LS == np.arange(NS)[None, :],
    }
    con = np.zeros((P, NCON), dt)
    for n, (at, w) in CON.items():
        con[:con_parts[n].shape[0], at:at + w] = con_parts[n]
    first = np.zeros(T, bool)
    first[[0] + [TP + LS * b for b in range(NS)]] = True
    rowc = np.zeros((4, NROWC), dt)
    for h in range(4):
        rowc[h, h * P:(h + 1) * P] = 1
    rowc[:, ROWC["keep"][0]:ROWC["keep"][0] + T] = ~first
    rowc[:, ROWC["drop"][0]:ROWC["drop"][0] + T] = np.where(first, -1e30, 0)

    def tiled(w, n_out):
        k = w.shape[0] // P
        return np.ascontiguousarray(w.reshape(k, P, n_out, P).transpose(2, 1, 0, 3)).reshape(n_out, P, k * P)

    w_in = g["w_in"]
    sizes = [("lx", MIX), ("lg", MIX), ("gu", MIX), ("gv", MIX), ("r", MIX), ("k", MIX), ("v", MIX), ("wd", 32),
             ("ad", 32), ("gd", 96), ("mx", MIX), ("mv", MIX), ("mo", MIX), ("mi", 4), ("mf", 4), ("gate", 4 * D)]
    col, at = {}, 0
    for n, w in sizes:
        col[n] = w_in[:, at:at + w]
        at += w
    wz = np.zeros((D, NZ * P), dt)
    for n, b in ZB.items():
        if n in col:
            wz[:, b * P:b * P + col[n].shape[1]] = col[n]
    low = ZB["low"] * P
    for n, o in (("wd", 0), ("ad", 32), ("mi", 64), ("mf", 96)):
        wz[:, low + o:low + o + col[n].shape[1]] = col[n]
    wf = g["w_ff_in"].reshape(D, 2, 2 * HALF, P).transpose(0, 2, 1, 3).reshape(D, 4 * HALF * P)

    def blocks(w):
        out = np.zeros((P, C4, P), dt)
        for b in range(8):
            o = 64 * (b % 2)
            out[o:o + 64, b // 2, o:o + 64] = w[b]
        return out

    ws = g["gmlp_ws"]
    wss = np.zeros((64, C4, 64), dt)
    for b in range(NS):
        wss[b * LS:(b + 1) * LS, :, b * LS:(b + 1) * LS] = ws[:, :LS, :LS].transpose(2, 0, 1)
    gbias = np.concatenate([g["gmlp_bs"], g["gmlp_bs"], np.tile(g["gmlp_bs"][:, :LS], (1, NS))], 1)

    def featb(x):
        return x.reshape(-1, C4, P).transpose(2, 1, 0)

    def conv_state(x):
        return x.reshape(NS, 3, C4, P).transpose(3, 2, 0, 1)

    x = np.concatenate([g["x_prompt"].reshape(TP, D), g["x_sample"].reshape(NS * LS, D)])
    sh = g["state_rwkv_shift"]
    m0 = g["state_mlstm_m"]
    arrays = {
        "x": x.reshape(T, KD, P).transpose(2, 1, 0), "vec": vec, "con": con, "rowc": rowc,
        "w_z": tiled(wz, NZ), "w_gate": tiled(col["gate"], 4 * KD),
        "w_br": np.concatenate([tiled(g["w_branch"][b], KD) for b in range(4)]),
        "w_o": tiled(g["w_out"], KD), "w_fi": tiled(wf, 4 * HALF),
        "w_fo": np.concatenate([tiled(g["w_ff_out"][h * HALF * P:(h + 1) * HALF * P], KD) for h in range(2)]),
        "lru_wa": blocks(g["lru_wa"]), "lru_wx": blocks(g["lru_wx"]),
        "lru_st": conv_state(g["state_lru_conv"]), "lru_h": featb(g["state_lru_h"]),
        "ws": ws.transpose(2, 0, 1), "wss": wss, "gbias": gbias.reshape(1, C4, T),
        "ml_st": conv_state(g["state_mlstm_conv"]),
        "ml_wq": g["mlstm_wq"], "ml_wk": g["mlstm_wk"],
        "ml_C": g["state_mlstm_C"].transpose(3, 1, 0, 2), "ml_n": g["state_mlstm_n"].transpose(2, 1, 0),
        "ml_m": np.concatenate([np.zeros((1, 4), dt), m0]).T, "ml_mb": np.broadcast_to(m0, (P, NS, 4)),
        "rw_sh": sh[:, :3 * MIX].reshape(NS, 24, 64).transpose(2, 1, 0),
        "rw_gd": sh[:, 3 * MIX + 64:].T, "rw_low": sh[:, 3 * MIX:3 * MIX + 64].T,
        "rw_lora": np.concatenate([g["rwkv_w2"], g["rwkv_a2"]]), "rw_g2": g["rwkv_g2"],
        "rw_S": g["state_rwkv_wkv"].transpose(3, 1, 0, 2),
    }
    arrays = {f"in_{k}": np.ascontiguousarray(v) for k, v in arrays.items()}
    outs = {"y": (P, KD, T), "small": (P, NOUT), "gv": (P, C4, NS * LS), "mCp": (P, 4, P), "mCs": (P, 4, NS, P),
            "Sp": (64, 8, HD), "Ss": (64, 8, NS, HD)}
    nc = bacc.Bacc("TRN2", target_bir_lowering=False, num_devices=1, dynamic_dma_scratch_size=1024)
    ap = {}
    for k, x_ in arrays.items():
        ap[k[3:]] = nc.dram_tensor(k, x_.shape, mybir.dt.from_np(x_.dtype), kind="ExternalInput").ap()
    for k, shape in outs.items():
        ap[k] = nc.dram_tensor(f"out_{k}", shape, F32, kind="ExternalOutput").ap()
    ap["z_scratch"] = nc.dram_tensor("z_scratch", (NZ, P, T), F32).ap()
    build(nc, ap)
    res = run(nc, [arrays], core_ids=[0]).results[0]
    o = {k: res[f"out_{k}"] for k in outs}

    y = o["y"].transpose(2, 1, 0).reshape(T, D)

    def sm(name, *shape, parts=P):
        at, w = OUTS[name]
        return o["small"][:parts, at:at + w].reshape((parts,) + shape)

    def convs(name):
        return sm(name, C4, NSEQ, 3).transpose(2, 3, 1, 0).reshape(NSEQ, 3, MIX)

    lc, mc = convs("lconv"), convs("mconv")
    lh = sm("lh", C4, NSEQ).transpose(2, 1, 0).reshape(NSEQ, MIX)
    nn = sm("n", 4, NSEQ).transpose(2, 1, 0)
    mm = sm("m", NSEQ, parts=4).T
    shift = np.concatenate([sm("shift64", 24, NSEQ, parts=64).transpose(2, 1, 0).reshape(NSEQ, 3 * MIX),
                            sm("shift_low", NSEQ, parts=64).T, sm("shift_gd", NSEQ, parts=96).T], 1)
    Cp = o["mCp"].transpose(1, 2, 0)[None]
    Cs = o["mCs"].transpose(2, 1, 3, 0)
    Sp = o["Sp"].transpose(1, 2, 0)[None]
    Ss = o["Ss"].transpose(2, 1, 3, 0)
    gv = o["gv"].transpose(2, 1, 0).reshape(NS, LS, MIX)
    res = [y[:TP].reshape(1, TP, D), y[TP:].reshape(NS, LS, D)]
    for sl, C_, S_ in ((slice(0, 1), Cp, Sp), (slice(1, NSEQ), Cs, Ss)):
        res += [v_[None] for v_ in (lc[sl], lh[sl], shift[sl], S_, mc[sl], C_, nn[sl], mm[sl])]
    res.append(gv[None])
    return tuple(np.ascontiguousarray(v_) for v_ in res)
```

```python
from contextlib import ExitStack

import numpy as np

import concourse.bass as bass
from concourse import mybir

F32 = mybir.dt.float32
F32R = mybir.dt.float32r
ALU = mybir.AluOpType
ACT = mybir.ActivationFunctionType
AX = mybir.AxisListType

P = 128
D = 2048
KD = D // P
TP = 256
NS, LS = 8, 8
T = TP + NS * LS
MIX = 512
C4 = MIX // P
DFF = 5632
HALF = DFF // P // 2
CW = 4
PAD3 = 3 + TP + NS * (3 + LS)
PAD1 = 1 + TP + NS * (1 + LS)
HD = 64
NSEQ = 1 + NS
PIECE = 8
RING = 4
AHEAD = 3
EXPM05 = float(np.exp(-0.5))

ZB = {"lx": 0, "lg": 4, "gv": 8, "gu": 12, "low": 16, "mx": 17, "mv": 21, "mo": 25, "r": 29, "k": 33, "v": 37,
      "gd": 41}
NZ = 42
NF = NZ + 4 * KD

NFRONT = 2 * NF
PASS0 = NFRONT
OUT0 = PASS0 + 2 * KD
FF0 = OUT0 + 2 * KD
FFIN = 4 * HALF
FFOUT = 3 * KD
NPIECES = FF0 + 2 * (FFIN + FFOUT)
OUT_TILES = [8, 8, HALF - 16]


def layout(widths):
    at, n = {}, 0
    for name, w in widths:
        at[name] = (n, w)
        n += w
    return at, n


VEC, NVEC = layout([("g_pre", KD), ("g_post", KD), ("g_pre2", KD), ("g_post2", KD),
                    ("cw_l", 16), ("cb_l", 4), ("ba", 4), ("bx", 4), ("lam", 4),
                    ("ln_g", 4), ("ln_b", 4), ("cw_m", 16), ("cb_m", 4), ("norm_g", 4), ("skip", 4),
                    ("mu_gd", 1), ("mu_low", 1), ("bi", 1), ("bf", 1),
                    ("mu_r", 4), ("mu_k", 4), ("mu_v", 4), ("w0", 4), ("a0", 4), ("kk", 4), ("ka", 4),
                    ("rk", 4), ("rln_g", 4), ("rln_b", 4),
                    ("eps6", 1), ("eps5", 1), ("eps64", 1)])
CON, NCON = layout([("ident", 128), ("ones", 128), ("ident2", 64), ("ones2", 128), ("maskD", 256), ("maskS", 64),
                    ("n_near", 64), ("n_far", 64), ("nT_near", 64), ("sT", 64), ("iT", 64),
                    ("n_seq", 64), ("nT_seq", 64),
                    ("seq", 8)])
ROWC, NROWC = layout([("sel", 4 * 128), ("keep", T), ("drop", T)])
OUTS, NOUT = layout([("lconv", C4 * NSEQ * 3), ("lh", C4 * NSEQ), ("mconv", C4 * NSEQ * 3), ("n", 4 * NSEQ),
                     ("m", NSEQ), ("shift", 12 * NSEQ), ("shift_gd", NSEQ), ("shift_low", NSEQ)])


def build(nc, a):
    sems = {}
    ctx = ExitStack()
    with ctx:
        def S(name):
            if name not in sems:
                sems[name] = ctx.enter_context(nc.semaphore(name))
            return sems[name]

        def sb(name, shape, dt=F32, c=ctx):
            return c.enter_context(nc.sbuf_tensor(name, shape, dt))

        w_raw = sb("w_raw", [P, RING, PIECE * P])
        w_hi = sb("w_hi", [P, RING, PIECE * P], F32R)
        w_lo = sb("w_lo", [P, RING, PIECE * P], F32R)
        x_hi = sb("x_hi", [P, KD, T], F32R)
        x_lo = sb("x_lo", [P, KD, T], F32R)
        rstd = sb("rstd", [P, T])
        vec = sb("vec", [P, NVEC])
        con = sb("con", [P, NCON])
        ev = sb("ev", [P, 4, T])

        def V(name, i=0, n=1, parts=P):
            return vec[0:parts, VEC[name][0] + i:VEC[name][0] + i + n]

        def K(name, parts=P):
            at, n = CON[name]
            return con[0:parts, at:at + n]

        gate = sb("gate", [P, 2, T])
        term = sb("term", [P, 2, T])
        ssum2 = sb("ssum2", [P, T])
        small = sb("small", [P, NOUT])

        p1 = ExitStack()
        y_hi = sb("y_hi", [P, 4 * C4, T], F32R, p1)
        y_lo = sb("y_lo", [P, 4 * C4, T], F32R, p1)
        ARENA = 17720
        arena = sb("arena", [P, ARENA], c=p1)
        p1.close()
        p2 = ExitStack()
        a_hi = sb("a_hi", [P, HALF, T], F32R, p2)
        a_lo = sb("a_lo", [P, HALF, T], F32R, p2)
        xres = sb("xres", [P, KD, T], c=p2)
        mix = sb("mix", [P, KD, T], c=p2)
        p2.close()

        def psum(i):
            return ctx.enter_context(nc.psum_tensor(f"bank{i}", [P, 512], F32))

        G = [psum(i) for i in range(4)]
        M = [psum(4 + i) for i in range(4)]

        class Views:

            def __init__(self, at=0, limit=ARENA):
                self.at, self.limit = at, limit

            def take(self, *shape, parts=P):
                n = int(np.prod(shape))
                v = arena[0:parts, self.at:self.at + n]
                self.at += n
                assert self.at <= self.limit, (self.at, self.limit)
                if len(shape) == 2:
                    v = v.rearrange("p (a b) -> p a b", a=shape[0])
                if len(shape) == 3:
                    v = v.rearrange("p (a b c) -> p a b c", a=shape[0], b=shape[1])
                return v

        start = Views()
        xin = start.take(KD, T)
        xsq = start.take(KD, T)
        ssum = start.take(T)
        va = Views()
        a_cin = va.take(C4, PAD3)
        a_acc = va.take(C4, PAD3)
        a_xc = va.take(C4, T)
        a_gz = va.take(C4, T)
        a_r = va.take(C4, T)
        a_i = va.take(C4, T)
        a_a = va.take(C4, T)
        a_st = va.take(C4, NS, 3)
        a_h0 = va.take(C4, NS)
        a_wa = va.take(C4, P)
        a_wx = va.take(C4, P)
        a_t = va.take(6, C4)
        a_sm = va.take(C4, NS)
        vb = Views()
        b_u = vb.take(C4, T)
        b_v = vb.take(C4, T)
        b_q = vb.take(C4, T)
        b_std = vb.take(T)
        b_tok = vb.take(3, MIX)
        b_ws = vb.take(C4, P)
        b_wss = vb.take(C4, 64, parts=64)
        b_bias = vb.take(C4, T, parts=1)
        vd = Views()
        d_cin = vd.take(C4, PAD3)
        d_acc = vd.take(C4, PAD3)
        d_c = vd.take(C4, T)
        d_v = vd.take(C4, T)
        d_o = vd.take(C4, T)
        d_st = vd.take(C4, NS, 3)
        d_wq = vd.take(P)
        d_wk = vd.take(P)
        d_C = vd.take(NS, P)
        d_n = vd.take(4, NS)
        d_m0b = vd.take(NS, 4)
        d_rows = vd.take(7, T, parts=4)
        d_m0 = vd.take(NSEQ, parts=4)
        d_mend = vd.take(NSEQ, parts=4)
        d_md = vd.take(NSEQ, 4, parts=4)
        d_g = vd.take(12)
        d_me = vd.take(NSEQ, 4)
        d_wp = vd.take(2, 4)
        d_wm = vd.take(NS, 4, parts=64)
        d_dec = vd.take(NS, 4)
        ve = Views(limit=2 * C4 * PAD3)
        e_q = ve.take(T)
        e_k = ve.take(T)
        e_ktok = ve.take(3, P)
        e_vtok = ve.take(3, P)
        e_E = ve.take(448)
        e_em = ve.take(T)
        d_vm = vd.take(NS + 2, P)
        d_h = vd.take(T)
        d_s = vd.take(T)
        d_qs = vd.take(64)
        d_qn = vd.take(64)
        d_rc = vd.take(NROWC, parts=4)
        vc = Views()
        c_zp = vc.take(4, PAD1)
        c_d96 = arena[0:96, vc.at:vc.at + PAD1]
        c_d = vc.take(4, PAD1)
        c_gdp = vc.take(PAD1, parts=96)
        c_lowp = vc.take(PAD1, parts=64)
        vc.take(42)
        vh = Views(limit=vc.at)
        (h_N, h_Q, h_F, h_ak, h_rb, h_rk, h_T, h_P2, h_Q2, h_E, h_btok, h_ktok, h_vtok) = [
            vh.take(4, 64) for _ in range(13)]
        c_r, c_k, c_v, c_w, c_a, c_kk, c_t, c_rk = [vc.take(4, T) for _ in range(8)]
        c_gd = vc.take(T, parts=96)
        c_low = vc.take(T, parts=64)
        c_g2 = vc.take(MIX, parts=96)
        c_lora = vc.take(MIX, parts=64)
        c_wend = vc.take(4, 4 + NS)
        c_S = vc.take(4, 64)
        c_Ss = vc.take(4, NS, HD)
        c_sh = vc.take(12, NS)
        c_shlow = vc.take(NS, parts=64)
        c_shgd = vc.take(NS, parts=96)
        c_um = c_a.rearrange("p a b -> p (a b)")[:, 0:2 * NS * HD].rearrange("p (a b) -> p a b", a=2)

        merging = Views()
        g_in = merging.take(2, 4, T)
        g_t = arena[:, vh.limit:vh.limit + 4 * T].rearrange("p (a b) -> p a b", a=4)

        def O(name, parts=P):
            at, n = OUTS[name]
            return small[0:parts, at:at + n]

        zD = a["front_scratch"]

        def bc(ap, axis, n):
            x = ap.unsqueeze(axis)
            shape = list(x.shape)
            shape[axis] = n
            return x.broadcast_to(shape)

        def seqs(ap, w):
            return ap.rearrange("p c (b e) -> p c b e", e=w)

        plan = {}
        uses = [0] * 4

        def planned(b, *key):
            plan[key] = (b, uses[b])
            uses[b] += 1

        for c in range(C4):
            planned(c, "A_r", c)
            planned(c, "A_i", c)
        planned(0, "B_sum")
        planned(1, "B_var")
        for t, b in enumerate((2, 3, 0)):
            planned(b, "B_turned", t)
        for c in range(C4):
            planned(c, "B_s", c)
        planned(0, "D_turned")
        for h in range(4):
            for b, name in ((0, "D_q"), (1, "D_k"), (2, "D_ktok"), (3, "D_vtok"), (0, "D_Mb"), (1, "D_eb"), (2, "D_sb"),
                            (3, "D_qk"), (0, "D_num"), (1, "D_den"), (2, "D_mean"), (3, "D_var")):
                planned(b, name, h)
            planned(0, "D_Cs", h, 0)
            planned(1, "D_Cs", h, 1)
            planned(2, "D_Cp", h)
        for h in range(4):
            for key in (("C_lora", 0, h), ("C_lora", 1, h), ("C_kk_sum", h), ("C_rk_sum", h)):
                planned(h, *key)
        for ch in range(5):
            for b, name in ((0, "C_N"), (1, "C_NT"), (2, "C_ak"), (3, "C_rb"), (0, "C_rk"), (1, "C_btok"),
                            (2, "C_ktok"), (3, "C_vtok"), (0, "C_p2"), (1, "C_q2"), (2, "C_t2"), (0, "C_p4"),
                            (1, "C_q4"), (2, "C_t4")):
                planned(b, name, ch)
            if ch < 4:
                for b, name in ((0, "C_p8"), (2, "C_t8"), (0, "C_zT"), (1, "C_z"), (2, "C_z2"), (0, "C_e"),
                                (3, "C_rhs"), (1, "C_y"), (2, "C_u"), (3, "C_o"), (0, "C_S")):
                    planned(b, name, ch)
            else:
                for b, name in ((0, "C_u0"), (3, "C_rhs"), (1, "C_y"), (3, "C_o")):
                    planned(b, name, ch)
                for h in range(4):
                    planned(h % 2, "C_Ss", h)
        for h in range(4):
            for name in ("C_mean", "C_var", "C_gate"):
                planned(h, name, h)

        at = {}
        part = {}

        def full(eng, *key):
            part[eng](at[key])
            b, i = plan[key]
            eng.wait_ge(S(f"bank_full{b}"), i + 1)

        def upto(eng, name, back=0):
            part[eng](at[name] - back)

        def stored(act, block):
            act_part = part[act]
            act_part(2 * block + 2)
            for b in range(4):
                n = len(range(b, block + 1, 4))
                if n:
                    act.wait_ge(S(f"ev_out{b}"), 16 * (n + 1))

        def read(*key):
            return S(f"bank_read{plan[key][0]}")

        def use(*key):
            b, i = plan[key]
            return f"bank_read{b}", i + 1

        def was_read(eng, *key):
            if eng in part:
                part[eng](at[key])
            b, i = plan[key]
            eng.wait_ge(S(f"bank_read{b}"), i + 1)

        def mixers_pe(pe, pieces):
            def fill(name, n):
                at[name] = pieces(n)

            ident, ones = K("ident"), K("ones")

            def bank(*key):
                at[key] = pieces(0)
                b, i = plan[key]
                if i:
                    pe.wait_ge(S(f"bank_read{b}"), i)
                return M[b]

            def filled(mm, *key):
                mm.then_inc(S(f"bank_full{plan[key][0]}"), 1)

            def single(lhs, rhs, *key, parts=P):
                o = bank(*key)
                filled(pe.matmul(o[0:parts, 0:T], lhs, rhs, start=True, stop=True), *key)

            fill("A_conv", 7)
            pe.wait_ge(S("A_weights_in"), 32)
            pe.wait_ge(S("A_conv"), 2 * C4)
            pe.wait_ge(S("x_std"), 1)
            for c in range(C4):
                single(a_wa[:, c, :], a_xc[:, c, :], "A_r", c)
            for c in range(C4):
                single(a_wx[:, c, :], a_xc[:, c, :], "A_i", c)

            fill("A_tail", 7)
            fill("B_in", 6)
            pe.wait_ge(S("B_gelu"), 1)
            o = bank("B_sum")
            for c in range(C4):
                mm = pe.matmul(o[:, 0:T], ones, b_v[:, c, :], start=c == 0, stop=c == C4 - 1)
            filled(mm, "B_sum")
            fill("B_sq", 1)
            pe.wait_ge(S("B_sq"), 1)
            o = bank("B_var")
            for c in range(C4):
                mm = pe.matmul(o[:, 0:T], ones, b_q[:, c, :], start=c == 0, stop=c == C4 - 1)
            filled(mm, "B_var")
            fill("B_v", 2)
            pe.wait_ge(S("B_v"), C4)
            for t, (t0, n) in enumerate(((0, P), (P, P), (TP, 64))):
                o = bank("B_turned", t)
                for c in range(C4):
                    mm = pe.transpose(o[0:n, c * P:(c + 1) * P], b_v[:, c, t0:t0 + n], ident)
                filled(mm, "B_turned", t)
            fill("B_tok", 1)
            for t in range(3):
                was_read(pe, "B_turned", t)
            pe.wait_ge(S("B_masked"), 2)
            pe.wait_ge(S("B_bias_in"), 16)
            for c in range(C4):
                f = slice(c * P, (c + 1) * P)
                o = bank("B_s", c)
                pe.matmul(o[:, 0:T], K("ones", 1), b_bias[:, c, :], start=True, stop=False)
                pe.matmul(o[:, 0:P], b_tok[:, 0, f], b_ws[:, c, :], start=False, stop=False)
                pe.matmul(o[:, P:TP], b_tok[:, 1, f], b_ws[:, c, :], start=False, stop=False)
                filled(pe.matmul(o[:, TP:T], b_tok[0:64, 2, f], b_wss[:, c, :], start=False, stop=True), "B_s", c)

            fill("D_rows", 10)
            pe.wait_ge(S("D_rows"), 1)
            token_tiles = ((0, P), (P, P), (TP, 64))
            o = bank("D_turned")
            for t, (t0, n) in enumerate(token_tiles):
                pe.transpose(o[0:n, 4 * t:4 * t + 4], d_rows[:, 1, t0:t0 + n], K("ident", 4)[:, 0:4])
            filled(pe.matmul(o[:, 16:16 + 4 * NSEQ], K("ones", 4), d_md.rearrange("p a b -> p (a b)"),
                             start=True, stop=True), "D_turned")
            fill("D_conv", 12)
            pe.wait_ge(S("D_silu"), 1)
            for h in range(4):
                fill(("D_wq", h), 3)
                pe.wait_ge(S("D_wq_in"), 32 * (h + 1))
                pe.wait_ge(S("D_v_in"), 16)
                single(d_wq, d_c[:, h, :], "D_q", h)
                single(d_wk, d_c[:, h, :], "D_k", h)
                o = bank("D_ktok", h)
                for t, (t0, n) in enumerate(token_tiles):
                    mm = pe.matmul(o[0:n, t * P:(t + 1) * P], d_c[:, h, t0:t0 + n], d_wk, start=True, stop=True,
                                   skip_group_check=True)
                filled(mm, "D_ktok", h)
                o = bank("D_vtok", h)
                for t, (t0, n) in enumerate(token_tiles):
                    mm = pe.transpose(o[0:n, t * P:(t + 1) * P], d_v[:, h, t0:t0 + n], ident)
                filled(mm, "D_vtok", h)
                sel = d_rc[:, h * P:(h + 1) * P]
                single(sel, d_rows[:, 0, :], "D_Mb", h)
                single(sel, d_rows[:, 5, :], "D_eb", h)
                o = bank("D_sb", h)
                filled(pe.matmul(o[:, 0:64], sel, d_rows[:, 6, TP:T], start=True, stop=True), "D_sb", h)
                fill(("D_qk_", h), 1)
                was_read(pe, "D_q", h)
                was_read(pe, "D_k", h)
                o = bank("D_qk", h)
                pe.matmul(o[:, 0:TP], e_k[:, 0:P], e_q[:, 0:TP], start=True, stop=True, skip_group_check=True)
                pe.matmul(o[:, TP:TP + P], e_k[:, P:TP], e_q[:, P:TP], start=True, stop=True, skip_group_check=True)
                filled(pe.matmul(o[0:64, 384:448], e_k[:, TP:T], e_q[:, TP:T], start=True, stop=True,
                                 skip_group_check=True), "D_qk", h)
                fill(("D_num_", h), 2)
                was_read(pe, "D_qk", h)
                was_read(pe, "D_vtok", h)
                was_read(pe, "D_sb", h)
                pe.wait_ge(S("D_C_in"), 16 * (h + 1))
                o = bank("D_num", h)
                pe.matmul(o[:, 0:TP], e_vtok[:, 0, :], e_E[:, 0:TP], start=True, stop=False)
                pe.matmul(o[:, P:TP], e_vtok[:, 1, :], e_E[:, TP:TP + P], start=False, stop=False)
                pe.matmul(o[:, TP:T], e_vtok[0:64, 2, :], e_E[0:64, 384:448], start=False, stop=False)
                for b in range(NS):
                    mm = pe.matmul(o[:, TP + LS * b:TP + LS * b + LS], d_C[:, b, :], d_qs[:, LS * b:LS * b + LS],
                                   start=False, stop=b == NS - 1)
                filled(mm, "D_num", h)
                pe.wait_ge(S("D_qn"), h + 1)
                o = bank("D_den", h)
                pe.matmul(o[:, 0:TP], ones, e_E[:, 0:TP], start=True, stop=False)
                pe.matmul(o[:, P:TP], ones, e_E[:, TP:TP + P], start=False, stop=False)
                pe.matmul(o[:, TP:T], K("ones", 64), e_E[0:64, 384:448], start=False, stop=False)
                filled(pe.matmul(o[:, TP:T], ones, d_qn, start=False, stop=True), "D_den", h)
                fill(("D_mean_", h), 1)
                was_read(pe, "D_num", h)
                single(ones, d_h, "D_mean", h)
                fill(("D_sq", h), 1)
                pe.wait_ge(S("D_sq"), h + 1)
                single(ones, d_s, "D_var", h)
                fill(("D_vm", h), 1)
                was_read(pe, "D_ktok", h)
                pe.wait_ge(S("D_vm"), 3 * (h + 1))
                for i in range(2):
                    o = bank("D_Cs", h, i)
                    filled(pe.matmul(o[:, :], e_ktok[0:64, 2, :], d_vm[0:64, 4 * i:4 * i + 4, :].rearrange("p a b -> p (a b)"),
                                     start=True, stop=True), "D_Cs", h, i)
                o = bank("D_Cp", h)
                for t in range(2):
                    pe.matmul(o[:, 0:P], e_ktok[:, t, :], d_vm[:, NS + t, :], start=t == 0, stop=t == 1,
                              skip_group_check=True)
                pe.matmul(o[:, P:P + NS], e_ktok[0:64, 2, :], d_wm[:, :, h], start=True, stop=True, skip_group_check=True)
                for t in range(2):
                    mm = pe.matmul(o[:, P + NS:P + NS + 1], e_ktok[:, t, :], d_wp[:, t, h:h + 1], start=t == 0,
                                   stop=t == 1, skip_group_check=True)
                filled(mm, "D_Cp", h)

            hs = range(4)
            both = (slice(0, 64), slice(64, P))
            ident2 = K("ident2")
            fill("C_low", 8)
            pe.wait_ge(S("C_low"), 2)
            for what in range(2):
                r = slice(32 * what, 32 * what + 32)
                for h in hs:
                    single(c_lora[r, h * P:(h + 1) * P], c_low[r, :], "C_lora", what, h)
            fill("C_kk", 6)
            pe.wait_ge(S("C_kk_sq"), 1)
            for h in hs:
                single(K("ones2"), c_t[:, h, :], "C_kk_sum", h)
            fill("C_rk", 6)
            pe.wait_ge(S("C_rk"), 1)
            for h in hs:
                single(K("ones2"), c_rk[:, h, :], "C_rk_sum", h)
            fill("C_scaled", 10)
            pe.wait_ge(S("C_scaled"), 1)
            for ch in range(5):
                n = ch
                ts = slice(64 * ch, 64 * ch + 64)
                smp = ch == 4
                At, Bt, Kt, Rt, Vt = [lambda q, h, x=x: x[q, h, ts] for x in (c_w, c_kk, c_k, c_r, c_v)]

                def of(x):
                    return lambda q, h: x[q, h, :]

                def heads(name, lhs, rhs, *more):
                    o = bank(name, n)
                    pairs = ((lhs, rhs),) + more
                    for h in hs:
                        for i, (l, r) in enumerate(pairs):
                            for q in both:
                                mm = pe.matmul(o[q, 64 * h:64 * h + 64], l(q, h), r(q, h), start=i == 0,
                                               stop=i == len(pairs) - 1, skip_group_check=True)
                    filled(mm, name, n)

                heads("C_N", At, Bt)
                heads("C_NT", Bt, At)
                heads("C_ak", Kt, At)
                heads("C_rb", Bt, Rt)
                heads("C_rk", Kt, Rt)
                for name, x in (("C_btok", Bt), ("C_ktok", Kt), ("C_vtok", Vt)):
                    o = bank(name, n)
                    for h in hs:
                        for q in both:
                            mm = pe.matmul(o[q, 64 * h:64 * h + 64], x(q, h), ident2[q, :], start=True, stop=True,
                                           skip_group_check=True)
                    filled(mm, name, n)
                fill(("C_QI", n), 1)
                pe.wait_ge(S("C_QI"), n + 1)
                heads("C_p2", of(h_Q), of(h_N))
                heads("C_q2", of(h_N), of(h_Q))
                fill(("C_2", n), 1)
                was_read(pe, "C_p2", n)
                was_read(pe, "C_q2", n)
                heads("C_t2", of(h_P2), of(h_T))
                heads("C_p4", of(h_Q2), of(h_P2))
                heads("C_q4", of(h_P2), of(h_Q2))
                fill(("C_4", n), 1)
                was_read(pe, "C_p4", n)
                was_read(pe, "C_q4", n)
                was_read(pe, "C_t2", n)
                heads("C_t4", of(h_P2), of(h_T))
                if not smp:
                    heads("C_p8", of(h_Q2), of(h_P2))
                    fill(("C_8", n), 1)
                    was_read(pe, "C_p8", n)
                    was_read(pe, "C_t4", n)
                    heads("C_t8", of(h_P2), of(h_T))
                    fill(("C_8t", n), 1)
                    was_read(pe, "C_t8", n)
                    heads("C_zT", of(h_F), of(h_T))
                    heads("C_z", of(h_T), of(h_F))
                    fill(("C_Z", n), 1)
                    was_read(pe, "C_zT", n)
                    was_read(pe, "C_z", n)
                    heads("C_z2", of(h_P2), of(h_Q2))
                    fill(("C_Z2", n), 1)
                    was_read(pe, "C_z2", n)
                    pe.wait_ge(S("C_E"), ch + 1)
                    heads("C_e", of(h_N), of(h_E))
                    pe.wait_ge(S("C_S_ready"), ch + 1)
                    heads("C_rhs", of(h_ak), of(h_vtok), (At, of(c_S)))
                    fill(("C_R", n), 1)
                    was_read(pe, "C_rhs", n)
                    heads("C_y", of(h_T), of(h_P2))
                    fill(("C_Y", n), 1)
                    was_read(pe, "C_e", n)
                    was_read(pe, "C_y", n)
                    heads("C_u", of(h_E), of(h_Q2))
                    fill(("C_U", n), 1)
                    was_read(pe, "C_u", n)
                    heads("C_o", of(h_vtok), of(h_rk), (of(h_F), of(h_rb)), (of(c_S), Rt))
                    heads("C_S", of(h_btok), of(h_F), (of(h_ktok), of(h_vtok)))
                else:
                    pe.wait_ge(S("C_Ss_in"), 16)
                    o = bank("C_u0", n)
                    for h in hs:
                        for b in range(NS):
                            for q in both:
                                mm = pe.matmul(o[q, 64 * h + LS * b:64 * h + LS * b + LS], c_Ss[q, h, b, :],
                                               c_w[q, h, TP + LS * b:TP + LS * b + LS], start=True, stop=True,
                                               skip_group_check=True)
                    filled(mm, "C_u0", n)
                    fill(("C_U0", n), 1)
                    was_read(pe, "C_u0", n)
                    was_read(pe, "C_t4", n)
                    heads("C_rhs", of(h_ak), of(h_vtok), (of(h_N), lambda q, h: ident2[q, :]))
                    fill(("C_R", n), 1)
                    was_read(pe, "C_rhs", n)
                    heads("C_y", of(h_T), of(h_P2))
                    was_read(pe, "C_y", n)
                    o = bank("C_o", n)
                    for h in hs:
                        for q in both:
                            oh = o[q, 64 * h:64 * h + 64]
                            pe.matmul(oh, h_vtok[q, h, :], h_rk[q, h, :], start=True, stop=False, skip_group_check=True)
                            pe.matmul(oh, h_F[q, h, :], h_rb[q, h, :], start=False, stop=False, skip_group_check=True)
                            for b in range(NS):
                                mm = pe.matmul(o[q, 64 * h + LS * b:64 * h + LS * b + LS], c_Ss[q, h, b, :],
                                               c_r[q, h, TP + LS * b:TP + LS * b + LS], start=False,
                                               stop=b == NS - 1, skip_group_check=True)
                    filled(mm, "C_o", n)
                    for h in hs:
                        fill(("C_um", h), 1)
                        pe.wait_ge(S("C_um"), 2 * h + 2)
                        o = bank("C_Ss", h)
                        for x, tok in enumerate((h_btok, h_ktok)):
                            for q in both:
                                mm = pe.matmul(o[q, :], tok[q, h, :], c_um[q, x, :], start=x == 0, stop=x == 1,
                                               skip_group_check=True)
                        filled(mm, "C_Ss", h)
            fill("C_mean", 1)
            was_read(pe, "C_o", 4)
            for h in hs:
                single(K("ones2"), c_t[:, h, :], "C_mean", h)
            fill("C_var", 1)
            pe.wait_ge(S("C_osq"), 1)
            for h in hs:
                single(K("ones2"), c_k[:, h, :], "C_var", h)
            for h in hs:
                single(c_g2[:, h * P:(h + 1) * P], c_gd, "C_gate", h)

        def padded(eng, dst, rows, pad, sem):
            src = zD[rows] if isinstance(rows, int) else rows
            eng.dma_start(dst[:, pad:pad + TP], src[:, 0:TP]).then_inc(sem, 16)
            eng.dma_start(dst[:, pad + TP:].rearrange("p (b e) -> p b e", b=NS)[:, :, pad:],
                          src[:, TP:T].rearrange("p (b e) -> p b e", b=NS)).then_inc(sem, 16)

        def whole(name):
            return zD[ZB[name]:ZB[name] + 4].rearrange("c p t -> p c t")

        def mixers_act(act):
            sc = nc.scalar
            act.wait_ge(S("x_lo_made"), KD)
            act.wait_ge(S("x_ss"), 1)
            for c in range(C4):
                stored(act, ZB["lx"] + c)
                padded(act, a_cin[:, c, :], ZB["lx"] + c, 3, S("A_in"))
            act.dma_start(a_st, a["lru_st"]).then_inc(S("A_in"), 16)
            act.dma_start(a_h0, a["lru_h"]).then_inc(S("A_in"), 16)
            stored(act, ZB["lg"] + 3)
            act.dma_start(a_gz, whole("lg")).then_inc(S("A_gz_in"), 16)
            act.dma_start(a_wa, a["lru_wa"]).then_inc(S("A_weights_in"), 16)
            act.dma_start(a_wx, a["lru_wx"]).then_inc(S("A_weights_in"), 16)
            act.wait_ge(S("A_abs"), 1)
            sc.activation(a_t[:, 1, :], a_t[:, 0, :], ACT.Exp, scale=-1.0).then_inc(S("A_exp"), 1)
            act.wait_ge(S("A_gz_in"), 16)
            sc.activation(a_gz, a_gz, ACT.Gelu_apprx_tanh).then_inc(S("A_gelu"), 1)
            for c in range(C4):
                full(act, "A_r", c)
                sc.activation(a_r[:, c, :], M[c][:, 0:T], ACT.Sigmoid, bias=V("ba", c)).then_inc(read("A_r", c), 1)
            for c in range(C4):
                full(act, "A_i", c)
                sc.activation(a_i[:, c, :], M[c][:, 0:T], ACT.Sigmoid, bias=V("bx", c)).then_inc(read("A_i", c), 1)
            act.wait_ge(S("A_soft"), 1)
            for c in range(C4):
                was_read(act, "A_r", c)
                sc.activation(a_r[:, c, :], a_r[:, c, :], ACT.Tanh, scale=a_t[:, 4, c:c + 1]).then_inc(S("A_p"), 1)
            act.wait_ge(S("A_p"), C4)
            act.wait_ge(S("A_conv"), 2 * C4)
            sc.activation(a_acc[:, :, 0:T], a_r, ACT.Sqrt).then_inc(S("A_root"), 1)
            upto(act, "A_tail")
            act.wait_ge(S("A_y"), 1)
            for c in range(C4):
                sc.activation(y_hi[:, c, :], a_i[:, c, :], ACT.Copy).then_inc(S("y_hi0"), 1)

            act.wait_ge(S("y_lo0"), C4)
            stored(act, ZB["gu"] + 3)
            act.dma_start(b_v, whole("gv")).then_inc(S("B_v_in"), 16)
            act.dma_start(b_u, whole("gu")).then_inc(S("B_u_in"), 16)
            act.dma_start(b_ws, a["ws"]).then_inc(S("B_ws_in"), 16)
            act.dma_start(b_wss, a["wss"]).then_inc(S("B_ws_in"), 16)
            act.dma_start(b_bias, a["gbias"]).then_inc(S("B_bias_in"), 16)
            upto(act, "B_in")
            act.wait_ge(S("B_v_in"), 16)
            sc.activation(b_v, b_v, ACT.Gelu_apprx_tanh).then_inc(S("B_gelu"), 1)
            act.wait_ge(S("B_u_in"), 16)
            sc.activation(b_u, b_u, ACT.Gelu_apprx_tanh).then_inc(S("B_gelu_u"), 1)
            full(act, "B_var")
            sc.activation(b_std, M[1][:, 0:T], ACT.Sqrt, scale=1.0 / MIX, bias=V("eps5")).then_inc(read("B_var"), 1)
            for t, (n, bank) in enumerate(((P, 2), (P, 3), (64, 0))):
                full(act, "B_turned", t)
                sc.activation(b_tok[0:n, t, :], M[bank][0:n, :], ACT.Copy).then_inc(read("B_turned", t), 1)
            act.dma_start(a["gv"], b_v[:, :, TP:T]).then_inc(S("B_out"), 16)
            for c in range(C4):
                was_read(act, "B_s", c)
                sc.activation(y_hi[:, 4 + c, :], b_q[:, c, :], ACT.Copy).then_inc(S("y_hi1"), 1)

            act.wait_ge(S("y_lo1"), C4)
            act.wait_ge(S("B_out"), 16)
            low = zD[ZB["low"]]
            stored(act, ZB["low"])
            act.dma_start(d_rows[:, 0, :], low[64:68, :]).then_inc(S("D_rows_in"), 16)
            act.dma_start(d_rows[:, 1, :], low[96:100, :]).then_inc(S("D_rows_in"), 16)
            act.dma_start(d_rc, a["rowc"]).then_inc(S("D_rows_in"), 16)
            act.dma_start(d_m0, a["ml_m"]).then_inc(S("D_rows_in"), 16)
            act.dma_start(d_m0b, a["ml_mb"]).then_inc(S("D_rows_in"), 16)
            act.dma_start(d_n, a["ml_n"]).then_inc(S("D_n_in"), 16)
            act.dma_start(d_st, a["ml_st"]).then_inc(S("D_in"), 16)
            for c in range(C4):
                stored(act, ZB["mx"] + c)
                padded(act, d_cin[:, c, :], ZB["mx"] + c, 3, S("D_in"))
            act.dma_start(d_wq, a["ml_wq"][0]).then_inc(S("D_wq_in"), 16)
            act.dma_start(d_wk, a["ml_wk"][0]).then_inc(S("D_wq_in"), 16)
            act.dma_start(d_C, a["ml_C"][:, 0]).then_inc(S("D_C_in"), 16)
            upto(act, "D_rows", 4)
            act.wait_ge(S("D_abs"), 1)
            sc.activation(d_rows[:, 4, :], d_rows[:, 3, :], ACT.Exp, scale=-1.0).then_inc(S("D_exp"), 1)
            upto(act, "D_rows")
            act.wait_ge(S("D_bm"), 2)
            sc.activation(d_rows[:, 5, :], d_rows[:, 5, :], ACT.Exp, scale=-1.0).then_inc(S("D_ex"), 1)
            sc.activation(d_rows[:, 6, TP:T], d_rows[:, 6, TP:T], ACT.Exp).then_inc(S("D_ex"), 1)
            act.wait_ge(S("D_warg"), 3)
            sc.activation(d_wp, d_wp, ACT.Exp).then_inc(S("D_wexp"), 1)
            sc.activation(d_wm, d_wm, ACT.Exp).then_inc(S("D_wexp"), 1)
            sc.activation(d_dec, d_dec, ACT.Exp).then_inc(S("D_wexp"), 1)
            upto(act, "D_conv", 2)
            stored(act, ZB["mo"] + 3)
            act.dma_start(d_v, whole("mv")).then_inc(S("D_v_in"), 16)
            act.dma_start(d_o, whole("mo")).then_inc(S("D_o_in"), 16)
            upto(act, "D_conv")
            act.wait_ge(S("D_conv"), 2 * C4)
            sc.activation(d_c, d_c, ACT.Silu).then_inc(S("D_silu"), 1)
            act.wait_ge(S("D_o_in"), 16)
            sc.activation(d_o, d_o, ACT.Sigmoid).then_inc(S("D_osig"), 1)
            for h in range(4):
                full(act, "D_q", h)
                sc.activation(e_q, M[0][:, 0:T], ACT.Copy).then_inc(read("D_q", h), 1)
                full(act, "D_k", h)
                sc.activation(e_k, M[1][:, 0:T], ACT.Copy, scale=float(P) ** -0.5).then_inc(read("D_k", h), 1)
                full(act, "D_eb", h)
                sc.activation(e_em, M[1][:, 0:T], ACT.Copy).then_inc(read("D_eb", h), 1)
                act.wait_ge(S("D_E"), 2 * (h + 1))
                was_read(act, "D_Mb", h)
                sc.activation(e_E[:, 0:384], e_E[:, 0:384], ACT.Exp, scale=-1.0).then_inc(S("D_Eexp"), 1)
                sc.activation(e_E[0:64, 384:448], e_E[0:64, 384:448], ACT.Exp, scale=-1.0).then_inc(S("D_Eexp"), 1)
                full(act, "D_var", h)
                sc.activation(d_s, M[3][:, 0:T], ACT.Sqrt, scale=1.0 / P, bias=V("eps6")).then_inc(read("D_var", h), 1)
                act.wait_ge(S("D_y"), h + 1)
                sc.activation(y_hi[:, 12 + h, :], d_h, ACT.Copy).then_inc(S("D_yhi"), 1)
                was_read(act, "D_Cs", h, 0)
                was_read(act, "D_Cs", h, 1)
                act.dma_start(a["mCs"][:, h], d_C).then_inc(S("D_out"), 16)
                act.wait_ge(S("D_Cp"), h + 1)
                act.dma_start(a["mCp"][:, h], e_vtok[:, 0, :]).then_inc(S("D_out"), 16)
                if h == 3:
                    upto(act, "C_low", 6)
                act.wait_ge(S("D_out"), 32 * (h + 1))
                if h < 3:
                    act.dma_start(d_wq, a["ml_wq"][h + 1]).then_inc(S("D_wq_in"), 16)
                    act.dma_start(d_wk, a["ml_wk"][h + 1]).then_inc(S("D_wq_in"), 16)
                    act.dma_start(d_C, a["ml_C"][:, h + 1]).then_inc(S("D_C_in"), 16)
                nc.scalar.nop().then_inc(S("D_out_done"), 1)

            act.wait_ge(S("y_lo3"), C4)
            was_read(act, "D_Cp", 3)
            def features(name):
                for h in range(4):
                    stored(act, ZB[name] + h)
                    padded(act, c_zp[:, h, :], ZB[name] + h, 1, S("C_z_in"))

            features("r")
            stored(act, ZB["gd"])
            padded(act, c_lowp, zD[ZB["low"]][0:64], 1, S("C_z_in"))
            padded(act, c_gdp, zD[ZB["gd"]][0:96], 1, S("C_z_in"))
            act.dma_start(c_sh, a["rw_sh"]).then_inc(S("C_sh_in"), 16)
            act.dma_start(c_shlow, a["rw_low"]).then_inc(S("C_sh_in"), 16)
            act.dma_start(c_shgd, a["rw_gd"]).then_inc(S("C_sh_in"), 16)
            act.dma_start(c_lora, a["rw_lora"]).then_inc(S("C_lora_in"), 16)
            act.dma_start(c_g2, a["rw_g2"]).then_inc(S("C_lora_in"), 16)
            act.dma_start(c_Ss, a["rw_S"]).then_inc(S("C_Ss_in"), 16)
            upto(act, "C_low", 3)
            act.wait_ge(S("C_mixed"), 2)
            act.wait_ge(S("C_mixed_low"), 4)
            features("k")
            act.wait_ge(S("C_lora_in"), 32)
            sc.activation(c_low[0:32, :], c_low[0:32, :], ACT.Tanh).then_inc(S("C_low"), 1)
            sc.activation(c_gd, c_gd, ACT.Sigmoid).then_inc(S("C_low"), 1)
            upto(act, "C_low")
            for what, dst, bias in ((0, c_w, "w0"), (1, c_a, "a0")):
                for h in range(4):
                    full(act, "C_lora", what, h)
                    sc.activation(dst[:, h, :], M[h][:, 0:T], ACT.Sigmoid,
                                  bias=V(bias, h)).then_inc(read("C_lora", what, h), 1)
            for h in range(4):
                was_read(act, "C_lora", 0, h)
            sc.activation(c_w, c_w, ACT.Exp, scale=-EXPM05).then_inc(S("C_decay"), 1)
            act.wait_ge(S("C_mixed"), 4)
            features("v")
            for h in range(4):
                full(act, "C_kk_sum", h)
                sc.activation(c_rk[:, h, :], M[h][:, 0:T], ACT.Sqrt).then_inc(read("C_kk_sum", h), 1)
            for h in range(4):
                full(act, "C_var", h)
                sc.activation(c_k[:, h, :], M[h][:, 0:T], ACT.Sqrt, scale=1.0 / HD,
                              bias=V("eps64")).then_inc(read("C_var", h), 1)
            upto(act, "end")
            for h in range(4):
                was_read(act, "C_gate", h)
                sc.activation(y_hi[:, 8 + h, :], c_t[:, h, :], ACT.Copy).then_inc(S("y_hi2"), 1)
            act.wait_ge(S("C_S_ready"), 5)
            act.dma_start(a["Sp"], c_S).then_inc(S("C_out"), 16)
            act.wait_ge(S("C_Ss_made"), 4)
            act.dma_start(a["Ss"], c_Ss).then_inc(S("C_out"), 16)

        def mixers_dve(dve, link, sync):
            v = nc.vector
            tt, ts, stt = v.tensor_tensor, v.tensor_scalar, v.scalar_tensor_tensor

            def put(ins, name, n):
                ins.then_inc(S(name), 1)
                dve.wait_ge(S(name), n)

            def softplus_of(x, y, s, s2, q, out, n_out):
                link(ts(s, y, 2.0, None, ALU.add)); sync()
                link(v.reciprocal(s, s)); sync()
                link(tt(s, s, y, ALU.mult)); sync()
                link(tt(s2, s, s, ALU.mult)); sync()
                link(ts(q, s2, 1.0 / 15, None, ALU.mult)); sync()
                for d in (13, 11, 9, 7, 5, 3):
                    link(stt(q, q, 1.0 / d, s2, ALU.add, ALU.mult)); sync()
                link(stt(q, q, 1.0, s, ALU.add, ALU.mult)); sync()
                link(ts(s, x, -1.0, 0.0, ALU.mult, ALU.max)); sync()
                link(stt(out, q, 2.0, s, ALU.mult, ALU.add)); sync()

            def conv(cin, acc, out, w, b, done):
                n = PAD3 - 3
                for c in range(C4):
                    link(ts(acc[:, c, 0:n], cin[:, c, 0:n], V(w, c), V(b, c), ALU.mult, ALU.add))
                for j in (1, 2):
                    sync()
                    for c in range(C4):
                        link(stt(acc[:, c, 0:n], cin[:, c, j:j + n], V(w, C4 * j + c), acc[:, c, 0:n], ALU.mult, ALU.add))
                sync()
                for c in range(C4):
                    stt(out[:, c, 0:TP], cin[:, c, 3:3 + TP], V(w, C4 * 3 + c), acc[:, c, 0:TP], ALU.mult,
                        ALU.add).then_inc(S(done), 1)
                    cs, as_ = [x[:, c, 3 + TP:].rearrange("p (b e) -> p b e", b=NS) for x in (cin, acc)]
                    stt(out[:, c, TP:T].rearrange("p (b e) -> p b e", b=NS), cs[:, :, 3:], V(w, C4 * 3 + c),
                        as_[:, :, 0:LS], ALU.mult, ALU.add).then_inc(S(done), 1)

            def conv_pads(cin, st, out):
                link(v.memset(cin[:, :, 0:3], 0.0))
                samples = cin[:, :, 3 + TP:].rearrange("p c (b e) -> p c b e", b=NS)
                link(v.tensor_copy(samples[:, :, :, 0:3], st))
                o = out.rearrange("p (c s e) -> p c s e", c=C4, e=3)
                sync()
                link(v.tensor_copy(o[:, :, 0, :], cin[:, :, TP:TP + 3]))
                link(v.tensor_copy(o[:, :, 1:, :], samples[:, :, :, LS:]))

            def halves(n0, src, hi_name, lo_name):
                for c in range(C4):
                    dve.wait_ge(S(hi_name), c + 1)
                    tt(y_lo[:, n0 + c, :], src[:, c, :], y_hi[:, n0 + c, :].bitcast(F32), ALU.subtract).then_inc(S(lo_name), 1)

            link(stt(a_t[:, 0, :], V("lam", 0, 4), -1.0, V("lam", 0, 4), ALU.mult, ALU.max)); sync()
            v.nop().then_inc(S("A_abs"), 1)
            dve.wait_ge(S("A_exp"), 1)
            softplus_of(V("lam", 0, 4), a_t[:, 1, :], a_t[:, 2, :], a_t[:, 3, :], a_t[:, 5, :], a_t[:, 4, :], 1)
            put(ts(a_t[:, 4, :], a_t[:, 4, :], 4.0, None, ALU.mult), "A_soft", 1)
            upto(dve, "A_conv", 5)
            dve.wait_ge(S("A_in"), 16 * (2 * C4 + 2))
            conv_pads(a_cin, a_st, O("lconv"))
            upto(dve, "A_conv", 3)
            conv(a_cin, a_acc, a_xc, "cw_l", "cb_l", "A_conv")
            dve.wait_ge(S("A_conv"), 2 * C4)
            upto(dve, "A_conv")
            dve.wait_ge(S("A_p"), C4)
            link(ts(a_a, a_r, 1.0, None, ALU.add)); sync()
            upto(dve, "A_conv")
            link(v.reciprocal(a_a, a_a)); sync()
            for c in range(C4):
                was_read(dve, "A_i", c)
            link(tt(a_i, a_i, a_xc, ALU.mult))
            upto(dve, "A_tail", 4)
            dve.wait_ge(S("A_root"), 1)
            link(stt(a_r, a_acc[:, :, 0:T], 2.0, a_a, ALU.mult, ALU.mult)); sync()
            link(v.memset(a_r[:, :, 0:1], 1.0)); sync()
            link(tt(a_i, a_i, a_r, ALU.mult))
            link(ts(a_a, a_a, 2.0, -1.0, ALU.mult, ALU.add)); sync()
            upto(dve, "A_tail", 2)
            a0, i0 = [x[:, :, TP:T].rearrange("p c (b e) -> p c b e", b=NS)[:, :, :, 0] for x in (a_a, a_i)]
            link(tt(a_sm, a0, a_h0, ALU.mult)); sync()
            link(tt(i0, i0, a_sm, ALU.add))
            link(v.memset(a0, 0.0)); sync()
            for c in range(C4):
                link(v.tensor_tensor_scan(a_r[:, c, :], a_a[:, c, :], a_i[:, c, :], 0.0, ALU.mult, ALU.add))
            sync()
            dve.wait_ge(S("A_gelu"), 1)
            o = O("lh").rearrange("p (c s) -> p c s", c=C4)
            link(v.tensor_copy(o[:, :, 0:1], a_r[:, :, TP - 1:TP]))
            link(v.tensor_copy(o[:, :, 1:], a_r[:, :, TP:T].rearrange("p c (b e) -> p c b e", b=NS)[:, :, :, LS - 1]))
            put(tt(a_i, a_r, a_gz, ALU.mult), "A_y", 1)
            upto(dve, "A_tail")
            halves(0, a_i, "y_hi0", "y_lo0")

            full(dve, "B_sum")
            put(stt(b_v, bc(M[0][:, 0:T], 1, C4), -1.0 / MIX, b_v, ALU.mult, ALU.add), *use("B_sum"))
            put(tt(b_q, b_v, b_v, ALU.mult), "B_sq", 1)
            dve.wait_ge(S("B_ws_in"), 32)
            tt(b_ws, b_ws, bc(K("maskD")[:, 0:P], 1, C4), ALU.mult).then_inc(S("B_masked"), 1)
            tt(b_wss, b_wss, bc(K("maskS", 64), 1, C4), ALU.mult).then_inc(S("B_masked"), 1)
            was_read(dve, "B_var")
            link(v.reciprocal(b_std, b_std)); sync()
            link(tt(b_v, b_v, bc(b_std, 1, C4), ALU.mult)); sync()
            for c in range(C4):
                ts(b_v[:, c, :], b_v[:, c, :], V("ln_g", c), V("ln_b", c), ALU.mult, ALU.add).then_inc(S("B_v"), 1)
            dve.wait_ge(S("B_gelu_u"), 1)
            for c in range(C4):
                full(dve, "B_s", c)
                tt(b_q[:, c, :], M[c][:, 0:T], b_u[:, c, :], ALU.mult).then_inc(read("B_s", c), 1)
            for c in range(C4):
                was_read(dve, "B_s", c)
            halves(4, b_q, "y_hi1", "y_lo1")

            dve.wait_ge(S("D_rows_in"), 80)
            ri, rf, r2, r3, r4, r5, r6 = [d_rows[:, i, :] for i in range(7)]
            keep = d_rc[:, ROWC["keep"][0]:ROWC["keep"][0] + T]
            drop = d_rc[:, ROWC["drop"][0]:ROWC["drop"][0] + T]

            def ends(row):
                return row[:, TP:T].rearrange("p (b e) -> p b e", b=NS)[:, :, LS - 1]

            def starts(row):
                return row[:, TP:T].rearrange("p (b e) -> p b e", b=NS)[:, :, 0]

            link(ts(ri, ri, V("bi", parts=4), None, ALU.add))
            link(ts(rf, rf, V("bf", parts=4), None, ALU.add)); sync()
            put(stt(r3, rf, -1.0, rf, ALU.mult, ALU.max), "D_abs", 1)
            upto(dve, "D_rows", 4)
            dve.wait_ge(S("D_exp"), 1)
            softplus_of(rf, r4, r2, r3, r5, r6, 1)
            upto(dve, "D_rows", 2)
            link(ts(r6, r6, -1.0, None, ALU.mult)); sync()
            link(v.tensor_tensor_scan(r2, keep, r6, 0.0, ALU.mult, ALU.add)); sync()
            link(tt(rf, ri, r2, ALU.subtract)); sync()
            link(v.tensor_copy(r3, rf)); sync()
            link(tt(r3[:, 0:1], rf[:, 0:1], d_m0[:, 0:1], ALU.max))
            link(tt(starts(r3), starts(rf), d_m0[:, 1:], ALU.max)); sync()
            link(v.tensor_tensor_scan(ri, drop, r3, 0.0, ALU.add, ALU.max)); sync()
            put(tt(r5, r2, ri, ALU.add), "D_bm", 1)
            link(v.tensor_copy(O("m", 4)[:, 0:1], r5[:, TP - 1:TP]))
            link(v.tensor_copy(O("m", 4)[:, 1:], ends(r5))); sync()
            put(tt(r6[:, TP:T].rearrange("p (b e) -> p b e", b=NS), bc(d_m0[:, 1:], 2, LS),
                   ri[:, TP:T].rearrange("p (b e) -> p b e", b=NS), ALU.subtract), "D_bm", 2)
            link(v.tensor_copy(d_mend[:, 0:1], ri[:, TP - 1:TP]))
            link(v.tensor_copy(d_mend[:, 1:], ends(ri))); sync()
            put(tt(d_md, bc(d_mend, 2, 4), bc(K("ident", 4)[:, 0:4], 1, NSEQ), ALU.mult), "D_rows", 1)
            full(dve, "D_turned")
            dve.wait_ge(S("D_ex"), 2)
            link(v.tensor_copy(d_g[:, 0:8], M[0][:, 0:8]))
            link(v.tensor_copy(d_g[0:64, 8:12], M[0][0:64, 8:12]))
            sync()
            put(v.tensor_copy(d_me.rearrange("p a b -> p (a b)"), M[0][:, 16:16 + 4 * NSEQ]), *use("D_turned"))
            g3 = d_g.rearrange("p (t h) -> p t h", t=3)
            tt(d_wp, g3[:, 0:2, :], bc(d_me[:, 0, :], 1, 2), ALU.subtract).then_inc(S("D_warg"), 1)
            link(tt(d_wm, bc(g3[0:64, 2, :], 1, NS), d_me[0:64, 1:, :], ALU.subtract)); sync()
            ts(d_wm, d_wm, 0.0, None, ALU.min).then_inc(S("D_warg"), 1)
            tt(d_dec, d_m0b, d_me[:, 1:, :], ALU.subtract).then_inc(S("D_warg"), 1)
            upto(dve, "D_conv", 8)
            dve.wait_ge(S("D_in"), 16 * (2 * C4 + 1))
            conv_pads(d_cin, d_st, O("mconv"))
            conv(d_cin, d_acc, d_c, "cw_m", "cb_m", "D_conv")
            dve.wait_ge(S("D_conv"), 2 * C4)
            sync()
            upto(dve, "D_conv")
            dve.wait_ge(S("D_wexp"), 3)
            link(tt(d_wm, d_wm, bc(K("seq", 64), 2, 4), ALU.mult)); sync()
            dve.wait_ge(S("D_silu"), 1)
            dve.wait_ge(S("D_osig"), 1)
            dve.wait_ge(S("D_n_in"), 16)
            dve.wait_ge(S("D_v_in"), 16)
            for h in range(4):
                tok = lambda bank: M[bank][:, 0:TP].rearrange("p (t e) -> p t e", t=2)
                if h:
                    dve.wait_ge(S("D_out_done"), h)
                full(dve, "D_ktok", h)
                link(ts(e_ktok[:, 0:2, :], tok(2), float(P) ** -0.5, None, ALU.mult))
                ts(e_ktok[0:64, 2, :], M[2][0:64, TP:TP + P], float(P) ** -0.5, None, ALU.mult).then_inc(read("D_ktok", h), 1)
                full(dve, "D_vtok", h)
                link(v.tensor_copy(e_vtok[:, 0:2, :], tok(3)))
                v.tensor_copy(e_vtok[0:64, 2, :], M[3][0:64, TP:TP + P]).then_inc(read("D_vtok", h), 1)
                full(dve, "D_Mb", h)
                for lo, n, t0, t in ((0, P, 0, 0), (TP, P, P, 1)):
                    w = TP if t == 0 else P
                    ts(e_E[:, lo:lo + w], M[0][:, t0:TP], g3[:, t, h:h + 1], 0.0, ALU.subtract, ALU.max).then_inc(S("D_E"), 1)
                ts(e_E[0:64, 384:448], M[0][0:64, TP:T], g3[0:64, 2, h:h + 1], 0.0, ALU.subtract, ALU.max).then_inc(read("D_Mb", h), 1)
                full(dve, "D_sb", h)
                was_read(dve, "D_q", h)
                put(tt(d_qs, e_q[:, TP:T], M[2][:, 0:64], ALU.mult), *use("D_sb", h))
                qs3, qn3 = [x.rearrange("p (b e) -> p b e", b=NS) for x in (d_qs, d_qn)]
                tt(qn3, qs3, bc(d_n[:, h, :], 2, LS), ALU.mult).then_inc(S("D_qn"), 1)
                dve.wait_ge(S("D_Eexp"), 2 * h + 2)
                link(tt(e_E[:, 0:TP], e_E[:, 0:TP], K("maskD"), ALU.mult))
                link(tt(e_E[:, TP:TP + P], e_E[:, TP:TP + P], K("maskD")[:, 0:P], ALU.mult))
                link(tt(e_E[0:64, 384:448], e_E[0:64, 384:448], K("maskS", 64), ALU.mult)); sync()
                full(dve, "D_qk", h)
                link(tt(e_E[:, 0:384], e_E[:, 0:384], M[3][:, 0:384], ALU.mult))
                was_read(dve, "D_Mb", h)
                tt(e_E[0:64, 384:448], e_E[0:64, 384:448], M[3][0:64, 384:448], ALU.mult).then_inc(read("D_qk", h), 1)
                full(dve, "D_den", h)
                was_read(dve, "D_eb", h)
                link(stt(d_s, M[1][:, 0:T], -1.0, e_em, ALU.mult, ALU.max)); sync()
                put(tt(d_s, d_s, M[1][:, 0:T], ALU.max), *use("D_den", h))
                link(v.reciprocal(d_s, d_s)); sync()
                full(dve, "D_num", h)
                put(tt(d_h, M[0][:, 0:T], d_s, ALU.mult), *use("D_num", h))
                full(dve, "D_mean", h)
                put(stt(d_h, M[2][:, 0:T], -1.0 / P, d_h, ALU.mult, ALU.add), *use("D_mean", h))
                put(tt(d_s, d_h, d_h, ALU.mult), "D_sq", h + 1)
                for t in range(2):
                    ts(d_vm[:, NS + t, :], e_vtok[:, t, :], d_wp[:, t, h:h + 1], None, ALU.mult).then_inc(S("D_vm"), 1)
                tt(d_vm[0:64, 0:NS, :], bc(e_vtok[0:64, 2, :], 1, NS), bc(d_wm[:, :, h], 2, P), ALU.mult).then_inc(S("D_vm"), 1)
                was_read(dve, "D_var", h)
                link(v.reciprocal(d_s, d_s)); sync()
                link(stt(d_h, d_h, V("norm_g", h), d_s, ALU.mult, ALU.mult)); sync()
                link(stt(d_h, d_c[:, h, :], V("skip", h), d_h, ALU.mult, ALU.add)); sync()
                put(tt(d_h, d_h, d_o[:, h, :], ALU.mult), "D_y", h + 1)
                dve.wait_ge(S("D_yhi"), h + 1)
                tt(y_lo[:, 12 + h, :], d_h, y_hi[:, 12 + h, :].bitcast(F32), ALU.subtract).then_inc(S("y_lo3"), 1)
                link(tt(d_C, d_C, bc(d_dec[:, :, h], 2, P), ALU.mult)); sync()
                for i in range(2):
                    full(dve, "D_Cs", h, i)
                    c4 = d_C[:, 4 * i:4 * i + 4, :]
                    tt(c4, c4, M[i][:, :].rearrange("p (a b) -> p a b", a=4), ALU.add).then_inc(read("D_Cs", h, i), 1)
                full(dve, "D_Cp", h)
                v.tensor_copy(e_vtok[:, 0, :], M[2][:, 0:P]).then_inc(S("D_Cp"), 1)
                on = O("n").rearrange("p (h s) -> p h s", h=4)
                link(v.tensor_copy(on[:, h, 0:1], M[2][:, P + NS:P + NS + 1]))
                link(tt(d_n[:, h, :], d_n[:, h, :], d_dec[:, :, h], ALU.mult)); sync()
                tt(on[:, h, 1:], d_n[:, h, :], M[2][:, P:P + NS], ALU.add).then_inc(read("D_Cp", h), 1)

            def seq9(x):
                return x[:, :, 1 + TP:].rearrange("p c (b e) -> p c b e", b=NS)

            def mix_in(zp, d, out, mu, shift_out, parts, heads, name, n):
                so = shift_out
                link(v.tensor_copy(so[:, :, 0:1], zp[:, :, TP:TP + 1]))
                link(v.tensor_copy(so[:, :, 1:], seq9(zp)[:, :, :, LS]))
                dd = d[:, :, 0:PAD1 - 1]
                link(tt(dd, zp[:, :, 0:PAD1 - 1], zp[:, :, 1:PAD1], ALU.subtract)); sync()
                link(tt(dd, dd, bc(mu, 2, PAD1 - 1), ALU.mult)); sync()
                tt(out[:, :, 0:TP], d[:, :, 0:TP], zp[:, :, 1:1 + TP], ALU.add).then_inc(S(name), 1)
                dz = d[:, :, TP + 1:TP + 1 + 9 * NS].rearrange("p c (b e) -> p c b e", b=NS)[:, :, :, 0:LS]
                tt(out[:, :, TP:T].rearrange("p c (b e) -> p c b e", b=NS), dz, seq9(zp)[:, :, :, 1:],
                   ALU.add).then_inc(S(name), 1)
                dve.wait_ge(S(name), n)

            seq_starts = lambda x: x[:, :, TP:T].rearrange("p c (b e) -> p c b e", b=NS)[:, :, :, 0]
            chunk_starts = lambda x: x[:, :, 0:TP].rearrange("p c (b e) -> p c b e", b=4)[:, :, :, 0]
            sh = O("shift").rearrange("p (c s) -> p c s", c=12)
            for x, (dst, mu) in enumerate(((c_r, "mu_r"), (c_k, "mu_k"), (c_v, "mu_v"))):
                upto(dve, "C_low", (6, 3, 0)[x])
                dve.wait_ge(S("C_z_in"), 16 * (8 * (x + 1) + 4))
                if x == 0:
                    dve.wait_ge(S("D_out_done"), 4)
                link(v.memset(c_zp[:, :, 0:1], 0.0))
                if x == 0:
                    dve.wait_ge(S("C_sh_in"), 48)
                link(v.tensor_copy(seq9(c_zp)[:, :, :, 0], c_sh[:, 4 * x:4 * x + 4, :]))
                sync()
                upto(dve, "C_low", (6, 1, 0)[x])
                mix_in(c_zp, c_d, dst, V(mu, 0, 4), sh[:, 4 * x:4 * x + 4, :], P, 4, "C_mixed", 2 * (x + 1))
                if x == 0:
                    upto(dve, "C_low", 5)
                    for zp, out, mu_, st, so, parts in (
                            (c_lowp, c_low, "mu_low", c_shlow, O("shift_low", 64), 64),
                            (c_gdp, c_gd, "mu_gd", c_shgd, O("shift_gd", 96), 96)):
                        upto(dve, "C_low", 4 if parts == 64 else 3)
                        z3, o3 = zp.unsqueeze(1), out.unsqueeze(1)
                        d3 = c_d96[0:parts, :].unsqueeze(1)
                        link(v.memset(z3[:, :, 0:1], 0.0))
                        link(v.tensor_copy(seq9(z3)[:, :, :, 0], st.unsqueeze(1))); sync()
                        mix_in(z3, d3, o3, V(mu_, parts=parts), so.unsqueeze(1), parts, 1, "C_mixed_low",
                               2 * (1 + (parts == 96)))
            vb4 = lambda name: bc(V(name, 0, 4), 2, T)
            upto(dve, "C_kk", 2)
            link(tt(c_kk, c_k, vb4("kk"), ALU.mult)); sync()
            put(tt(c_t, c_kk, c_kk, ALU.mult), "C_kk_sq", 1)
            for h in range(4):
                was_read(dve, "C_lora", 1, h)
                was_read(dve, "C_kk_sum", h)
            link(ts(c_rk, c_rk, 1e-12, None, ALU.max)); sync()
            link(v.reciprocal(c_rk, c_rk)); sync()
            link(tt(c_kk, c_kk, c_rk, ALU.mult)); sync()
            link(stt(c_t, c_a, -1.0, vb4("ka"), ALU.add, ALU.mult)); sync()
            link(stt(c_k, c_t, 1.0, c_k, ALU.add, ALU.mult)); sync()
            upto(dve, "C_rk", 3)
            link(tt(c_rk, c_r, c_k, ALU.mult)); sync()
            put(tt(c_rk, c_rk, vb4("rk"), ALU.mult), "C_rk", 1)
            upto(dve, "C_scaled", 6)
            dve.wait_ge(S("C_decay"), 1)
            link(v.memset(c_t, 0.0)); sync()
            for sel in (seq_starts, chunk_starts):
                link(v.tensor_copy(sel(c_t), sel(c_w)))
            sync()
            for sel in (seq_starts, chunk_starts):
                link(v.memset(sel(c_w), 0.0))
            sync()
            for h in range(4):
                link(v.tensor_tensor_scan(c_t[:, h, :], c_w[:, h, :], c_t[:, h, :], 0.0, ALU.mult, ALU.add))
            sync()
            upto(dve, "C_scaled", 4)
            link(stt(c_w[:, :, 1:T], c_kk[:, :, 1:T], -1.0, c_t[:, :, 0:T - 1], ALU.mult, ALU.mult)); sync()
            for sel in (seq_starts, chunk_starts):
                link(ts(sel(c_w), sel(c_kk), -1.0, None, ALU.mult))
            sync()
            upto(dve, "C_scaled", 3)
            link(tt(c_kk, c_kk, c_a, ALU.mult)); sync()
            link(v.reciprocal(c_a, c_t)); sync()
            upto(dve, "C_scaled", 1)
            link(tt(c_kk, c_kk, c_a, ALU.mult))
            link(tt(c_k, c_k, c_a, ALU.mult))
            link(tt(c_r, c_r, c_t, ALU.mult))
            link(v.tensor_copy(c_wend[:, :, 0:4], c_t[:, :, 0:TP].rearrange("p c (b e) -> p c b e", b=4)[:, :, :, 63]))
            link(v.tensor_copy(c_wend[:, :, 4:], c_t[:, :, TP:T].rearrange("p c (b e) -> p c b e", b=NS)[:, :, :, LS - 1]))
            for h in range(4):
                full(dve, "C_rk_sum", h)
                tt(c_rk[:, h, :], M[h][:, 0:T], c_v[:, h, :], ALU.mult).then_inc(read("C_rk_sum", h), 1)
            for h in range(4):
                was_read(dve, "C_rk_sum", h)
            sync()
            v.nop().then_inc(S("C_scaled"), 1)
            link(v.memset(c_S, 0.0)); sync()
            v.nop().then_inc(S("C_S_ready"), 1)
            for ch in range(5):
                n = ch
                smp = ch == 4
                bank = lambda i: M[i][:, 0:256].rearrange("p (h e) -> p h e", h=4)

                def masked(dst, i, mask, name):
                    full(dve, name, n)
                    put(tt(dst, bank(i), bc(K(mask), 1, 4), ALU.mult), *use(name, n))

                def copied(dst, i, *key):
                    full(dve, *key)
                    put(v.tensor_copy(dst, bank(i)), *use(*key))

                def added(dst, i, *key):
                    full(dve, *key)
                    put(tt(dst, dst, bank(i), ALU.add), *use(*key))

                near = "n_seq" if smp else "n_near"
                full(dve, "C_N", n)
                if not smp:
                    link(tt(h_F, bank(0), bc(K("n_far"), 1, 4), ALU.mult)); sync()
                masked(h_N, 0, near, "C_N")
                masked(h_Q, 1, "nT_seq" if smp else "nT_near", "C_NT")
                masked(h_ak, 2, "nT_seq" if smp else "sT", "C_ak")
                masked(h_rb, 3, "maskS" if smp else "iT", "C_rb")
                masked(h_rk, 0, "maskS" if smp else "iT", "C_rk")
                copied(h_btok, 1, "C_btok", n)
                copied(h_ktok, 2, "C_ktok", n)
                copied(h_vtok, 3, "C_vtok", n)
                put(tt(h_T, h_Q, bc(K("ident2"), 1, 4), ALU.add), "C_QI", n + 1)
                copied(h_P2, 0, "C_p2", n)
                copied(h_Q2, 1, "C_q2", n)
                added(h_T, 2, "C_t2", n)
                full(dve, "C_q4", n)
                copied(h_P2, 0, "C_p4", n)
                copied(h_Q2, 1, "C_q4", n)
                added(h_T, 2, "C_t4", n)
                if not smp:
                    copied(h_P2, 0, "C_p8", n)
                    added(h_T, 2, "C_t8", n)
                    copied(h_P2, 0, "C_zT", n)
                    copied(h_Q2, 1, "C_z", n)
                    put(tt(h_E, h_P2, bc(K("ident2"), 1, 4), ALU.add), "C_E", n + 1)
                    copied(h_N, 2, "C_z2", n)
                    added(h_E, 0, "C_e", n)
                    copied(h_P2, 3, "C_rhs", n)
                    copied(h_Q2, 1, "C_y", n)
                    copied(h_F, 2, "C_u", n)
                else:
                    copied(h_N, 0, "C_u0", n)
                    copied(h_P2, 3, "C_rhs", n)
                    copied(h_F, 1, "C_y", n)
                copied(c_t[:, :, 64 * ch:64 * ch + 64], 3, "C_o", n)
                if not smp:
                    added(c_S, 0, "C_S", n)
                    put(tt(c_S, c_S, bc(c_wend[:, :, ch], 2, 64), ALU.mult), "C_S_ready", n + 2)
                else:
                    for h in range(4):
                        if h:
                            full(dve, "C_Ss", h - 1)
                        for x, src in ((0, h_F), (1, h_vtok)):
                            um = c_um[:, x, :].rearrange("p (b e) -> p b e", b=NS)
                            tt(um, bc(src[:, h, :], 1, NS), bc(K("seq"), 2, HD), ALU.mult).then_inc(S("C_um"), 1)
                        full(dve, "C_Ss", h)
                        put(tt(c_Ss[:, h, :, :], c_Ss[:, h, :, :], M[h % 2][:, :].rearrange("p (b e) -> p b e", b=NS),
                               ALU.add), *use("C_Ss", h))
                        tt(c_Ss[:, h, :, :], c_Ss[:, h, :, :], bc(c_wend[:, h, 4:], 2, HD), ALU.mult).then_inc(S("C_Ss_made"), 1)
                    dve.wait_ge(S("C_Ss_made"), 4)
            for h in range(4):
                full(dve, "C_mean", h)
                stt(c_t[:, h, :], M[h][:, 0:T], -1.0 / HD, c_t[:, h, :], ALU.mult, ALU.add).then_inc(read("C_mean", h), 1)
            for h in range(4):
                was_read(dve, "C_mean", h)
            put(tt(c_k, c_t, c_t, ALU.mult), "C_osq", 1)
            for h in range(4):
                was_read(dve, "C_var", h)
            upto(dve, "end", 6)
            link(v.reciprocal(c_k, c_k)); sync()
            link(tt(c_t, c_t, c_k, ALU.mult)); sync()
            link(tt(c_t, c_t, vb4("rln_g"), ALU.mult)); sync()
            upto(dve, "end", 3)
            link(tt(c_t, c_t, vb4("rln_b"), ALU.add)); sync()
            link(tt(c_t, c_t, c_rk, ALU.add)); sync()
            upto(dve, "end")
            for h in range(4):
                full(dve, "C_gate", h)
                tt(c_t[:, h, :], M[h][:, 0:T], c_t[:, h, :], ALU.mult).then_inc(read("C_gate", h), 1)
            for h in range(4):
                was_read(dve, "C_gate", h)
            halves(8, c_t, "y_hi2", "y_lo2")
            sync()
            v.nop().then_inc(S("small_done"), 1)

        block = ctx.enter_context(nc.Block())

        use_pass = [len(range(b, NF, 4)) for b in range(4)]
        use_out = [u + KD for u in use_pass]
        use_ff = [[use_out[0] + 8 + 15 * h, use_out[1] + 8 + 15 * h, use_out[2] + 15 * h, use_out[3] + 15 * h]
                  for h in range(2)]
        use_ffo = [[u + 11 for u in use_ff[h]] for h in range(2)]
        LEAD = 16
        END_MORE = 8

        def phases():
            yield "front", 0, NF // 2, [8, 8, 8, 8]
            yield "pass", PASS0, KD // 2, [8, 8, 8, 8]
            yield "out", OUT0, KD // 2, [8, 8, 8, 8]
            for h in range(2):
                yield f"in{h}", FF0 + h * (FFIN + FFOUT), HALF // 2, [8] * 8
                yield f"ff{h}", FF0 + h * (FFIN + FFOUT) + FFIN, 4, OUT_TILES * 4

        tiles_of = {}
        for _, base, turns, pat in phases():
            for q in range(turns * len(pat)):
                tiles_of[base + q] = pat[q % len(pat)]
        assert len(tiles_of) == NPIECES

        @block.sync
        def _(sp):
            def load(p, q, src):
                sp.wait_ge(S("w_lo_made"), p + 1)
                sp.dma_start(w_raw[:, q % RING, 0:src.shape[1]], src).then_inc(S(f"w_raw_in{q % RING}"), 16)

            def one(ap):
                return ap.rearrange("a p n -> (a p) n")

            sp.dma_start(vec[:, :], a["vec"]).then_inc(S("vec_in"), 16)
            for h in range(2):
                sp.dma_start(xin[:, 8 * h:8 * h + 8, :], a["x"][:, 8 * h:8 * h + 8, :]).then_inc(S(f"x_in{h}"), 16)
            with sp.Fori(0, NF // 2) as i:
                for q in range(4):
                    load(i * 4 + q, q, one(a["w_f"][bass.ds(i * 2 + q // 2, 1), :, (q % 2) * 1024:(q % 2) * 1024 + 1024]))
            with sp.Fori(0, KD // 2) as i:
                for q in range(4):
                    load(i * 4 + (PASS0 + q), q,
                         one(a["w_br"][bass.ds(i * 2 + q // 2, 1), :, (q % 2) * 1024:(q % 2) * 1024 + 1024]))
                for b in range(4):
                    sp.wait_ge(S(f"ev_out{b}"), 16 * (use_pass[b] + 1))
                sp.wait_ge(S("y_lo2"), C4)
                for j in range(2):
                    sp.wait_ge(S("g_used"), i * 2 + (j + 1))
                    sp.dma_start(g_in[:, j, :, :], zD[bass.ds(i * 8 + (NZ + 4 * j), 4), :, :].rearrange("b p t -> p b t")
                                 ).then_inc(S(f"g_in{j}"), 16)
            with sp.Fori(0, KD // 2) as i:
                for q in range(4):
                    load(i * 4 + (OUT0 + q), q, one(a["w_o"][bass.ds(i * 2 + q // 2, 1), :, (q % 2) * 1024:(q % 2) * 1024 + 1024]))
            for h in range(2):
                with sp.Fori(0, HALF // 2) as i:
                    for q in range(8):
                        load(i * 8 + (FF0 + h * (FFIN + FFOUT) + q), q,
                             one(a["w_fi"][bass.ds(i * 4 + (h * HALF * 2 + q // 2), 1), :, (q % 2) * 1024:(q % 2) * 1024 + 1024]))
                with sp.Fori(0, 4) as i:
                    for q in range(12):
                        c0 = sum(OUT_TILES[:q % 3]) * P
                        load(i * 12 + (FF0 + h * (FFIN + FFOUT) + FFIN + q), q,
                             one(a["w_fo"][bass.ds(i * 4 + (h * KD + q // 3), 1), :, c0:c0 + OUT_TILES[q % 3] * P]))

        @block.gpsimd
        def _(pool):
            nc.gpsimd.nop().then_inc(S("w_lo_made"), RING)
            for name, base, turns, pat in phases():
                with pool.Fori(0, turns) as i:
                    for q, tiles in enumerate(pat):
                        n = tiles * P
                        pool.wait_ge(S("w_hi_made"), i * len(pat) + (base + q + 1))
                        nc.gpsimd.tensor_tensor(w_lo[:, q % RING, 0:n], w_raw[:, q % RING, 0:n],
                                                w_hi[:, q % RING, 0:n].bitcast(F32), ALU.subtract).then_inc(S("w_lo_made"), 1)

        @block.tensor
        def _(pe):
            nc.tensor.nop().then_inc(S("w_used"), RING)
            for b in range(4):
                nc.tensor.nop().then_inc(S(f"evac{b}"), 1)

            def products(p, q, b, tiles, hi, lo, k0, first, last, halves_made=None):
                pe.wait_ge(S("w_lo_made"), p + (RING + 1))
                for k in range(tiles):
                    if halves_made:
                        pe.wait_ge(S(halves_made), k0 + k + 1)
                    wh = w_hi[:, q % RING, k * P:(k + 1) * P]
                    wl = w_lo[:, q % RING, k * P:(k + 1) * P]
                    out = G[b][:, 0:T]
                    pe.matmul(out, wh, hi[:, k0 + k, :], start=first and k == 0, stop=False)
                    pe.matmul(out, wh, lo[:, k0 + k, :], start=False, stop=False)
                    mm = pe.matmul(out, wl, hi[:, k0 + k, :], start=False, stop=last and k == tiles - 1)
                mm.then_inc(S("w_used"), 1)

            def block_of(use, b, parts):
                pe.wait_ge(S(f"evac{b}"), use + 1)
                for n, (p, q, tiles, hi, lo, k0, *made) in enumerate(parts):
                    products(p, q, b, tiles, hi, lo, k0, n == 0, n == len(parts) - 1, *made)

            def sum_squares(ready):
                pe.wait_ge(S(ready), 1)
                pe.matmul(M[0][:, 0:T], K("ones"), ssum if ready == "x_ss" else ssum2[:, :], start=True,
                          stop=True).then_inc(S(ready + "_all"), 1)

            pe.wait_ge(S("con_in"), 16)
            def front_block(use, b, p, halves=(0, 1), halves_made=None):
                for half in halves:
                    if half == 0:
                        pe.wait_ge(S(f"evac{b}"), use + 1)
                    products(p + half, 2 * b + half, b, 8, x_hi, x_lo, 8 * half, half == 0, half == 1,
                             halves_made)

            def front_turns(p0, turns):
                with pe.Fori(0, turns) as i:
                    for j in range(4):
                        block, b = p0 // 2 + j, (p0 // 2 + j) % 4
                        front_block(i + block // 4, b, i * 8 + (p0 + 2 * j))

            for b in range(4):
                front_block(0, b, 2 * b, halves_made="x_lo_made" if b == 0 else None)
                if b == 1:
                    sum_squares("x_ss")
            front_turns(8, LEAD // 8 - 1)
            front_done = [LEAD]

            def pieces(n):
                for p in range(front_done[0], min(front_done[0] + n, NFRONT)):
                    front_block(p // 8, p // 2 % 4, p - p % 2, (p % 2,))
                    front_done[0] = p + 1
                return front_done[0]

            mixers_pe(pe, pieces)
            at["end"] = pieces(END_MORE + (NFRONT - END_MORE - pieces(0)) % 8)
            if at["end"] < NFRONT:
                front_turns(at["end"], (NFRONT - at["end"]) // 8)
            for br in range(4):
                pe.wait_ge(S(f"y_lo{br}"), C4)
            with pe.Fori(0, KD // 2) as i:
                for j in range(2):
                    for half in range(2):
                        q = 2 * j + half
                        pe.wait_ge(S("w_lo_made"), i * 4 + (PASS0 + q + RING + 1))
                        for b in (2 * half, 2 * half + 1):
                            pe.wait_ge(S(f"evac{b}"), i * 2 + (use_pass[b] + j + 1))
                            for k in range(4):
                                c = (4 * (b % 2) + k) * P
                                wh, wl = w_hi[:, q, c:c + P], w_lo[:, q, c:c + P]
                                out, y = G[b][:, 0:T], 4 * b + k
                                pe.matmul(out, wh, y_hi[:, y, :], start=k == 0, stop=False)
                                pe.matmul(out, wh, y_lo[:, y, :], start=False, stop=False)
                                mm = pe.matmul(out, wl, y_hi[:, y, :], start=False, stop=k == 3)
                        mm.then_inc(S("w_used"), 1)
            pe.wait_ge(S("m_lo_made"), KD)
            with pe.Fori(0, KD // 2) as i:
                for j in range(2):
                    p = i * 4 + (OUT0 + 2 * j)
                    block_of(i + use_out[j], j, [(p, 2 * j, 8, x_hi, x_lo, 0), (p + 1, 2 * j + 1, 8, x_hi, x_lo, 8)])
            sum_squares("mix_ss")
            for h in range(2):
                base = FF0 + h * (FFIN + FFOUT)
                if h == 0:
                    for b in range(4):
                        p, made = base + 2 * b, ("x2_lo_made" if b == 0 else None,)
                        block_of(use_ff[h][b], b, [(p, 2 * b, 8, x_hi, x_lo, 0) + made,
                                                   (p + 1, 2 * b + 1, 8, x_hi, x_lo, 8) + made])
                        if b == 1:
                            sum_squares("x2_ss")
                with pe.Fori(1 - h, HALF // 2) as i:
                    for b in range(4):
                        p = i * 8 + (base + 2 * b)
                        block_of(i + use_ff[h][b], b, [(p, 2 * b, 8, x_hi, x_lo, 0), (p + 1, 2 * b + 1, 8, x_hi, x_lo, 8)])
                pe.wait_ge(S("a_lo_made"), HALF * (h + 1))
                base += FFIN
                with pe.Fori(0, 4) as i:
                    for b in range(4):
                        p = i * 12 + (base + 3 * b)
                        block_of(i + use_ffo[h][b], b, [(p + t, 3 * b + t, OUT_TILES[t], a_hi, a_lo, 8 * t) for t in range(3)])
            sum_squares("ff_ss")

        @block.scalar
        def _(act):
            split_early = (AHEAD, AHEAD + 1, AHEAD + 2, FF0 + AHEAD)

            def run(base, turns, pat, tasks):
                n = len(pat)

                def turn(i, last):
                    for q in range(n):
                        ahead = q + AHEAD
                        if last:
                            p = base + (turns - 1) * n + ahead
                            if p < NPIECES:
                                split_at(p, ahead, tiles_of[p], None, None)
                        else:
                            split_at(base + ahead, ahead, pat[ahead % n], i, n)
                        if q in tasks:
                            tasks[q](i)

                def split_at(p0, q, tiles, i, n):
                    if i is None and p0 in split_early:
                        return
                    slot = q % RING
                    raw = 16 * (p0 // RING + 1)
                    act.wait_ge(S(f"w_raw_in{slot}"), raw if i is None else i * (16 * n // RING) + raw)
                    act.wait_ge(S("w_used"), p0 + 1 if i is None else i * n + (p0 + 1))
                    nc.scalar.activation(w_hi[:, slot, 0:tiles * P], w_raw[:, slot, 0:tiles * P],
                                         ACT.Copy).then_inc(S("w_hi_made"), 1)

                peeled = base in (0, FF0)
                if peeled:
                    for q in range(n):
                        split_at(base + q + AHEAD, q + AHEAD, pat[(q + AHEAD) % n], None, None)
                        if q in tasks:
                            tasks[q](0)
                if turns > 1 + peeled:
                    with act.Fori(int(peeled), turns - 1) as i:
                        turn(i, False)
                turn(turns - 1, True)

            def root(src, dst, name, wait):
                act.wait_ge(S(wait), 1)
                nc.scalar.activation(dst, src, ACT.Sqrt, scale=1.0 / D, bias=V("eps6")).then_inc(S(name), 1)

            act.dma_start(con[:, :], a["con"]).then_inc(S("con_in"), 16)
            act.wait_ge(S("vec_in"), 16)

            def first_split(p):
                act.wait_ge(S(f"w_raw_in{p}"), 16)
                act.wait_ge(S("w_used"), p + 1)
                nc.scalar.activation(w_hi[:, p, :], w_raw[:, p, :], ACT.Copy).then_inc(S("w_hi_made"), 1)

            for k in range(KD):
                act.wait_ge(S(f"x_in{k // 8}"), 16)
                nc.scalar.activation(x_hi[:, k, :], xin[:, k, :], ACT.Copy, scale=V("g_pre", k)).then_inc(S("x_hi_made"), 1)
                if k in (3, 7):
                    first_split(k // 4)
            nc.scalar.activation(xsq[:, :, :], xin[:, :, :], ACT.Square).then_inc(S("x_sq"), 1)
            first_split(2)
            for p in range(AHEAD, 6):
                act.wait_ge(S(f"w_raw_in{p % RING}"), 16 * (p // RING + 1))
                act.wait_ge(S("w_used"), p + 1)
                nc.scalar.activation(w_hi[:, p % RING, :], w_raw[:, p % RING, :], ACT.Copy).then_inc(S("w_hi_made"), 1)
            root(M[0][:, 0:T], rstd[:, :], "x_std", "x_ss_all")

            def front_out(use, b, row, gates):
                act.wait_ge(S(f"evac{b}"), use + 2)
                if gates:
                    nc.scalar.activation(ev[:, b, :], ev[:, b, :], ACT.Sigmoid).then_inc(S(f"gate{b}"), 1)
                    act.wait_ge(S(f"gate{b}"), use + (1 - len(range(b, NZ, 4))))
                act.dma_start(zD[row].rearrange("a p n -> (a p) n"), ev[:, b, :]).then_inc(S(f"ev_out{b}"), 16)

            def front_turns(p0, turns, gates):
                def task(j):
                    block = p0 // 2 + j
                    return lambda i: front_out(i + block // 4, block % 4,
                                               slice(4 * i + block, 4 * i + block + 1) if isinstance(i, int)
                                               else bass.ds(i * 4 + block, 1), gates)
                run(p0, turns, [8] * 8, {2 * j + 1: task(j) for j in range(4)})

            for b in range(4):
                nc.scalar.nop().then_inc(S(f"ev_out{b}"), 16)
            front_turns(0, LEAD // 8, False)
            front_done = [LEAD]

            def front_act(level):
                for p in range(front_done[0], level):
                    q = p + AHEAD
                    act.wait_ge(S(f"w_raw_in{q % RING}"), 16 * (q // RING + 1))
                    act.wait_ge(S("w_used"), q + 1)
                    nc.scalar.activation(w_hi[:, q % RING, :], w_raw[:, q % RING, :], ACT.Copy).then_inc(S("w_hi_made"), 1)
                    if p % 2:
                        block = p // 2
                        front_out(block // 4, block % 4, slice(block, block + 1), block >= NZ)
                front_done[0] = max(front_done[0], level)

            part[act] = front_act
            mixers_act(act)
            front_act(at["end"])
            if at["end"] < NFRONT:
                front_turns(at["end"], (NFRONT - at["end"]) // 8, True)

            def high_merged(j):
                def task(i):
                    act.wait_ge(S("g_sum"), i * 6 + (3 * j + 3))
                    row = bass.ds(i * 2 + j, 1) if not isinstance(i, int) else slice(i * 2 + j, i * 2 + j + 1)
                    nc.scalar.activation(x_hi[:, row, :], g_t[:, 0:1, :], ACT.Copy).then_inc(S("m_hi_made"), 1)
                return task
            run(PASS0, KD // 2, [8] * 4, {1: high_merged(0), 3: high_merged(1)})
            act.wait_ge(S("m_lo_made"), KD)
            act.wait_ge(S("C_out"), 32)
            act.dma_start(xres[:, :, :], a["x"]).then_inc(S("x_again"), 16)
            run(OUT0, KD // 2, [8] * 4, {})
            root(M[0][:, 0:T], rstd[:, :], "mix_std", "mix_ss_all")
            for k in range(KD):
                act.wait_ge(S("x2_made"), k + 1)
                nc.scalar.activation(x_hi[:, k, :], xres[:, k, :], ACT.Copy, scale=V("g_pre2", k)).then_inc(S("x2_hi_made"), 1)
            nc.scalar.activation(mix[:, :, :], xres[:, :, :], ACT.Square).then_inc(S("x2_sq"), 1)
            early = FF0 + AHEAD
            act.wait_ge(S(f"w_raw_in{early % RING}"), 16 * (early // RING + 1))
            act.wait_ge(S("w_used"), early + 1)
            nc.scalar.activation(w_hi[:, early % RING, :], w_raw[:, early % RING, :], ACT.Copy).then_inc(S("w_hi_made"), 1)
            root(M[0][:, 0:T], rstd[:, :], "x2_std", "x2_ss_all")
            for h in range(2):
                def silu(j):
                    def task(i):
                        act.wait_ge(S(f"evac{2 * j}"), i + (use_ff[h][2 * j] + 2))
                        nc.scalar.activation(gate[:, j, :], gate[:, j, :], ACT.Silu).then_inc(S("silu_made"), 1)
                    return task

                def high(j):
                    def task(i):
                        act.wait_ge(S("a_made"), i * 2 + (h * HALF + j + 1))
                        row = bass.ds(i * 2 + j, 1) if not isinstance(i, int) else slice(i * 2 + j, i * 2 + j + 1)
                        nc.scalar.activation(a_hi[:, row, :], term[:, j:j + 1, :], ACT.Copy).then_inc(S("a_hi_made"), 1)
                    return task
                base = FF0 + h * (FFIN + FFOUT)
                run(base, HALF // 2, [8] * 8, {1: silu(0), 3: high(0), 5: silu(1), 7: high(1)})
                run(base + FFIN, 4, OUT_TILES * 4, {})
            root(M[0][:, 0:T], rstd[:, :], "ff_std", "ff_ss_all")
            for k in range(4):
                act.wait_ge(S("y_made"), 4 * k + 4)
                act.dma_start(a["y"][:, 4 * k:4 * k + 4, :], xres[:, 4 * k:4 * k + 4, :]).then_inc(S("y_out"), 16)
            act.wait_ge(S("small_done"), 1)
            act.dma_start(a["small"], small[:, :]).then_inc(S("small_out"), 16)
            act.wait_ge(S("small_out"), 16)
            act.wait_ge(S("y_out"), 64)

        @block.vector
        def _(dve):
            count = [0]

            def link(ins):
                count[0] += 1
                ins.then_inc(S("dve_order"), 1)

            def sync():
                dve.wait_ge(S("dve_order"), count[0])

            v = nc.vector

            def multiplied(p):
                dve.wait_ge(S("w_used"), p + (RING + 1))

            def flip(std, made):
                dve.wait_ge(S(std), 1)
                v.reciprocal(rstd[:, :], rstd[:, :]).then_inc(S(made), 1)
                dve.wait_ge(S(made), 1)

            link(v.memset(small[:, :], 0.0))
            for k in range(KD):
                dve.wait_ge(S("x_hi_made"), k + 1)
                v.scalar_tensor_tensor(x_lo[:, k, :], xin[:, k, :], V("g_pre", k), x_hi[:, k, :].bitcast(F32),
                                       ALU.mult, ALU.subtract).then_inc(S("x_lo_made"), 1)
            dve.wait_ge(S("x_sq"), 1)
            v.tensor_reduce(ssum, xsq.rearrange("p k t -> p t k"), AX.X, ALU.add).then_inc(S("x_ss"), 1)
            flip("x_std", "x_rstd")

            def front_evac(use, b, p):
                multiplied(p)
                dve.wait_ge(S(f"ev_out{b}"), use * 16 + 16)
                v.tensor_tensor(ev[:, b, :], G[b][:, 0:T], rstd[:, :], ALU.mult).then_inc(S(f"evac{b}"), 1)

            def front_turns(p0, turns):
                with dve.Fori(0, turns) as i:
                    for j in range(4):
                        block = p0 // 2 + j
                        front_evac(i + block // 4, block % 4, i * 8 + (p0 + 2 * j + 1))

            front_turns(0, LEAD // 8)
            front_done = [LEAD]

            def front_dve(level):
                for p in range(front_done[0], level):
                    if p % 2:
                        front_evac(p // 8, p // 2 % 4, p)
                front_done[0] = max(front_done[0], level)

            part[dve] = front_dve
            mixers_dve(dve, link, sync)
            front_dve(at["end"])
            if at["end"] < NFRONT:
                front_turns(at["end"], (NFRONT - at["end"]) // 8)

            v.nop().then_inc(S("g_used"), 2)
            with dve.Fori(0, KD // 2) as i:
                for j in range(2):
                    dve.wait_ge(S(f"g_in{j}"), i * 16 + 16)
                    for b in range(4):
                        if b % 2 == 0:
                            multiplied(i * 4 + (PASS0 + 2 * j + b // 2))
                        v.tensor_tensor(g_t[:, b, :], G[b][:, 0:T], g_in[:, j, b, :], ALU.mult).then_inc(S(f"evac{b}"), 1)
                    for n, (x, y) in enumerate(((0, 1), (2, 3), (0, 2))):
                        if n < 2:
                            for b in (x, y):
                                dve.wait_ge(S(f"evac{b}"), i * 2 + (use_pass[b] + j + 2))
                        else:
                            dve.wait_ge(S("g_sum"), i * 6 + (3 * j + 2))
                        v.tensor_tensor(g_t[:, x, :], g_t[:, x, :], g_t[:, y, :], ALU.add).then_inc(S("g_sum"), 1)
                    v.nop().then_inc(S("g_used"), 1)
                    row = bass.ds(i * 2 + j, 1)
                    dve.wait_ge(S("m_hi_made"), i * 2 + (j + 1))
                    v.tensor_tensor(x_lo[:, row, :], g_t[:, 0:1, :], x_hi[:, row, :].bitcast(F32),
                                    ALU.subtract).then_inc(S("m_lo_made"), 1)
                    dve.wait_ge(S("m_lo_made"), i * 2 + (j + 1))

            def square(n, src, made, added):
                v.tensor_tensor(term[:, 0:1, :], src, src, ALU.mult).then_inc(S(made), 1)
                dve.wait_ge(S(made), n + 1)
                dve.wait_ge(S(added), n + 1)
                v.tensor_tensor(ssum2[:, :], ssum2[:, :], term[:, 0, :], ALU.add).then_inc(S(added), 1)

            v.memset(ssum2[:, :], 0.0).then_inc(S("mix_added"), 1)
            with dve.Fori(0, KD // 2) as i:
                for j in range(2):
                    row = mix[:, bass.ds(i * 2 + j, 1), :]
                    multiplied(i * 4 + (OUT0 + 2 * j + 1))
                    v.tensor_copy(row, G[j][:, 0:T].unsqueeze(1)).then_inc(S(f"evac{j}"), 1)
                    dve.wait_ge(S(f"evac{j}"), i + (use_out[j] + 2))
                    square(i * 2 + j, row, "mix_sq", "mix_added")
            dve.wait_ge(S("mix_added"), KD + 1)
            v.nop().then_inc(S("mix_ss"), 1)
            flip("mix_std", "mix_rstd")
            dve.wait_ge(S("x_again"), 16)
            for k in range(KD + 2):
                if k < KD:
                    link(v.scalar_tensor_tensor(mix[:, k, :], mix[:, k, :], V("g_post", k), rstd[:, :], ALU.mult, ALU.mult))
                if k > 1:
                    dve.wait_ge(S("x2_hi_made"), k - 1)
                    v.scalar_tensor_tensor(x_lo[:, k - 2, :], xres[:, k - 2, :], V("g_pre2", k - 2),
                                           x_hi[:, k - 2, :].bitcast(F32), ALU.mult, ALU.subtract).then_inc(S("x2_lo_made"), 1)
                if k < KD:
                    sync()
                    v.tensor_tensor(xres[:, k, :], xres[:, k, :], mix[:, k, :], ALU.add).then_inc(S("x2_made"), 1)
            dve.wait_ge(S("x2_sq"), 1)
            v.tensor_reduce(ssum2[:, :], mix[:, :, :].rearrange("p k t -> p t k"), AX.X, ALU.add).then_inc(S("x2_ss"), 1)
            flip("x2_std", "x2_rstd")
            v.memset(mix[:, :, :], 0.0).then_inc(S("ff_sum"), 1)
            v.memset(ssum2[:, :], 0.0).then_inc(S("ff_added"), 1)
            for h in range(2):
                base = FF0 + h * (FFIN + FFOUT)
                with dve.Fori(0, HALF // 2) as i:
                    for j in range(2):
                        uu = i + use_ff[h][2 * j + 1]
                        pair = i * 2 + (h * HALF + j)
                        multiplied(i * 8 + (base + 4 * j + 1))
                        v.tensor_tensor(gate[:, j, :], G[2 * j][:, 0:T], rstd[:, :], ALU.mult).then_inc(S(f"evac{2 * j}"), 1)
                        multiplied(i * 8 + (base + 4 * j + 3))
                        v.tensor_tensor(term[:, j, :], G[2 * j + 1][:, 0:T], rstd[:, :], ALU.mult).then_inc(S(f"evac{2 * j + 1}"), 1)
                        dve.wait_ge(S(f"evac{2 * j + 1}"), uu + 2)
                        dve.wait_ge(S("silu_made"), pair + 1)
                        v.tensor_tensor(term[:, j, :], term[:, j, :], gate[:, j, :], ALU.mult).then_inc(S("a_made"), 1)
                        dve.wait_ge(S("a_hi_made"), pair + 1)
                        row = bass.ds(i * 2 + j, 1)
                        v.tensor_tensor(a_lo[:, row, :], term[:, j:j + 1, :], a_hi[:, row, :].bitcast(F32),
                                        ALU.subtract).then_inc(S("a_lo_made"), 1)
                with dve.Fori(0, 4) as i:
                    for b in range(4):
                        row = mix[:, bass.ds(i * 4 + b, 1), :]
                        multiplied(i * 12 + (base + FFIN + 3 * b + 2))
                        dve.wait_ge(S("ff_sum"), 1)
                        v.tensor_tensor(row, row, G[b][:, 0:T].unsqueeze(1), ALU.add).then_inc(S(f"evac{b}"), 1)
                        if h == 1:
                            dve.wait_ge(S(f"evac{b}"), i + (use_ffo[h][b] + 2))
                            square(i * 4 + b, row, "ff_sq", "ff_added")
                if h == 0:
                    for b in range(4):
                        dve.wait_ge(S(f"evac{b}"), use_ffo[h][b] + 5)
            dve.wait_ge(S("ff_added"), KD + 1)
            v.nop().then_inc(S("ff_ss"), 1)
            flip("ff_std", "ff_rstd")
            for k in range(KD):
                link(v.scalar_tensor_tensor(mix[:, k, :], mix[:, k, :], V("g_post2", k), rstd[:, :], ALU.mult, ALU.mult))
            sync()
            for k in range(KD):
                v.tensor_tensor(xres[:, k, :], xres[:, k, :], mix[:, k, :], ALU.add).then_inc(S("y_made"), 1)


def kernel(**inp):
    import concourse.bacc as bacc
    from concourse.bass_utils import run_bass_kernel_spmd as run

    f = {k: np.asarray(v) for k, v in inp.items()}
    dt = f["w_in"].dtype
    g = {k: (v[0] if k not in ("x_prompt", "x_sample") else v) for k, v in f.items()}

    def feat(x):
        return x.reshape(-1, P).T

    pairs = np.arange(MIX).reshape(2, 4, HD).transpose(1, 0, 2).reshape(-1)

    def head(x):
        return feat(x[pairs])

    def rows(x, at=0):
        out = np.zeros((P, 1), dt)
        out[at:at + x.size, 0] = x
        return out

    def conv_w(w):
        return w.reshape(CW, C4, P).transpose(2, 0, 1).reshape(P, CW * C4)

    mu = g["rwkv_mu"]
    full = np.ones((P, 1), dt)
    parts = {
        "g_pre": feat(g["norm_pre_mix"]), "g_post": feat(g["norm_post_mix"]),
        "g_pre2": feat(g["norm_pre_ffn"]), "g_post2": feat(g["norm_post_ffn"]),
        "cw_l": conv_w(g["lru_conv_w"]), "cb_l": feat(g["lru_conv_b"]), "ba": feat(g["lru_ba"]),
        "bx": feat(g["lru_bx"]), "lam": feat(g["lru_lambda"]), "ln_g": feat(g["gmlp_ln_g"]),
        "ln_b": feat(g["gmlp_ln_b"]), "cw_m": conv_w(g["mlstm_conv_w"]), "cb_m": feat(g["mlstm_conv_b"]),
        "norm_g": feat(g["mlstm_norm_g"]), "skip": feat(g["mlstm_skip"]),
        "mu_gd": rows(mu[3 * MIX + 64:]), "mu_low": rows(mu[3 * MIX:3 * MIX + 64]),
        "bi": rows(g["mlstm_bi"]), "bf": rows(g["mlstm_bf"]),
        "mu_r": head(mu[0:MIX]), "mu_k": head(mu[MIX:2 * MIX]), "mu_v": head(mu[2 * MIX:3 * MIX]),
        "w0": head(g["rwkv_w0"]), "a0": head(g["rwkv_a0"]), "kk": head(g["rwkv_kk"]), "ka": head(g["rwkv_ka"]),
        "rk": head(g["rwkv_rk"].reshape(-1)), "rln_g": head(g["rwkv_ln_g"]), "rln_b": head(g["rwkv_ln_b"]),
        "eps6": full * dt.type(1e-6), "eps5": full * dt.type(1e-5), "eps64": full * dt.type(64e-5),
    }
    vec = np.concatenate([parts[n] for n in VEC], 1)
    assert vec.shape == (P, NVEC)

    r, c = np.arange(P)[:, None], np.arange(P)[None, :]
    r6, c6 = r[:64], c[:, :64]
    near, oneseq = r6 // 16 == c6 // 16, r6 // LS == c6 // LS
    con_parts = {
        "ident": r == c, "ones": np.ones((P, P)), "ident2": r % 64 == c[:, :64], "ones2": r // 64 == c // 64,
        "maskD": np.arange(P)[:, None] <= np.arange(TP)[None, :], "maskS": (r6 <= c6) & oneseq,
        "n_near": (r6 > c6) & near, "n_far": (r6 > c6) & ~near, "nT_near": (r6 < c6) & near,
        "sT": r6 < c6, "iT": r6 <= c6, "n_seq": (r6 > c6) & oneseq, "nT_seq": (r6 < c6) & oneseq,
        "seq": r6 // LS == np.arange(NS)[None, :],
    }
    for n in ("maskS", "n_near", "n_far", "nT_near", "sT", "iT", "n_seq", "nT_seq", "seq"):
        con_parts[n] = np.tile(con_parts[n], (2, 1))
    con = np.zeros((P, NCON), dt)
    for n, (at, w) in CON.items():
        con[:con_parts[n].shape[0], at:at + w] = con_parts[n]
    first = np.zeros(T, bool)
    first[[0] + [TP + LS * b for b in range(NS)]] = True
    rowc = np.zeros((4, NROWC), dt)
    for h in range(4):
        rowc[h, h * P:(h + 1) * P] = 1
    rowc[:, ROWC["keep"][0]:ROWC["keep"][0] + T] = ~first
    rowc[:, ROWC["drop"][0]:ROWC["drop"][0] + T] = np.where(first, -1e30, 0)

    def tiled(w, n_out):
        k = w.shape[0] // P
        return np.ascontiguousarray(w.reshape(k, P, n_out, P).transpose(2, 1, 0, 3)).reshape(n_out, P, k * P)

    def by_tile(w):
        return w.reshape((4, KD) + w.shape[1:]).swapaxes(0, 1)

    w_in = g["w_in"]
    sizes = [("lx", MIX), ("lg", MIX), ("gu", MIX), ("gv", MIX), ("r", MIX), ("k", MIX), ("v", MIX), ("wd", 32),
             ("ad", 32), ("gd", 96), ("mx", MIX), ("mv", MIX), ("mo", MIX), ("mi", 4), ("mf", 4), ("gate", 4 * D)]
    col, at = {}, 0
    for n, w in sizes:
        col[n] = w_in[:, at:at + w] if n not in ("r", "k", "v") else w_in[:, at:at + w][:, pairs]
        at += w
    wz = np.zeros((D, NZ * P), dt)
    for n, b in ZB.items():
        if n in col:
            wz[:, b * P:b * P + col[n].shape[1]] = col[n]
    low = ZB["low"] * P
    for n, o in (("wd", 0), ("ad", 32), ("mi", 64), ("mf", 96)):
        wz[:, low + o:low + o + col[n].shape[1]] = col[n]
    wf = g["w_ff_in"].reshape(D, 2, 2 * HALF, P).transpose(0, 2, 1, 3).reshape(D, 4 * HALF * P)

    def blocks(w):
        out = np.zeros((P, C4, P), dt)
        for b in range(8):
            o = 64 * (b % 2)
            out[o:o + 64, b // 2, o:o + 64] = w[b]
        return out

    ws = g["gmlp_ws"]
    wss = np.zeros((64, C4, 64), dt)
    for b in range(NS):
        wss[b * LS:(b + 1) * LS, :, b * LS:(b + 1) * LS] = ws[:, :LS, :LS].transpose(2, 0, 1)
    gbias = np.concatenate([g["gmlp_bs"], g["gmlp_bs"], np.tile(g["gmlp_bs"][:, :LS], (1, NS))], 1)

    def featb(x):
        return x.reshape(-1, C4, P).transpose(2, 1, 0)

    def conv_state(x):
        return x.reshape(NS, 3, C4, P).transpose(3, 2, 0, 1)

    x = np.concatenate([g["x_prompt"].reshape(TP, D), g["x_sample"].reshape(NS * LS, D)])
    sh = g["state_rwkv_shift"]
    m0 = g["state_mlstm_m"]
    arrays = {
        "x": x.reshape(T, KD, P).transpose(2, 1, 0), "vec": vec, "con": con, "rowc": rowc,
        "w_f": np.concatenate([tiled(wz, NZ), by_tile(tiled(col["gate"], 4 * KD)).reshape(4 * KD, P, D)]),
        "w_br": by_tile(np.concatenate([tiled(g["w_branch"][b] if b != 2 else g["w_branch"][b][pairs], KD)
                                        for b in range(4)])).transpose(0, 2, 1, 3).reshape(KD, P, D),
        "w_o": tiled(g["w_out"], KD), "w_fi": tiled(wf, 4 * HALF),
        "w_fo": np.concatenate([tiled(g["w_ff_out"][h * HALF * P:(h + 1) * HALF * P], KD) for h in range(2)]),
        "lru_wa": blocks(g["lru_wa"]), "lru_wx": blocks(g["lru_wx"]),
        "lru_st": conv_state(g["state_lru_conv"]), "lru_h": featb(g["state_lru_h"]),
        "ws": ws.transpose(2, 0, 1), "wss": wss, "gbias": gbias.reshape(1, C4, T),
        "ml_st": conv_state(g["state_mlstm_conv"]),
        "ml_wq": g["mlstm_wq"], "ml_wk": g["mlstm_wk"],
        "ml_C": g["state_mlstm_C"].transpose(3, 1, 0, 2), "ml_n": g["state_mlstm_n"].transpose(2, 1, 0),
        "ml_m": np.concatenate([np.zeros((1, 4), dt), m0]).T, "ml_mb": np.broadcast_to(m0, (P, NS, 4)),
        "rw_sh": sh[:, :3 * MIX].reshape(NS, 3, MIX)[:, :, pairs].reshape(NS, 12, P).transpose(2, 1, 0),
        "rw_gd": sh[:, 3 * MIX + 64:].T, "rw_low": sh[:, 3 * MIX:3 * MIX + 64].T,
        "rw_lora": np.concatenate([g["rwkv_w2"], g["rwkv_a2"]])[:, pairs], "rw_g2": g["rwkv_g2"][:, pairs],
        "rw_S": g["state_rwkv_wkv"].reshape(NS, 2, 4, HD, HD).transpose(1, 4, 2, 0, 3).reshape(P, 4, NS, HD),
    }
    arrays = {f"in_{k}": np.ascontiguousarray(v) for k, v in arrays.items()}
    outs = {"y": (P, KD, T), "small": (P, NOUT), "gv": (P, C4, NS * LS), "mCp": (P, 4, P), "mCs": (P, 4, NS, P),
            "Sp": (P, 4, HD), "Ss": (P, 4, NS, HD)}
    nc = bacc.Bacc("TRN2", target_bir_lowering=False, num_devices=1, dynamic_dma_scratch_size=1024)
    ap = {}
    for k, x_ in arrays.items():
        ap[k[3:]] = nc.dram_tensor(k, x_.shape, mybir.dt.from_np(x_.dtype), kind="ExternalInput").ap()
    for k, shape in outs.items():
        ap[k] = nc.dram_tensor(f"out_{k}", shape, F32, kind="ExternalOutput").ap()
    ap["front_scratch"] = nc.dram_tensor("front_scratch", (NF, P, T), F32).ap()
    build(nc, ap)
    res = run(nc, [arrays], core_ids=[0]).results[0]
    o = {k: res[f"out_{k}"] for k in outs}

    y = o["y"].transpose(2, 1, 0).reshape(T, D)

    def sm(name, *shape, parts=P):
        at, w = OUTS[name]
        return o["small"][:parts, at:at + w].reshape((parts,) + shape)

    def convs(name):
        return sm(name, C4, NSEQ, 3).transpose(2, 3, 1, 0).reshape(NSEQ, 3, MIX)

    lc, mc = convs("lconv"), convs("mconv")
    lh = sm("lh", C4, NSEQ).transpose(2, 1, 0).reshape(NSEQ, MIX)
    nn = sm("n", 4, NSEQ).transpose(2, 1, 0)
    mm = sm("m", NSEQ, parts=4).T
    rkv = np.empty((NSEQ, 3, MIX), dt)
    rkv[:, :, pairs] = sm("shift", 12, NSEQ).transpose(2, 1, 0).reshape(NSEQ, 3, MIX)
    shift = np.concatenate([rkv.reshape(NSEQ, 3 * MIX),
                            sm("shift_low", NSEQ, parts=64).T, sm("shift_gd", NSEQ, parts=96).T], 1)
    Cp = o["mCp"].transpose(1, 2, 0)[None]
    Cs = o["mCs"].transpose(2, 1, 3, 0)
    Sp = o["Sp"].reshape(2, HD, 4, HD).transpose(0, 2, 3, 1).reshape(1, 8, HD, HD)
    Ss = o["Ss"].reshape(2, HD, 4, NS, HD).transpose(3, 0, 2, 4, 1).reshape(NS, 8, HD, HD)
    gv = o["gv"].transpose(2, 1, 0).reshape(NS, LS, MIX)
    res = [y[:TP].reshape(1, TP, D), y[TP:].reshape(NS, LS, D)]
    for sl, C_, S_ in ((slice(0, 1), Cp, Sp), (slice(1, NSEQ), Cs, Ss)):
        res += [v_[None] for v_ in (lc[sl], lh[sl], shift[sl], S_, mc[sl], C_, nn[sl], mm[sl])]
    res.append(gv[None])
    return tuple(np.ascontiguousarray(v_) for v_ in res)
```
